# Optimizing a Trainium2 kernel written in Bass

```python
import jax, jax.numpy as jnp
from jax import lax
import numpy as np

D_MODEL = 1024
BATCH = 1
SEQ = 256
DEPTH = 2

N_META = 16
CONV_GROUPS = 8
CONV_GROUP_DIM = 64
D_CONV = CONV_GROUPS * CONV_GROUP_DIM
CONV_WIDTH = 3
MLA_HEADS = 8
QK_NOPE = 64
QK_ROPE = 32
V_HEAD = 64
Q_LORA = 256
KV_LORA = 128
D_MLA = MLA_HEADS * V_HEAD
ROPE_BASE = 10000.0
Q_BLOCK = 128
NEG_INF = -1e30
D_FF = 2816
N_BRANCH = 2
ALPHA = (2 * DEPTH) ** 0.25
BETA = (8 * DEPTH) ** -0.25
LN_EPS = 1e-5
RMS_EPS = 1e-6
IN_SPLITS = (D_CONV, D_CONV, D_CONV, Q_LORA, KV_LORA, QK_ROPE, D_MODEL, D_MODEL)
D_IN = sum(IN_SPLITS)


def layer_norm(x, g, b):
    xf = x.astype(jnp.float32)
    mu = jnp.mean(xf, axis=-1, keepdims=True)
    var = jnp.mean(jnp.square(xf - mu), axis=-1, keepdims=True)
    return ((xf - mu) * lax.rsqrt(var + LN_EPS) * g + b).astype(x.dtype)

def rms_norm(x, g):
    xf = x.astype(jnp.float32)
    return (xf * lax.rsqrt(jnp.mean(jnp.square(xf), axis=-1, keepdims=True) + RMS_EPS) * g).astype(x.dtype)

def rope_tables(T):
    inv_freq = 1.0 / (ROPE_BASE ** (jnp.arange(0, QK_ROPE, 2, dtype=jnp.float32) / QK_ROPE))
    ang = jnp.arange(T, dtype=jnp.float32)[:, None] * inv_freq[None, :]
    return jnp.cos(ang), jnp.sin(ang)

def apply_rope(x, cos, sin):
    x1, x2 = jnp.split(x.astype(jnp.float32), 2, axis=-1)
    return jnp.concatenate([x1 * cos - x2 * sin, x2 * cos + x1 * sin], axis=-1).astype(x.dtype)

def swiglu(x, w_up, w_down):
    gate, up = jnp.split(x @ w_up, 2, axis=-1)
    return (jax.nn.silu(gate) * up) @ w_down

def causal_short_conv(u, w):
    T = u.shape[1]
    up = jnp.pad(u, ((0, 0), (CONV_WIDTH - 1, 0), (0, 0)))
    out = up[:, 0:T] * w[0]
    for k in range(1, CONV_WIDTH):
        out = out + up[:, k:k + T] * w[k]
    return out

def mla_causal_attention(q_nope, q_rope, k_nope, k_rope, v):
    bsz, T = q_nope.shape[:2]
    n_blocks = -(-T // Q_BLOCK)
    pad = n_blocks * Q_BLOCK - T
    scale = (QK_NOPE + QK_ROPE) ** -0.5

    def to_blocks(a):
        a = jnp.pad(a, ((0, 0), (0, pad), (0, 0), (0, 0)))
        return jnp.moveaxis(a.reshape(bsz, n_blocks, Q_BLOCK, *a.shape[2:]), 1, 0)

    q_pos = jnp.arange(n_blocks * Q_BLOCK, dtype=jnp.int32).reshape(n_blocks, Q_BLOCK)
    k_pos = jnp.arange(T, dtype=jnp.int32)

    def one_block(args):
        qn, qr, qp = args
        s = (jnp.einsum('bqhd,bkhd->bhqk', qn, k_nope)
             + jnp.einsum('bqhr,bkr->bhqk', qr, k_rope)).astype(jnp.float32) * scale
        s = jnp.where(k_pos[None, :] <= qp[:, None], s, NEG_INF)
        p = jax.nn.softmax(s, axis=-1).astype(v.dtype)
        return jnp.einsum('bhqk,bkhd->bqhd', p, v)

    out = lax.map(one_block, (to_blocks(q_nope), to_blocks(q_rope), q_pos))
    out = jnp.moveaxis(out, 0, 1).reshape(bsz, n_blocks * Q_BLOCK, MLA_HEADS, V_HEAD)
    return out[:, :T]

def hybrid_mixer(x, w_in, b_gate, conv_w, q_norm_g, w_uq, kv_norm_g, w_ukv, w_br_conv, w_br_mla, w_o, cos, sin):
    bsz, T, _ = x.shape
    cuts = [int(c) for c in np.cumsum(IN_SPLITS)[:-1]]
    b_in, c_in, h_in, c_q, c_kv, k_r, g_conv, g_mla = jnp.split(x @ w_in, cuts, axis=-1)
    y_conv = b_in * causal_short_conv(c_in * h_in, conv_w)
    q = (rms_norm(c_q, q_norm_g) @ w_uq).reshape(bsz, T, MLA_HEADS, QK_NOPE + QK_ROPE)
    q_nope = q[..., :QK_NOPE]
    q_rope = apply_rope(q[..., QK_NOPE:], cos[None, :, None], sin[None, :, None])
    kv = (rms_norm(c_kv, kv_norm_g) @ w_ukv).reshape(bsz, T, MLA_HEADS, QK_NOPE + V_HEAD)
    k_nope, v = kv[..., :QK_NOPE], kv[..., QK_NOPE:]
    k_rope = apply_rope(k_r, cos[None], sin[None])
    y_mla = mla_causal_attention(q_nope, q_rope, k_nope, k_rope, v).reshape(bsz, T, D_MLA)
    merged = (jax.nn.sigmoid(g_conv + b_gate[0]) * (y_conv @ w_br_conv)
              + jax.nn.sigmoid(g_mla + b_gate[1]) * (y_mla @ w_br_mla))
    return merged @ w_o

def first_inputs(seed: int = 0) -> dict:
    key = jax.random.key(seed)
    ks = jax.random.split(key, 18)
    L = DEPTH

    def dense(k, shape, scale=1.0):
        return jax.random.normal(k, shape, jnp.float32) * (scale * shape[-2] ** -0.5)

    def near_one(k, shape):
        return 1.0 + 0.02 * jax.random.normal(k, shape, jnp.float32)

    def small(k, shape):
        return 0.02 * jax.random.normal(k, shape, jnp.float32)

    return {
        'x': jax.random.normal(ks[0], (BATCH, SEQ, D_MODEL), jnp.float32),
        'meta_tokens': jax.random.normal(ks[1], (N_META, D_MODEL), jnp.float32),
        'ffn1_w_up': dense(ks[2], (L, D_MODEL, 2 * D_FF)),
        'ffn1_w_down': dense(ks[3], (L, D_FF, D_MODEL), BETA),
        'mix_w_in': dense(ks[4], (L, D_MODEL, D_IN)),
        'mix_b_gate': small(ks[5], (L, N_BRANCH, D_MODEL)),
        'conv_w': dense(ks[6], (L, CONV_WIDTH, D_CONV)),
        'q_norm_g': near_one(ks[7], (L, Q_LORA)),
        'w_uq': dense(ks[8], (L, Q_LORA, MLA_HEADS * (QK_NOPE + QK_ROPE))),
        'kv_norm_g': near_one(ks[9], (L, KV_LORA)),
        'w_ukv': dense(ks[10], (L, KV_LORA, MLA_HEADS * (QK_NOPE + V_HEAD))),
        'w_br_conv': dense(ks[11], (L, D_CONV, D_MODEL)),
        'w_br_mla': dense(ks[12], (L, D_MLA, D_MODEL)),
        'w_o': dense(ks[13], (L, D_MODEL, D_MODEL), BETA),
        'ffn2_w_up': dense(ks[14], (L, D_MODEL, 2 * D_FF)),
        'ffn2_w_down': dense(ks[15], (L, D_FF, D_MODEL), BETA),
        'ln_g': near_one(ks[16], (L, 3, D_MODEL)),
        'ln_b': small(ks[17], (L, 3, D_MODEL)),
    }

def first_block(x, meta_tokens, ffn1_w_up, ffn1_w_down, mix_w_in, mix_b_gate, conv_w, q_norm_g, w_uq,
              kv_norm_g, w_ukv, w_br_conv, w_br_mla, w_o, ffn2_w_up, ffn2_w_down, ln_g, ln_b):
    bsz = x.shape[0]
    meta = jnp.broadcast_to(meta_tokens[None].astype(x.dtype), (bsz, N_META, D_MODEL))
    h = jnp.concatenate([meta, x], axis=1)
    cos, sin = rope_tables(h.shape[1])
    for l in range(DEPTH):
        h = layer_norm(ALPHA * h + 0.5 * swiglu(h, ffn1_w_up[l], ffn1_w_down[l]), ln_g[l, 0], ln_b[l, 0])
        mix = hybrid_mixer(h, mix_w_in[l], mix_b_gate[l], conv_w[l], q_norm_g[l], w_uq[l], kv_norm_g[l],
                           w_ukv[l], w_br_conv[l], w_br_mla[l], w_o[l], cos, sin)
        h = layer_norm(ALPHA * h + mix, ln_g[l, 1], ln_b[l, 1])
        h = layer_norm(ALPHA * h + 0.5 * swiglu(h, ffn2_w_up[l], ffn2_w_down[l]), ln_g[l, 2], ln_b[l, 2])
    return h[:, N_META:]


CHUNK = 64
N_BRANCH_2 = 3
POOL_GROUPS = 4
POOL_GW = 128
POOL_W = POOL_GROUPS * POOL_GW
POOL_WINDOWS = (2, 4, 8, 16)
ML_HEADS = 4
ML_DH = 128
ML_W = ML_HEADS * ML_DH
CONV_W = 4
FOX_HEADS = 8
FOX_DH = 64
FOX_W = FOX_HEADS * FOX_DH
N_EXPERTS = 8
TOP_K = 2
D_FF_EXPERT = 3584
MOE_BLOCK = 128
NORM_EPS = 1e-6
IN_SIZES = (POOL_W, ML_W, ML_W, ML_W, ML_W, ML_HEADS, ML_HEADS, FOX_W, FOX_W, FOX_W, FOX_HEADS, N_BRANCH_2 * D_MODEL)
IN_W = sum(IN_SIZES)
N_DENSE = (DEPTH + 1) // 2
N_MOE = DEPTH // 2


def rmsnorm(x, g):
    xf = x.astype(jnp.float32)
    y = xf * lax.rsqrt(jnp.mean(xf * xf, axis=-1, keepdims=True) + NORM_EPS)
    return (y * g.astype(jnp.float32)).astype(x.dtype)

def causal_depthwise_conv(u, w):
    return lax.conv_general_dilated(u, w[:, None, :].astype(u.dtype), window_strides=(1,),
                                    padding=[(CONV_W - 1, 0)], dimension_numbers=('NWC', 'WIO', 'NWC'),
                                    feature_group_count=u.shape[-1])

def pool_mixer(u, w_grp, scale):
    bsz, s_len, _ = u.shape
    uf = u.astype(jnp.float32).reshape(bsz, s_len, POOL_GROUPS, POOL_GW)
    cs = jnp.concatenate([jnp.zeros_like(uf[:, :1]), jnp.cumsum(uf, axis=1)], axis=1)
    pos = jnp.arange(s_len)
    outs = []
    for g, w in enumerate(POOL_WINDOWS):
        csg = cs[:, :, g]
        lower = jnp.concatenate([jnp.zeros_like(csg[:, :w - 1]), csg[:, :s_len - w + 1]], axis=1)
        cnt = jnp.minimum(pos + 1, w).astype(jnp.float32)[None, :, None]
        outs.append((csg[:, 1:] - lower) / cnt - uf[:, :, g])
    d = jnp.stack(outs, axis=2)
    y = jnp.einsum('bsgc,gcd->bsgd', d, w_grp.astype(jnp.float32)).reshape(bsz, s_len, POOL_W)
    return (y * scale.astype(jnp.float32)).astype(u.dtype)

def mlstm_mixer(q, k, v, o_pre, i_pre, f_pre, g_norm):
    bsz, s_len, _ = q.shape
    nc = s_len // CHUNK

    def heads(t):
        return t.astype(jnp.float32).reshape(bsz, nc, CHUNK, ML_HEADS, ML_DH).transpose(1, 0, 3, 2, 4)

    def gates(t):
        return t.astype(jnp.float32).reshape(bsz, nc, CHUNK, ML_HEADS).transpose(1, 0, 3, 2)

    qc, kc, vc = heads(q), heads(k) * (ML_DH ** -0.5), heads(v)
    lic = gates(i_pre)
    lfc = gates(jax.nn.log_sigmoid(f_pre.astype(jnp.float32)))
    tri = jnp.tril(jnp.ones((CHUNK, CHUNK), dtype=bool))

    def step(carry, inp):
        c_mat, n_vec, m = carry
        qb, kb, vb, li, lf = inp
        b = jnp.cumsum(lf, axis=-1)
        dmat = jnp.where(tri, b[..., :, None] - b[..., None, :] + li[..., None, :], -jnp.inf)
        m_inter = b + m[..., None]
        m_t = jnp.maximum(m_inter, jnp.max(dmat, axis=-1))
        w_inter = jnp.exp(m_inter - m_t)
        p = jnp.exp(dmat - m_t[..., None]) * jnp.einsum('bhtd,bhsd->bhts', qb, kb)
        num = w_inter[..., None] * jnp.einsum('bhvk,bhtk->bhtv', c_mat, qb) + jnp.einsum('bhts,bhsv->bhtv', p, vb)
        den = w_inter * jnp.einsum('bhk,bhtk->bht', n_vec, qb) + jnp.sum(p, axis=-1)
        h = num / jnp.maximum(jnp.abs(den), jnp.exp(-m_t))[..., None]
        b_last = b[..., -1]
        g = b_last[..., None] - b + li
        m_new = jnp.maximum(b_last + m, jnp.max(g, axis=-1))
        decay = jnp.exp(b_last + m - m_new)
        wk = jnp.exp(g - m_new[..., None])
        c_mat = decay[..., None, None] * c_mat + jnp.einsum('bhs,bhsv,bhsk->bhvk', wk, vb, kb)
        n_vec = decay[..., None] * n_vec + jnp.einsum('bhs,bhsk->bhk', wk, kb)
        return (c_mat, n_vec, m_new), h

    init = (jnp.zeros((bsz, ML_HEADS, ML_DH, ML_DH), jnp.float32),
            jnp.zeros((bsz, ML_HEADS, ML_DH), jnp.float32),
            jnp.zeros((bsz, ML_HEADS), jnp.float32))
    _, h = lax.scan(step, init, (qc, kc, vc, lic, lfc))
    h = h.transpose(1, 0, 3, 2, 4)
    h = h * lax.rsqrt(jnp.mean(h * h, axis=-1, keepdims=True) + NORM_EPS) * g_norm.astype(jnp.float32).reshape(ML_HEADS, ML_DH)
    h = h.reshape(bsz, s_len, ML_W) * jax.nn.sigmoid(o_pre.astype(jnp.float32))
    return h.astype(q.dtype)

def fox_mixer(q, k, v, f_pre):
    bsz, s_len, _ = q.shape
    nb = s_len // Q_BLOCK
    qh = q.reshape(bsz, s_len, FOX_HEADS, FOX_DH).transpose(0, 2, 1, 3)
    kh = k.reshape(bsz, s_len, FOX_HEADS, FOX_DH).transpose(0, 2, 1, 3)
    vh = v.reshape(bsz, s_len, FOX_HEADS, FOX_DH).transpose(0, 2, 1, 3)
    f_cum = jnp.cumsum(jax.nn.log_sigmoid(f_pre.astype(jnp.float32)), axis=1).transpose(0, 2, 1)
    q_blocks = qh.reshape(bsz, FOX_HEADS, nb, Q_BLOCK, FOX_DH).transpose(2, 0, 1, 3, 4)
    f_blocks = f_cum.reshape(bsz, FOX_HEADS, nb, Q_BLOCK).transpose(2, 0, 1, 3)
    kpos = jnp.arange(s_len)
    scale = FOX_DH ** -0.5

    def block(args):
        qb, fq, i = args
        qpos = i * Q_BLOCK + jnp.arange(Q_BLOCK)
        s = jnp.einsum('bhtd,bhsd->bhts', qb, kh).astype(jnp.float32) * scale + fq[..., :, None] - f_cum[:, :, None, :]
        s = jnp.where(kpos[None, :] <= qpos[:, None], s, -jnp.inf)
        p = jax.nn.softmax(s, axis=-1)
        return jnp.einsum('bhts,bhsd->bhtd', p.astype(vh.dtype), vh)

    o = lax.map(block, (q_blocks, f_blocks, jnp.arange(nb)))
    return o.transpose(1, 0, 3, 2, 4).reshape(bsz, s_len, FOX_W)

def token_mixing(x, norm_g, w_in, pool_w_grp, pool_scale, ml_conv_w, ml_b_i, ml_b_f, ml_norm_g,
                 fox_b_f, w_br_pool, w_br_ml, w_br_fox, w_out):
    h = rmsnorm(x, norm_g)
    proj = h @ w_in
    splits = np.cumsum(IN_SIZES)[:-1].tolist()
    (u_pool, ml_q, ml_k, ml_v, ml_o, ml_i, ml_f, fx_q, fx_k, fx_v, fx_f, gate_pre) = jnp.split(proj, splits, axis=-1)
    qk = jax.nn.silu(causal_depthwise_conv(jnp.concatenate([ml_q, ml_k], axis=-1), ml_conv_w))
    ml_q, ml_k = qk[..., :ML_W], qk[..., ML_W:]
    y_pool = pool_mixer(u_pool, pool_w_grp, pool_scale) @ w_br_pool
    y_ml = mlstm_mixer(ml_q, ml_k, ml_v, ml_o, ml_i + ml_b_i, ml_f + ml_b_f, ml_norm_g) @ w_br_ml
    y_fox = fox_mixer(fx_q, fx_k, fx_v, fx_f + fox_b_f) @ w_br_fox
    gts = jax.nn.sigmoid(gate_pre).reshape(gate_pre.shape[:-1] + (N_BRANCH_2, D_MODEL))
    merged = gts[..., 0, :] * y_pool + gts[..., 1, :] * y_ml + gts[..., 2, :] * y_fox
    return merged @ w_out

def swiglu_2(h, w_gate, w_up, w_down):
    return (jax.nn.silu(h @ w_gate) * (h @ w_up)) @ w_down

def moe_swiglu(h, w_router, b_router, w_gate, w_up, w_down):
    bsz, s_len, d = h.shape
    n_tok = bsz * s_len
    t = h.reshape(n_tok, d)
    logits = (t @ w_router).astype(jnp.float32) + b_router.astype(jnp.float32)
    top_v, top_e = lax.top_k(logits, TOP_K)
    gate = jax.nn.softmax(top_v, axis=-1)
    n_asg = n_tok * TOP_K
    e_flat = top_e.reshape(n_asg)
    tok_flat = jnp.repeat(jnp.arange(n_tok, dtype=jnp.int32), TOP_K)
    g_flat = gate.reshape(n_asg)
    order = jnp.argsort(e_flat)
    e_s, tok_s, g_s = e_flat[order], tok_flat[order], g_flat[order]
    counts = jnp.bincount(e_flat, length=N_EXPERTS).astype(jnp.int32)
    start = jnp.cumsum(counts) - counts
    padded = ((counts + MOE_BLOCK - 1) // MOE_BLOCK) * MOE_BLOCK
    pend = jnp.cumsum(padded)
    pstart = pend - padded
    dest = pstart[e_s] + (jnp.arange(n_asg, dtype=jnp.int32) - start[e_s])
    n_blk = (n_asg + N_EXPERTS * (MOE_BLOCK - 1) + MOE_BLOCK - 1) // MOE_BLOCK
    n_rows = n_blk * MOE_BLOCK
    row_tok = jnp.full((n_rows,), n_tok, dtype=jnp.int32).at[dest].set(tok_s)
    row_g = jnp.zeros((n_rows,), jnp.float32).at[dest].set(g_s)
    blk_e = jnp.minimum(jnp.searchsorted(pend, jnp.arange(n_blk, dtype=jnp.int32) * MOE_BLOCK, side='right'), N_EXPERTS - 1)
    t_pad = jnp.concatenate([t, jnp.zeros((1, d), t.dtype)], axis=0)
    xr = t_pad[row_tok].reshape(n_blk, MOE_BLOCK, d)

    def one(args):
        xb, e = args
        return (jax.nn.silu(xb @ w_gate[e]) * (xb @ w_up[e])) @ w_down[e]

    out = lax.map(one, (xr, blk_e)).reshape(n_rows, d)
    y = jnp.zeros((n_tok + 1, d), out.dtype).at[row_tok].add(out * row_g[:, None].astype(out.dtype))[:n_tok]
    return y.reshape(bsz, s_len, d)

def second_inputs(seed: int = 0) -> dict:
    key = jax.random.key(seed)
    ks = iter(jax.random.split(key, 32))

    def nrm(shape, scale):
        return jax.random.normal(next(ks), shape, jnp.float32) * scale

    return {
        'x': nrm((BATCH, SEQ, D_MODEL), 1.0),
        'mix_norm_g': 1.0 + nrm((DEPTH, D_MODEL), 0.05),
        'w_in': nrm((DEPTH, D_MODEL, IN_W), D_MODEL ** -0.5),
        'pool_w_grp': nrm((DEPTH, POOL_GROUPS, POOL_GW, POOL_GW), POOL_GW ** -0.5),
        'pool_scale': 1.0 + nrm((DEPTH, POOL_W), 0.05),
        'ml_conv_w': nrm((DEPTH, CONV_W, 2 * ML_W), CONV_W ** -0.5),
        'ml_b_i': nrm((DEPTH, ML_HEADS), 0.1),
        'ml_b_f': 3.0 + nrm((DEPTH, ML_HEADS), 0.5),
        'ml_norm_g': 1.0 + nrm((DEPTH, ML_W), 0.05),
        'fox_b_f': 3.0 + nrm((DEPTH, FOX_HEADS), 0.5),
        'w_br_pool': nrm((DEPTH, POOL_W, D_MODEL), POOL_W ** -0.5),
        'w_br_ml': nrm((DEPTH, ML_W, D_MODEL), ML_W ** -0.5),
        'w_br_fox': nrm((DEPTH, FOX_W, D_MODEL), FOX_W ** -0.5),
        'w_out': nrm((DEPTH, D_MODEL, D_MODEL), D_MODEL ** -0.5),
        'ffn_norm_g': 1.0 + nrm((DEPTH, D_MODEL), 0.05),
        'ff_w_gate': nrm((N_DENSE, D_MODEL, D_FF), D_MODEL ** -0.5),
        'ff_w_up': nrm((N_DENSE, D_MODEL, D_FF), D_MODEL ** -0.5),
        'ff_w_down': nrm((N_DENSE, D_FF, D_MODEL), D_FF ** -0.5),
        'moe_w_router': nrm((N_MOE, D_MODEL, N_EXPERTS), D_MODEL ** -0.5),
        'moe_b_router': nrm((N_MOE, N_EXPERTS), 0.01),
        'moe_w_gate': nrm((N_MOE, N_EXPERTS, D_MODEL, D_FF_EXPERT), D_MODEL ** -0.5),
        'moe_w_up': nrm((N_MOE, N_EXPERTS, D_MODEL, D_FF_EXPERT), D_MODEL ** -0.5),
        'moe_w_down': nrm((N_MOE, N_EXPERTS, D_FF_EXPERT, D_MODEL), D_FF_EXPERT ** -0.5),
        'final_norm_g': 1.0 + nrm((D_MODEL,), 0.05),
    }

def second_block(x, mix_norm_g, w_in, pool_w_grp, pool_scale, ml_conv_w, ml_b_i, ml_b_f, ml_norm_g, fox_b_f,
              w_br_pool, w_br_ml, w_br_fox, w_out, ffn_norm_g, ff_w_gate, ff_w_up, ff_w_down,
              moe_w_router, moe_b_router, moe_w_gate, moe_w_up, moe_w_down, final_norm_g):
    for l in range(DEPTH):
        x = x + token_mixing(x, mix_norm_g[l], w_in[l], pool_w_grp[l], pool_scale[l], ml_conv_w[l],
                             ml_b_i[l], ml_b_f[l], ml_norm_g[l], fox_b_f[l], w_br_pool[l], w_br_ml[l],
                             w_br_fox[l], w_out[l])
        h = rmsnorm(x, ffn_norm_g[l])
        if l % 2 == 0:
            x = x + swiglu_2(h, ff_w_gate[l // 2], ff_w_up[l // 2], ff_w_down[l // 2])
        else:
            x = x + moe_swiglu(h, moe_w_router[l // 2], moe_b_router[l // 2], moe_w_gate[l // 2],
                               moe_w_up[l // 2], moe_w_down[l // 2])
    return rmsnorm(x, final_norm_g)


def setup_inputs(seed=0):
    out = dict(first_inputs(seed))
    for name, value in second_inputs(seed + 1).items():
        if name != "x":
            out[name + "_2"] = value
    return out


def reference(
    x, meta_tokens, ffn1_w_up, ffn1_w_down, mix_w_in, mix_b_gate, conv_w, q_norm_g, w_uq,
    kv_norm_g, w_ukv, w_br_conv, w_br_mla, w_o, ffn2_w_up, ffn2_w_down, ln_g, ln_b,
    mix_norm_g_2, w_in_2, pool_w_grp_2, pool_scale_2, ml_conv_w_2, ml_b_i_2, ml_b_f_2,
    ml_norm_g_2, fox_b_f_2, w_br_pool_2, w_br_ml_2, w_br_fox_2, w_out_2, ffn_norm_g_2,
    ff_w_gate_2, ff_w_up_2, ff_w_down_2, moe_w_router_2, moe_b_router_2, moe_w_gate_2,
    moe_w_up_2, moe_w_down_2, final_norm_g_2,
):
    x = first_block(
        x, meta_tokens, ffn1_w_up, ffn1_w_down, mix_w_in, mix_b_gate, conv_w, q_norm_g, w_uq,
        kv_norm_g, w_ukv, w_br_conv, w_br_mla, w_o, ffn2_w_up, ffn2_w_down, ln_g, ln_b,
    )
    return second_block(
        x, mix_norm_g_2, w_in_2, pool_w_grp_2, pool_scale_2, ml_conv_w_2, ml_b_i_2, ml_b_f_2,
        ml_norm_g_2, fox_b_f_2, w_br_pool_2, w_br_ml_2, w_br_fox_2, w_out_2, ffn_norm_g_2,
        ff_w_gate_2, ff_w_up_2, ff_w_down_2, moe_w_router_2, moe_b_router_2, moe_w_gate_2,
        moe_w_up_2, moe_w_down_2, final_norm_g_2,
    )


_drawn_inputs = setup_inputs


def setup_inputs(seed=0):
    import zlib

    import numpy as np

    out = dict(_drawn_inputs(seed))
    spreads = {}
    factors = {'mix_b_gate': 8.0,
     'q_norm_g': 8.0,
     'kv_norm_g': 6.786,
     'ml_b_i_2': 64.0,
     'moe_b_router_2': 3.671}
    for name, (base, spread) in spreads.items():
        noise = np.random.default_rng([zlib.crc32(name.encode()), seed]).standard_normal(out[name].shape)
        drawn = base * np.exp(spread * noise) if base else spread * noise
        out[name] = __import__('jax').numpy.asarray(drawn.astype(out[name].dtype))
    for name, factor in factors.items():
        out[name] = (out[name] * factor).astype(out[name].dtype)
    return out
```

```python
from contextlib import ExitStack

import numpy as np

import concourse.bass as bass
from concourse import mybir

F32 = mybir.dt.float32
F16 = mybir.dt.float16
U32 = mybir.dt.uint32
ALU = mybir.AluOpType
ACT = mybir.ActivationFunctionType
AX = mybir.AxisListType

P = 128
D = 1024
KC = D // P
SEQ = 256
META = 16
T1 = SEQ + META
T2 = SEQ
DEPTH = 2
FF = 2816
FC = FF // P
FFE = 3584
EC = FFE // P
EXPERTS = 8
HEADS1 = 8
NOPE, ROPE, VH = 64, 32, 64
QK = NOPE + ROPE
ML_HEADS = 4
FOX_HEADS, FOX_DH = 8, 64
ALPHA = (2 * DEPTH) ** 0.25
LN_EPS, RMS_EPS = 1e-5, 1e-6
NEG = -1e30
WS = 64.0
UNW = 1.0 / WS
SLOTS = 4
AHEAD = 2
UNIT = 16 * P


class Phase:

    def __init__(self, first, units, size, base, after, gates):
        self.first, self.units, self.size, self.base, self.after, self.gates = first, units, size, base, after, gates


def schedule(rows, first, vec, act, gates, behind):
    out = {}
    sizes = [size for _, units, size, _, _, _ in rows for _ in range(units)] + behind
    at = 0
    for name, units, size, who, outputs, up in rows:
        out[name] = Phase(first + at, units, size, vec if who == "vec" else act, sizes[at + units:at + units + 2], gates)
        at += units
        vec += outputs if who == "vec" else 0
        act += outputs if who == "act" else 0
        gates += outputs if up else 0
    return out, first + at, vec, act, gates


ROWS1 = [
    ("up1", FC, UNIT, "vec", FC, True),
    ("down1", 2 * KC, FC // 2 * P, "vec", KC, False),
    ("win", 16, UNIT, "act", 16, False),
    ("uq", 2, 2 * 4 * QK, "act", 4, False),
    ("uk", 1, HEADS1 * NOPE, "act", 4, False),
    ("uv", 1, HEADS1 * VH, "act", 3, False),
    ("branch", KC, 8 * P, "vec", KC, False),
    ("wo", 4, UNIT, "vec", 4, False),
    ("up2", FC, UNIT, "vec", FC, True),
    ("down2", 2 * KC, FC // 2 * P, "vec", KC, False),
]
MIX2 = [
    ("values", 4, UNIT, "act", 4, False),
    ("small", 1, KC * 16, "act", 1, False),
    ("plain", 10, UNIT, "act", 10, False),
    ("gated", 14, UNIT, "act", 14, False),
    ("group", 1, 4 * P, "act", 2, False),
    ("branch", KC, 12 * P, "vec", KC, False),
    ("wout", 4, UNIT, "vec", 4, False),
]
DENSE2 = [("up", FC, UNIT, "vec", FC, True), ("down", 2 * KC, FC // 2 * P, "vec", KC, False)]
EXPERT2 = [("up", EC, UNIT, "vec", EC, True), ("down", 2 * KC, EC // 2 * P, "vec", KC, False)]

S1, L_UNITS, L_VEC, L_ACT, L_GATES = schedule(ROWS1, 0, 0, 0, 0, [UNIT, UNIT])
S20, g_, v_, a_, s_ = schedule(MIX2 + DENSE2, DEPTH * L_UNITS, DEPTH * L_VEC, DEPTH * L_ACT, DEPTH * L_GATES, [UNIT, UNIT])
V_LAYER1 = v_
S21, E_FIRST, E_VEC, E_ACT, E_GATES = schedule(MIX2, g_, v_, a_, s_, [UNIT, UNIT])
SE, g_, _, _, _ = schedule(EXPERT2, E_FIRST, E_VEC, E_ACT, E_GATES, [UNIT, UNIT])
E_UNITS = g_ - E_FIRST
E_OUT = EC + KC
SE_LAST, _, _, _, _ = schedule(EXPERT2, E_FIRST, E_VEC, E_ACT, E_GATES, [0, 0])
assert L_UNITS % SLOTS == 0 and E_UNITS % SLOTS == 0
V_END0 = S21["branch"].base
A_PER2 = 4 + 1 + 10 + 14 + 2

C1 = {"ln_g": 0, "ln_b": 24, "gate_b": 48, "conv": 64, "q_g": 76, "kv_g": 78}
N1 = 79
C2 = {"mix_g": 0, "pool_s": 8, "conv": 12, "ml_g": 44, "ffn_g": 48, "final_g": 56}
N2 = 64
N_CONST = 15
QB2 = [(0, 128, 128), (128, 128, 256)]
KB2 = [(0, 0, 128, 0), (128, 256, 128, 128)]
QB1 = [(0, 128, 128), (128, 128, 256), (256, 16, 272)]
KB1 = [(0, 0, 128, 0), (128, 272, 128, 128), (256, 416, 16, 256)]


def over_units(eng, phase, quads, body):
    trips = phase.units // SLOTS
    if trips > 1:
        with eng.Fori(0, trips) as trip:
            for j in range(SLOTS):
                body(trip, j, phase.first + j, quads + trip)
    else:
        trips = 0
    for u in range(trips * SLOTS, phase.units):
        body(u // SLOTS, u % SLOTS, phase.first + u % SLOTS, quads + u // SLOTS)


def over_units_ahead(eng, phase, quads, split, take):
    same = phase.after == [phase.size, phase.size]
    inner = phase.units if same else max(phase.units - AHEAD, 0)
    trips = inner // SLOTS

    def step(trip, j, q, size):
        g = phase.first + j
        if size:
            split(g + AHEAD, q, size)
        take(trip, j, g, q)

    if trips > 1:
        with eng.Fori(0, trips) as trip:
            for j in range(SLOTS):
                step(trip, j, quads + trip, phase.size)
    else:
        trips = 0
    for u in range(trips * SLOTS, phase.units):
        late = u + AHEAD - phase.units
        step(u // SLOTS, u % SLOTS, quads + u // SLOTS, phase.size if late < 0 else phase.after[late])


class Core:
    pass


def allocate(nc, ctx):
    k = Core()

    def sb(name, shape, dt):
        return ctx.enter_context(nc.sbuf_tensor(name, shape, dt))

    def sem(name):
        return ctx.enter_context(nc.semaphore(name))

    k.w32 = sb("w32", [P, SLOTS, UNIT], F32)
    k.w_hi = sb("w_hi", [P, SLOTS, UNIT], F16)
    k.w_lo = sb("w_lo", [P, SLOTS, UNIT], F16)
    k.h = sb("h", [P, KC, T1], F32)
    k.x_hi = sb("x_hi", [P, KC, T1], F16)
    k.x_lo = sb("x_lo", [P, KC, T1], F16)
    k.sq = sb("sq", [P, KC, T1], F32)
    ff = sb("ff", [P, EC * T2], F32)
    k.a_hi1 = ff[:, 0:FC * T1 // 2].bitcast(F16).rearrange("p (c t) -> p c t", t=T1)
    k.a_lo1 = ff[:, FC * T1 // 2:FC * T1].bitcast(F16).rearrange("p (c t) -> p c t", t=T1)
    k.a_hi2 = ff[:, 0:EC * T2 // 2].bitcast(F16).rearrange("p (c t) -> p c t", t=T2)
    k.a_lo2 = ff[:, EC * T2 // 2:EC * T2].bitcast(F16).rearrange("p (c t) -> p c t", t=T2)
    n = HEADS1 * T1
    k.qf = ff[:, 0:n].rearrange("p (h t) -> p h t", t=T1)
    k.kf = ff[:, n:2 * n].rearrange("p (h t) -> p h t", t=T1)
    k.rope_a = ff[:, 2 * n:3 * n].rearrange("p (h t) -> p h t", t=T1)
    k.qkc = ff[:, 0:8 * T2].rearrange("p (c t) -> p c t", t=T2)
    k.vtok = ff[:, 8 * T2:16 * T2].rearrange("p (t n) -> p t n", n=4 * T2)
    k.tap = ff[:, 16 * T2:24 * T2].rearrange("p (c t) -> p c t", t=T2)
    mix = sb("mix", [P, 48 * T2], F32)
    k.mix1 = mix[:, 0:32 * T1].rearrange("p (c t) -> p c t", t=T1)
    k.vt1 = mix[:, 32 * T1:32 * T1 + 3 * 512].rearrange("p (b n) -> p b n", n=512)
    k.mix2 = mix[:, :].rearrange("p (c t) -> p c t", t=T2)
    k.tokens = mix[:, 0:3 * D].rearrange("p (b n) -> p b n", n=D)
    k.gate_bc = mix[:, 0:EXPERTS * T2].rearrange("p (e t) -> p e t", t=T2)
    k.out_rows = mix[:, 0:2 * D].rearrange("p (b n) -> p b n", n=D)
    k.out_fm = mix[:, 2 * D:2 * D + KC * T2].rearrange("p (c t) -> p c t", t=T2)
    k.prod = sb("prod", [P, 2, T1], F32)
    k.tmp = sb("tmp", [P, 3, T1], F32)
    k.silu = k.tmp[:, 0:2, :]
    k.y_hi = sb("y_hi", [P, 3, 4, T1], F16)
    k.y_lo = sb("y_lo", [P, 3, 4, T1], F16)
    k.pa = sb("pa", [P, 4, T1 + 2], F32)
    k.pb = sb("pb", [P, 4, T1 + 2], F32)
    at = 2 * n
    k.sc = ff[:, at:at + 2 * T1].rearrange("p (b t) -> p b t", t=T1)
    k.pr = ff[:, at + 2 * T1:at + 4 * T1].rearrange("p (b t) -> p b t", t=T1)
    at += 4 * T1
    k.pt = ff[:, at:at + 2 * 432].rearrange("p (b t) -> p b t", t=432)
    at += 2 * 432
    k.gm = ff[:, at:at + 2 * T2].rearrange("p (b t) -> p b t", t=T2)
    k.stat = sb("stat", [P, 2, 8], F32)
    k.std = k.sq[:, 6:8, :]
    k.rstd = sb("rstd", [P, 2, T1], F32)
    k.gp = sb("gp", [P, 2, 16], F32)
    k.gx = sb("gx", [P, 2, 16], F32)
    k.ge = sb("ge", [P, 2, 16], F32)
    k.gl = sb("gl", [P, 2, 16], F32)
    k.lf = sb("lf", [P, 2, 12], F32)
    k.cum = sb("cum", [P, 2, 12], F32)
    k.gbias = sb("gbias", [P, DEPTH, 16], F32)
    k.wr = sb("wr", [P, KC, EXPERTS], F32)
    k.rb = sb("rb", [P, EXPERTS], F32)
    k.lg = sb("lg", [P, 2, EXPERTS], F32)
    k.top = sb("top", [P, 2, 8], F32)
    k.topi = sb("topi", [P, 2, 8], U32)
    k.topf = sb("topf", [P, 2, 8], F32)
    k.rt = sb("rt", [P, 2, 8], F32)
    k.ga = sb("ga", [P, 2, EXPERTS], F32)
    k.gb = sb("gb", [P, 2, EXPERTS], F32)
    k.gates = sb("gates", [P, 2, EXPERTS], F32)
    k.rows = sb("rows", [N1, P], F32)
    k.col = sb("col", [P, N1], F32)
    k.rows2 = sb("rows2", [N2, DEPTH, P], F32)
    k.col2 = sb("col2", [P, DEPTH, N2], F32)
    k.pscale = sb("pscale", [P, DEPTH, 4], F32)
    k.ident = sb("ident", [P, P], F32)
    k.tri = sb("tri", [P, P], F32)
    k.ntri = sb("ntri", [P, 2 * P], F32)
    k.mask = sb("mask", [P, 3 * P], F32)
    k.mean_w = sb("mean_w", [P, P], F32)
    k.ones = sb("ones", [P, P], F32)
    k.cos = sb("cos", [P, T1], F32)
    k.sin = sb("sin", [P, T1], F32)
    k.rot = sb("rot", [P, ROPE], F32)
    k.place = sb("place", [ROPE, 2, QK], F32)
    k.icnt = sb("icnt", [P, 4, 16], F32)
    k.eidx = sb("eidx", [P, EXPERTS], F32)
    k.eps = sb("eps", [P, 3], F32)
    k.ps = ctx.enter_context(nc.psum_tensor("ps", [P, 8, 512], F32))

    k.loaded = [sem(f"loaded{j}") for j in range(SLOTS)]
    k.fox_loaded = [sem(f"fox_loaded{j}") for j in range(SLOTS)]
    k.hi_ready = sem("hi_ready")
    k.parts_ready = sem("parts_ready")
    k.unit_done = sem("unit_done")
    k.vec_evac = sem("vec_evac")
    k.act_evac = sem("act_evac")
    k.silu_ready = sem("silu_ready")
    k.ff_ready = sem("ff_ready")
    k.const_loaded = sem("const_loaded")
    k.consts_set = sem("consts_set")
    k.vec_loaded = sem("vec_loaded")
    k.vec_turned = sem("vec_turned")
    k.vec_ready = sem("vec_ready")
    k.tokens_loaded = sem("tokens_loaded")
    k.turned = sem("turned")
    k.turned_out = sem("turned_out")
    k.h_ready = sem("h_ready")
    k.x_hi_ready = sem("x_hi_ready")
    k.x_ready = sem("x_ready")
    k.ln_mean = sem("ln_mean")
    k.ln_centered = sem("ln_centered")
    k.ln_squared = sem("ln_squared")
    k.ln_var = sem("ln_var")
    k.ln_std = sem("ln_std")
    k.lat_squared = sem("lat_squared")
    k.lat_mean = sem("lat_mean")
    k.lat_std = sem("lat_std")
    k.lat_normed = sem("lat_normed")
    k.lat_hi = sem("lat_hi")
    k.lat_ready = sem("lat_ready")
    k.kr_placed = sem("kr_placed")
    k.q_turned = sem("q_turned")
    k.q_rot_used = sem("q_rot_used")
    k.k_full = sem("k_full")
    k.q_full = sem("q_full")
    k.conv_ready = sem("conv_ready")
    k.scored = sem("scored")
    k.masked = sem("masked")
    k.exped = sem("exped")
    k.probs_ready = sem("probs_ready")
    k.pt_written = sem("pt_written")
    k.pt_ready = sem("pt_ready")
    k.heads_summed = sem("heads_summed")
    k.y_hi_ready = sem("y_hi_ready")
    k.y_ready = sem("y_ready")
    k.merged_ready = sem("merged_ready")
    k.small_ready = sem("small_ready")
    k.gate_ln = sem("gate_ln")
    k.lf_ready = sem("lf_ready")
    k.cum_summed = sem("cum_summed")
    k.cum_ready = sem("cum_ready")
    k.pool_ready = sem("pool_ready")
    k.taps_ready = sem("taps_ready")
    k.qk_ready = sem("qk_ready")
    k.ml_squared = sem("ml_squared")
    k.ml_mean = sem("ml_mean")
    k.ml_std = sem("ml_std")
    k.ml_ready = sem("ml_ready")
    k.rms_squared = sem("rms_squared")
    k.rms_mean = sem("rms_mean")
    k.rms_std = sem("rms_std")
    k.routed = sem("routed")
    k.lg_ready = sem("lg_ready")
    k.lg_exped = sem("lg_exped")
    k.gates_ready = sem("gates_ready")
    k.gate_spread = sem("gate_spread")
    k.gate_bc_ready = sem("gate_bc_ready")
    k.out_turned = sem("out_turned")
    k.out_copied = sem("out_copied")
    k.stored = sem("stored")
    k.rows2_loaded = sem("rows2_loaded")
    k.cols2_turned = sem("cols2_turned")
    k.cols2_ready = sem("cols2_ready")
    k.pe_steps = sem("pe_steps")
    k.latent_out = sem("latent_out")
    k.ml_hi = sem("ml_hi")
    k.ml_parts = sem("ml_parts")
    return k


def sp_program(sp, k, i, out):
    def slot(g, q, shape_a, src_a, shape_b=None, src_b=None):
        s = g % SLOTS
        sp.wait_ge(k.parts_ready, q * SLOTS + (g + 1))
        lo = 0
        for (c, n), src in ((shape_a, src_a), (shape_b, src_b)):
            dst = k.w32[:, s, lo:lo + c * n].rearrange("p (c n) -> p c n", n=n)
            sp.dma_start(dst, src).then_inc(k.loaded[s], 16)
            lo += c * n

    def chunks(w, c0, c, n0, n):
        return w[c0 * P:(c0 + c) * P, :][:, bass.ds(n0, n)].rearrange("(c p) n -> p c n", p=P)

    def up(phase, q, w_gate, w_up, gate0, up0):
        def unit(trip, j, g, q):
            u = (trip * SLOTS + j) * P
            slot(g, q, (KC, P), chunks(w_gate, 0, KC, u + gate0, P), (KC, P), chunks(w_up, 0, KC, u + up0, P))
        over_units(sp, phase, q, unit)

    def down(phase, q, w, fc):
        half, part = fc // 2, fc // 4
        cut = [(0, part), (part, half - part)]

        def unit(trip, j, g, q):
            m = (trip * 2 + j // 2) * P
            at = (j % 2) * half
            (a0, an), (b0, bn) = cut
            slot(g, q, (an, P), chunks(w, at + a0, an, m, P), (bn, P), chunks(w, at + b0, bn, m, P))
        over_units(sp, phase, q, unit)

    def wide(phase, q, w, col):
        def unit(trip, j, g, q):
            c = col(trip, j)
            slot(g, q, (KC // 2, 256), chunks(w, 0, KC // 2, c, 256), (KC // 2, 256), chunks(w, KC // 2, KC // 2, c, 256))
        over_units(sp, phase, q, unit)

    def part(phase, first, units):
        return Phase(phase.first + first, units, phase.size, 0, [], 0)

    with sp.Fori(0, DEPTH) as l:
        q = l * (L_UNITS // SLOTS)
        up(S1["up1"], q, i["ffn1_w_up"][l], i["ffn1_w_up"][l], 0, FF)
        down(S1["down1"], q, i["ffn1_w_down"][l], FC)
        w_in = i["mix_w_in"][l]
        win = S1["win"]
        over = lambda t, j: (t * SLOTS + j) * 256
        for u in range(16):
            c0 = u * 256 if u < 8 else 1952 + (u - 8) * 256
            slot(win.first + u % SLOTS, q + u // SLOTS, (KC // 2, 256), chunks(w_in, 0, KC // 2, c0, 256),
                 (KC // 2, 256), chunks(w_in, KC // 2, KC // 2, c0, 256))
        for u in range(2):
            n = 4 * QK
            slot(S1["uq"].first + u, q, (1, n), chunks(i["w_uq"][l], 0, 1, u * n, n), (1, n), chunks(i["w_uq"][l], 1, 1, u * n, n))
        kv = i["w_ukv"][l].rearrange("p (h n) -> p h n", n=NOPE + VH)
        for u, name in enumerate(("uk", "uv")):
            slot(S1[name].first, q, (4, NOPE), kv[:, 0:4, u * NOPE:(u + 1) * NOPE], (4, NOPE), kv[:, 4:8, u * NOPE:(u + 1) * NOPE])

        def branch(trip, j, g, q):
            m = (trip * SLOTS + j) * P
            slot(g, q, (4, P), chunks(i["w_br_conv"][l], 0, 4, m, P), (4, P), chunks(i["w_br_mla"][l], 0, 4, m, P))
        over_units(sp, S1["branch"], q, branch)
        wide(S1["wo"], q, i["w_o"][l], over)
        up(S1["up2"], q, i["ffn2_w_up"][l], i["ffn2_w_up"][l], 0, FF)
        down(S1["down2"], q, i["ffn2_w_down"][l], FC)

    for l in range(DEPTH):
        s = S20 if l == 0 else S21
        w_in = i["w_in_2"][l]
        wide(s["values"], 0, w_in, lambda t, j: 1536 + 256 * j if j < 2 else 3592 + 256 * (j - 2))
        g = s["small"].first
        slot(g, 0, (KC, 8), chunks(w_in, 0, KC, 2560, 8), (KC, 8), chunks(w_in, 0, KC, 4104, 8))
        wide(part(s["plain"], 0, 6), 0, w_in, lambda t, j: (t * SLOTS + j) * 256)
        wide(part(s["plain"], 6, 4), 0, w_in, lambda t, j: 2568 + (t * SLOTS + j) * 256)
        wide(part(s["gated"], 0, 2), 0, w_in, lambda t, j: 2048 + (t * SLOTS + j) * 256)
        wide(part(s["gated"], 2, 12), 0, w_in, lambda t, j: 4112 + (t * SLOTS + j) * 256)
        grp = i["pool_w_grp_2"][l].rearrange("g c n -> c g n")
        slot(s["group"].first, 0, (2, P), grp[:, 0:2, :], (2, P), grp[:, 2:4, :])

        def branch2(trip, j, g, q):
            m = (trip * SLOTS + j) * P
            slot(g, q, (4, P), chunks(i["w_br_pool_2"][l], 0, 4, m, P), (4, P), chunks(i["w_br_ml_2"][l], 0, 4, m, P))
            dst = k.w32[:, g % SLOTS, 8 * P:12 * P].rearrange("p (c n) -> p c n", n=P)
            sp.dma_start(dst, chunks(i["w_br_fox_2"][l], 0, 4, m, P)).then_inc(k.fox_loaded[g % SLOTS], 16)
        over_units(sp, s["branch"], 0, branch2)
        wide(s["wout"], 0, i["w_out_2"][l], lambda t, j: (t * SLOTS + j) * 256)
        if l == 0:
            up(s["up"], 0, i["ff_w_gate_2"][0], i["ff_w_up_2"][0], 0, 0)
            down(s["down"], 0, i["ff_w_down_2"][0], FC)
    with sp.Fori(0, EXPERTS) as e:
        q = e * (E_UNITS // SLOTS)
        up(SE["up"], q, i["moe_w_gate_2"][0][e], i["moe_w_up_2"][0][e], 0, 0)
        down(SE["down"], q, i["moe_w_down_2"][0][e], EC)


def act_program(act, k, i, out):
    def split(g, q, size):
        s = g % SLOTS
        act.wait_ge(k.loaded[s], (q + g // SLOTS) * 32 + 32)
        if size == 12 * P:
            layer = 0 if g < S21["values"].first else 1
            first = (S20, S21)[layer]["branch"].first
            act.wait_ge(k.fox_loaded[s], (q + (g - first) // SLOTS + 2 * layer) * 16 + 16)
        act.wait_ge(k.unit_done, q * SLOTS + (g + 1))
        act.activation(k.w_hi[:, s, 0:size], k.w32[:, s, 0:size], ACT.Copy, scale=WS).then_inc(k.hi_ready, 1)

    def unit_used(g, q):
        act.wait_ge(k.unit_done, q * SLOTS + (g + 1 + SLOTS))

    def up(phase, q, vec0, gates0, t):
        def take(trip, j, g, q):
            o = trip * SLOTS + j
            unit_used(g, q)
            act.wait_ge(k.vec_evac, vec0 + o + (phase.base + 1))
            act.activation(k.silu[:, j % 2, 0:t], k.ps[:, 2 * (j % 2), 0:t], ACT.Silu, scale=UNW).then_inc(k.silu_ready, 1)
        over_units_ahead(act, phase, q, split, take)

    def ahead_only(phase, q):
        over_units_ahead(act, phase, q, split, lambda trip, j, g, q: None)

    def layer_norm(n):
        act.wait_ge(k.ln_centered, n + 1)
        act.activation(k.sq[:, :, :], k.h[:, :, :], ACT.Square).then_inc(k.ln_squared, 1)
        act.wait_ge(k.ln_var, n + 1)
        act.activation(k.std[:, 0, :], k.ps[:, 5, 0:T1], ACT.Sqrt, bias=k.eps[:, 0:1]).then_inc(k.ln_std, 1)
        act.wait_ge(k.h_ready, n + 1)
        act.activation(k.x_hi[:, :, :], k.h[:, :, :], ACT.Copy).then_inc(k.x_hi_ready, 1)

    def rms_norm(n, to_parts=True):
        act.activation(k.sq[:, :, 0:T2], k.h[:, :, META:T1], ACT.Square).then_inc(k.rms_squared, 1)
        act.wait_ge(k.rms_mean, n + 1)
        act.activation(k.std[:, 0, 0:T2], k.ps[:, 4, 0:T2], ACT.Sqrt, bias=k.eps[:, 1:2]).then_inc(k.rms_std, 1)
        if to_parts:
            act.wait_ge(k.h_ready, 3 * DEPTH + n + 1)
            act.activation(k.x_hi[:, :, 0:T2], k.sq[:, :, 0:T2], ACT.Copy).then_inc(k.x_hi_ready, 1)

    def heads(items0, heads0, blocks, heads, exp, last_rows):
        nb = len(blocks)
        items = heads * nb

        def copy(h):
            act.wait_ge(k.pt_written, items0 + nb * (h + 1))
            if h >= 2:
                act.wait_ge(k.heads_summed, heads0 + h - 1)
            if last_rows:
                act.activation(k.pt[:, h % 2, 0:416], k.ps[:, 6 + h % 2, 0:416], ACT.Copy)
                act.activation(k.pt[0:last_rows, h % 2, 416:432], k.ps[0:last_rows, 6 + h % 2, 416:432], ACT.Copy).then_inc(k.pt_ready, 1)
            else:
                act.activation(k.pt[:, h % 2, 0:384], k.ps[:, 6 + h % 2, 0:384], ACT.Copy).then_inc(k.pt_ready, 1)

        for n in range(items):
            act.wait_ge(k.masked, items0 + n + 1)
            if n >= 2:
                act.wait_ge(k.pt_written, items0 + n - 1)
            exp(n % 2, *blocks[n % nb][1:])
            if n >= nb + 1 and (n - nb - 1) % nb == 0:
                copy((n - nb - 1) // nb)
        copy(heads - 1)

    def softmax_exp(b, queries, keys):
        act.activation(k.pr[0:queries, b, 0:keys], k.sc[0:queries, b, 0:keys], ACT.Exp, bias=k.stat[0:queries, b, 0:1],
                       accum_out=k.stat[0:queries, b, 1:2]).then_inc(k.exped, 1)

    def ml_exp(b, queries, keys):
        act.activation(k.pr[:, b, 0:keys], k.sc[:, b, 0:keys], ACT.Exp, bias=k.stat[:, b, 1:2])
        act.activation(k.stat[:, b, 4:5], k.stat[:, b, 1:2], ACT.Exp).then_inc(k.exped, 1)

    n_const = 0
    for dst, src in ((k.ident, "c_ident"), (k.tri, "c_tri"), (k.ntri, "c_ntri"), (k.mask, "c_mask"), (k.rot, "c_rot")):
        act.dma_start(dst[:, :], i[src]).then_inc(k.const_loaded, 16)
        n_const += 1
    act.dma_start(k.tokens[0:META, 0, :], i["meta_tokens"]).then_inc(k.tokens_loaded, 16)
    act.dma_start(k.tokens[:, 1:3, :], i["x"][0].rearrange("(b p) d -> p b d", p=P)).then_inc(k.tokens_loaded, 16)
    for dst, src in ((k.cos[64:96, :], i["c_cos"]), (k.sin[64:96, :], i["c_sin"]), (k.place[:, :, :], i["c_place"]),
                     (k.icnt[:, :, :], i["c_icnt"].rearrange("(a g) t -> a g t", a=1).broadcast_to([P, 4, 16])),
                     (k.eidx[:, :], i["c_eidx"].broadcast_to([P, EXPERTS])),
                     (k.rb[:, :], i["moe_b_router_2"].broadcast_to([P, EXPERTS])),
                     (k.wr[:, :, :], i["moe_w_router_2"][0].rearrange("(c p) e -> p c e", p=P))):
        act.dma_start(dst, src).then_inc(k.const_loaded, 16)
        n_const += 1
    for name, c0, n in (("ml_b_i_2", 0, 4), ("ml_b_f_2", 4, 4), ("fox_b_f_2", 8, 8)):
        act.dma_start(k.gbias[:, :, c0:c0 + n], i[name].rearrange("(a l) n -> a l n", a=1).broadcast_to([P, DEPTH, n])).then_inc(k.const_loaded, 16)
        n_const += 1
    assert n_const == N_CONST
    for name, n in (("mix_g", 8), ("pool_s", 4), ("ml_g", 4), ("ffn_g", 8)):
        src = {"mix_g": "mix_norm_g_2", "pool_s": "pool_scale_2", "ml_g": "ml_norm_g_2", "ffn_g": "ffn_norm_g_2"}[name]
        act.dma_start(k.rows2[C2[name]:C2[name] + n, :, :], i[src].rearrange("l (c p) -> c l p", p=P)).then_inc(k.rows2_loaded, 16)
    for l in range(DEPTH):
        act.dma_start(k.rows2[C2["conv"]:C2["conv"] + 32, l, :], i["ml_conv_w_2"][l].rearrange("k (c p) -> (k c) p", p=P)).then_inc(k.rows2_loaded, 16)
        act.dma_start(k.rows2[C2["final_g"]:C2["final_g"] + 8, l, :], i["final_norm_g_2"].rearrange("(c p) -> c p", p=P)).then_inc(k.rows2_loaded, 16)

    for c in range(KC):
        act.wait_ge(k.turned, c + 1)
        act.activation(k.h[:, c, :], k.ps[:, 4 + c % 4, 0:T1], ACT.Copy).then_inc(k.turned_out, 1)
    act.drain()
    act.activation(k.x_hi[:, :, :], k.h[:, :, :], ACT.Copy).then_inc(k.x_hi_ready, 1)
    act.wait_ge(k.cols2_turned, 1)
    for l in range(DEPTH):
        cp = act.activation(k.col2[:, l, :], k.ps[:, 6, l * N2:(l + 1) * N2], ACT.Copy)
    cp.then_inc(k.cols2_ready, 1)
    split(0, 0, UNIT)
    split(1, 0, UNIT)

    with act.Fori(0, DEPTH) as l:
        q, vec0, act0, gates0 = l * (L_UNITS // SLOTS), l * L_VEC, l * L_ACT, l * L_GATES
        act.wait_ge(k.vec_turned, l + 1)
        for name, src, n in (("ln_g", i["ln_g"][l].rearrange("i (c p) -> (i c) p", p=P), 24),
                             ("ln_b", i["ln_b"][l].rearrange("i (c p) -> (i c) p", p=P), 24),
                             ("gate_b", i["mix_b_gate"][l].rearrange("i (c p) -> (i c) p", p=P), 16),
                             ("conv", i["conv_w"][l].rearrange("i (c p) -> (i c) p", p=P), 12),
                             ("q_g", i["q_norm_g"][l].rearrange("(c p) -> c p", p=P), 2),
                             ("kv_g", i["kv_norm_g"][l].rearrange("(c p) -> c p", p=P), 1)):
            act.dma_start(k.rows[C1[name]:C1[name] + n, :], src).then_inc(k.vec_loaded, 16)
        up(S1["up1"], q, vec0, gates0 + S1["up1"].gates, T1)
        ahead_only(S1["down1"], q)
        act.wait_ge(k.vec_turned, l + 2)
        act.activation(k.col[:, :], k.ps[:, 6, 0:N1], ACT.Copy).then_inc(k.vec_ready, 1)
        act.drain()
        layer_norm(l * 3)

        def take_win(u, g, q):
            unit_used(g, q)
            b = 2 * (u % 2)
            if u < 8:
                act.activation(k.mix1[:, 2 * u:2 * u + 2, :], k.ps[:, b:b + 2, 0:T1], ACT.Copy, scale=UNW).then_inc(k.act_evac, 1)
            else:
                for c in range(2):
                    n = 2 * (u - 8) + c
                    a = act.activation(k.mix1[:, 16 + n, :], k.ps[:, b + c, 0:T1], ACT.Sigmoid, scale=UNW,
                                       bias=k.col[:, C1["gate_b"] + n:C1["gate_b"] + n + 1])
                a.then_inc(k.act_evac, 1)
        win = S1["win"]
        for u in range(win.units):
            late = u + AHEAD - win.units
            split(win.first + u + AHEAD, q, win.size if late < 0 else win.after[late])
            take_win(u, win.first + u, q)
        act.drain()
        act.activation(k.sq[:, 0:3, :], k.mix1[:, 12:15, :], ACT.Square).then_inc(k.lat_squared, 1)
        act.wait_ge(k.lat_mean, l + 1)
        act.activation(k.std[:, 0, :], k.ps[:, 4, 0:T1], ACT.Sqrt, bias=k.eps[:, 1:2], scale=float(D) / 256)
        act.activation(k.std[:, 1, :], k.ps[:, 5, 0:T1], ACT.Sqrt, bias=k.eps[:, 1:2], scale=float(D) / 128).then_inc(k.lat_std, 1)
        act.wait_ge(k.lat_normed, l + 1)
        act.activation(k.y_hi[:, 2, 0:3, :], k.sq[:, 3:6, :], ACT.Copy).then_inc(k.lat_hi, 1)
        outs = 0
        lat0 = l * 7
        later = [S1["uk"].size, S1["uv"].size, S1["branch"].size, S1["branch"].size]
        for u, (name, n_out) in enumerate((("uq", 2), ("uq", 2), ("uk", 4), ("uv", 3))):
            g = S1["uq"].first + u
            split(g + AHEAD, q, later[u])
            for o in range(n_out):
                if o < n_out - 1:
                    act.wait_ge(k.latent_out, lat0 + outs + 1)
                    outs += 1
                else:
                    unit_used(g, q)
                b = 2 * (o % 2)
                if name == "uq":
                    h = 4 * u + 2 * o
                    a = act.activation(k.qf[0:QK, h:h + 2, :], k.ps[0:QK, b:b + 2, 0:T1], ACT.Copy, scale=UNW)
                elif name == "uk":
                    a = act.activation(k.kf[0:NOPE, 2 * o:2 * o + 2, :], k.ps[0:NOPE, b:b + 2, 0:T1], ACT.Copy, scale=UNW)
                else:
                    n = QB1[o][1]
                    a = act.activation(k.vt1[0:n, o, :], k.ps[0:n, b, :], ACT.Copy, scale=UNW)
                a.then_inc(k.act_evac, 1)
        heads(l * 24, l * 8, QB1, HEADS1, softmax_exp, META)
        for c in range(4):
            act.wait_ge(k.heads_summed, l * 8 + 2 * c + 2)
            act.activation(k.y_hi[:, 1, c, :], k.ps[:, c, 0:T1], ACT.Copy).then_inc(k.y_hi_ready, 1)
        ahead_only(S1["branch"], q)
        ahead_only(S1["wo"], q)
        layer_norm(l * 3 + 1)
        up(S1["up2"], q, vec0, gates0 + S1["up2"].gates, T1)
        ahead_only(S1["down2"], q)
        layer_norm(l * 3 + 2)

    for l in range(DEPTH):
        s = S20 if l == 0 else S21
        if l == 0:
            act.wait_ge(k.h_ready, 3 * DEPTH)
        else:
            act.wait_ge(k.vec_evac, V_LAYER1 + 2)
        rms_norm(2 * l)

        def take_values(trip, j, g, q):
            unit_used(g, q)
            b = 2 * (j % 2)
            act.activation(k.vtok[:, :, 256 * j:256 * j + 256], k.ps[:, b:b + 2, 0:256], ACT.Copy, scale=UNW).then_inc(k.act_evac, 1)
        over_units_ahead(act, s["values"], 0, split, take_values)

        def take_small(trip, j, g, q):
            unit_used(g, q)
            act.activation(k.gp[:, :, :], k.ps[:, 0:2, 0:16], ACT.Copy, scale=UNW).then_inc(k.act_evac, 1)
        over_units_ahead(act, s["small"], 0, split, take_small)

        def take_plain(trip, j, g, q):
            c = (trip * SLOTS + j) * 2
            unit_used(g, q)
            b = 2 * (j % 2)
            act.activation(k.mix2[:, bass.ds(c, 2), :], k.ps[:, b:b + 2, 0:T2], ACT.Copy, scale=UNW).then_inc(k.act_evac, 1)
        over_units_ahead(act, s["plain"], 0, split, take_plain)
        act.wait_ge(k.small_ready, l + 1)
        act.activation(k.ge[:, :, :], k.gx[:, :, :], ACT.Abs)
        act.drain()
        act.activation(k.gl[:, :, :], k.ge[:, :, :], ACT.Exp, scale=-1.0)
        act.drain()
        act.activation(k.ge[:, :, :], k.gl[:, :, :], ACT.Ln, bias=1.0).then_inc(k.gate_ln, 1)

        def take_gated(trip, j, g, q):
            c = (trip * SLOTS + j) * 2 + 20
            unit_used(g, q)
            b = 2 * (j % 2)
            act.activation(k.mix2[:, bass.ds(c, 2), :], k.ps[:, b:b + 2, 0:T2], ACT.Sigmoid, scale=UNW).then_inc(k.act_evac, 1)
        over_units_ahead(act, s["gated"], 0, split, take_gated)
        act.wait_ge(k.taps_ready, l + 1)
        act.activation(k.qkc[:, :, :], k.qkc[:, :, :], ACT.Silu).then_inc(k.qk_ready, 1)

        g = s["group"].first
        split(g + AHEAD, 0, s["group"].after[1])
        act.wait_ge(k.unit_done, g + 1 + SLOTS)
        for o in range(2):
            for c in range(2):
                n = 2 * o + c
                a = act.activation(k.pa[:, n, 0:T2], k.ps[:, 2 * o + c, 0:T2], ACT.Copy, scale=k.pscale[:, l, n:n + 1])
            a.then_inc(k.act_evac, 1)

        i0 = (DEPTH + l) * 24
        h0 = DEPTH * 8 + l * 12
        heads(i0, h0, QB2, ML_HEADS, ml_exp, 0)
        act.wait_ge(k.heads_summed, h0 + ML_HEADS)
        act.activation(k.sq[:, 0:4, 0:T2], k.ps[:, 0:4, 0:T2], ACT.Square).then_inc(k.ml_squared, 1)
        act.wait_ge(k.ml_mean, l + 1)
        act.activation(k.sq[:, 4:8, 0:T2], k.ps[:, 4:6, :].rearrange("p b (h t) -> p (b h) t", t=T2), ACT.Sqrt, bias=k.eps[:, 1:2],
                       scale=float(D) / P).then_inc(k.ml_std, 1)
        act.wait_ge(k.ml_ready, l + 1)
        act.activation(k.y_hi[:, 1, :, 0:T2], k.sq[:, 0:4, 0:T2], ACT.Copy).then_inc(k.ml_hi, 1)
        heads(i0 + 8, h0 + ML_HEADS, QB2, FOX_HEADS, softmax_exp, 0)
        for c in range(4):
            act.wait_ge(k.heads_summed, h0 + ML_HEADS + 2 * c + 2)
            act.activation(k.y_hi[:, 2, c, 0:T2], k.ps[:, c, 0:T2], ACT.Copy).then_inc(k.y_hi_ready, 1)
        ahead_only(s["branch"], 0)
        ahead_only(s["wout"], 0)
        act.wait_ge(k.vec_evac, s["wout"].base + 4 + 2)
        rms_norm(2 * l + 1)
        if l == 0:
            up(s["up"], 0, 0, s["up"].gates, T2)
            ahead_only(s["down"], 0)
    act.wait_ge(k.lg_ready, 1)
    act.activation(k.rt[:, :, 1], k.rt[:, :, 0], ACT.Exp).then_inc(k.lg_exped, 1)

    def expert(e, sched):
        q = e * (E_UNITS // SLOTS)
        up(sched["up"], q, e * E_OUT, None, T2)
        ahead_only(sched["down"], q)
    with act.Fori(0, EXPERTS - 1) as e:
        expert(e, SE)
    expert(EXPERTS - 1, SE_LAST)

    act.wait_ge(k.vec_evac, E_VEC + EXPERTS * E_OUT + 2)
    rms_norm(2 * DEPTH, to_parts=False)
    for b in range(4):
        act.wait_ge(k.out_turned, b + 1)
        act.activation(k.out_rows[:, b // 2, (b % 2) * 512:(b % 2) * 512 + 512], k.ps[:, 4 + b, :], ACT.Copy).then_inc(k.out_copied, 1)
        if b % 2 == 1:
            act.wait_ge(k.out_copied, b + 1)
            act.dma_start(out[0, (b // 2) * P:(b // 2 + 1) * P, :], k.out_rows[:, b // 2, :]).then_inc(k.stored, 16)
    act.wait_ge(k.stored, 32)


def vec_program(vec, k, i, out):
    def split(g, q, size):
        s = g % SLOTS
        vec.wait_ge(k.hi_ready, q * SLOTS + (g + 1))
        vec.scalar_tensor_tensor(k.w_lo[:, s, 0:size], k.w32[:, s, 0:size], WS, k.w_hi[:, s, 0:size],
                                 ALU.mult, ALU.subtract).then_inc(k.parts_ready, 1)

    def unit_used(g, q):
        vec.wait_ge(k.unit_done, q * SLOTS + (g + 1 + SLOTS))

    def ahead_only(phase, q):
        over_units_ahead(vec, phase, q, split, lambda trip, j, g, q: None)

    def up(phase, q, gates0, t, factor, a_hi, a_lo):
        def take(trip, j, g, q):
            o, b = trip * SLOTS + j, j % 2
            vec.wait_ge(k.silu_ready, gates0 + o + (phase.gates + 1))
            vec.scalar_tensor_tensor(k.prod[:, b, 0:t], k.silu[:, b, 0:t], factor * UNW, k.ps[:, 2 * b + 1, 0:t],
                                     ALU.mult, ALU.mult).then_inc(k.vec_evac, 1)
            vec.drain()
            vec.tensor_copy(a_hi[:, bass.ds(o, 1), :], k.prod[:, b:b + 1, 0:t])
            vec.drain()
            vec.tensor_tensor(a_lo[:, bass.ds(o, 1), :], k.prod[:, b:b + 1, 0:t], a_hi[:, bass.ds(o, 1), :], ALU.subtract).then_inc(k.ff_ready, 1)
        over_units_ahead(vec, phase, q, split, take)

    def down(phase, q, add):
        def take(trip, j, g, q):
            if (j % 2) == 1:
                unit_used(g, q)
                add(trip * 2 + j // 2, k.ps[:, 2 * (j // 2), :])
        over_units_ahead(vec, phase, q, split, take)

    def add_scaled(m, acc):
        vec.scalar_tensor_tensor(k.h[:, bass.ds(m, 1), :], k.h[:, bass.ds(m, 1), :], WS * ALPHA, acc[:, 0:T1].unsqueeze(1),
                                 ALU.mult, ALU.add).then_inc(k.vec_evac, 1)

    def add_plain(m, acc):
        x = k.h[:, bass.ds(m, 1), META:T1]
        vec.scalar_tensor_tensor(x, acc[:, 0:T2].unsqueeze(1), UNW, x, ALU.mult, ALU.add).then_inc(k.vec_evac, 1)

    def per_chunk(x, t, n):
        return x[:, 0:t].unsqueeze(1).broadcast_to([P, n, t])

    def layer_norm(n, g0, b0):
        vec.wait_ge(k.ln_mean, n + 1)
        vec.tensor_tensor(k.h[:, :, :], k.h[:, :, :], per_chunk(k.ps[:, 4, :], T1, KC), ALU.subtract).then_inc(k.ln_centered, 1)
        vec.wait_ge(k.ln_std, n + 1)
        vec.reciprocal(k.rstd[:, 0, :], k.std[:, 0, :])
        vec.drain()
        vec.tensor_tensor(k.h[:, :, :], k.h[:, :, :], per_chunk(k.rstd[:, 0, :], T1, KC), ALU.mult)
        vec.drain()
        for c in range(KC):
            a = vec.tensor_scalar(k.h[:, c, :], k.h[:, c, :], k.col[:, g0 + c:g0 + c + 1], k.col[:, b0 + c:b0 + c + 1], ALU.mult, ALU.add)
        a.then_inc(k.h_ready, 1)
        vec.wait_ge(k.x_hi_ready, n + 2)
        vec.tensor_tensor(k.x_lo[:, :, :], k.h[:, :, :], k.x_hi[:, :, :], ALU.subtract).then_inc(k.x_ready, 1)

    def rms_norm(n, l, g0, dst, to_parts=True):
        vec.wait_ge(k.rms_std, n + 1)
        vec.reciprocal(k.rstd[:, 0, 0:T2], k.std[:, 0, 0:T2])
        vec.drain()
        for c in range(KC):
            a = vec.scalar_tensor_tensor(dst[:, c, 0:T2], k.h[:, c, META:T1], k.col2[:, l, g0 + c:g0 + c + 1], k.rstd[:, 0, 0:T2],
                                         ALU.mult, ALU.mult)
        a.then_inc(k.h_ready, 1)
        if to_parts:
            vec.wait_ge(k.x_hi_ready, 3 * DEPTH + n + 2)
            vec.tensor_tensor(k.x_lo[:, :, 0:T2], dst[:, :, 0:T2], k.x_hi[:, :, 0:T2], ALU.subtract).then_inc(k.x_ready, 1)

    def heads(items0, blocks, heads, mask, norm):
        nb = len(blocks)
        items = heads * nb
        for n in range(items + 1):
            if n < items:
                vec.wait_ge(k.scored, items0 + n + 1)
                if n >= 2:
                    vec.wait_ge(k.exped, items0 + n - 1)
                mask(n // nb, n % nb, n % 2, *blocks[n % nb])
            if n >= 1:
                m = n - 1
                vec.wait_ge(k.exped, items0 + m + 1)
                norm(m % 2, *blocks[m % nb][1:])

    def softmax_max(b, queries, keys):
        vec.drain()
        vec.tensor_reduce(k.stat[0:queries, b, 0:1], k.sc[0:queries, b, 0:keys], AX.X, ALU.max, negate=True).then_inc(k.masked, 1)

    def softmax_norm(b, queries, keys):
        vec.reciprocal(k.stat[0:queries, b, 2:3], k.stat[0:queries, b, 1:2])
        vec.drain()
        vec.tensor_scalar(k.pr[0:queries, b, 0:keys], k.pr[0:queries, b, 0:keys], k.stat[0:queries, b, 2:3], None, ALU.mult).then_inc(k.probs_ready, 1)

    def mla_mask(h, j, b, first, queries, keys):
        vec.scalar_tensor_tensor(k.sc[0:queries, b, 0:keys], k.ps[0:queries, 4 + b, 0:keys], QK ** -0.5,
                                 k.mask[0:queries, 256 - first:256 - first + keys], ALU.mult, ALU.add)
        softmax_max(b, queries, keys)

    vec.memset(k.mean_w[:, :], 1.0 / D)
    vec.memset(k.ones[:, :], 1.0)
    vec.memset(k.eps[:, 0:1], LN_EPS * WS * WS)
    vec.memset(k.eps[:, 1:2], RMS_EPS).then_inc(k.consts_set, 1)
    vec.sem_inc(k.parts_ready, SLOTS)
    vec.sem_inc(k.unit_done, SLOTS)
    vec.sem_inc(k.vec_evac, 2)
    vec.sem_inc(k.vec_turned, 1)
    vec.sem_inc(k.act_evac, 2)
    vec.wait_ge(k.const_loaded, 16 * N_CONST)
    vec.wait_ge(k.x_hi_ready, 1)
    vec.tensor_tensor(k.x_lo[:, :, :], k.h[:, :, :], k.x_hi[:, :, :], ALU.subtract).then_inc(k.x_ready, 1)
    vec.wait_ge(k.cols2_ready, 1)
    vec.tensor_scalar(k.pscale[:, :, :], k.col2[:, :, C2["pool_s"]:C2["pool_s"] + 4], UNW, None, ALU.mult).then_inc(k.consts_set, 1)
    split(0, 0, UNIT)
    split(1, 0, UNIT)

    with vec.Fori(0, DEPTH) as l:
        q, gates0 = l * (L_UNITS // SLOTS), l * L_GATES
        up(S1["up1"], q, gates0, T1, 0.5, k.a_hi1, k.a_lo1)
        down(S1["down1"], q, add_scaled)
        vec.drain()
        vec.wait_ge(k.vec_ready, l + 1)
        layer_norm(l * 3, C1["ln_g"], C1["ln_b"])
        ahead_only(S1["win"], q)
        vec.wait_ge(k.lat_std, l + 1)
        vec.reciprocal(k.rstd[:, :, :], k.std[:, :, :])
        vec.drain()
        for c in range(3):
            a = vec.scalar_tensor_tensor(k.sq[:, 3 + c, :], k.mix1[:, 12 + c, :], k.col[:, C1["q_g"] + c:C1["q_g"] + c + 1],
                                         k.rstd[:, c // 2, :], ALU.mult, ALU.mult)
        a.then_inc(k.lat_normed, 1)
        vec.wait_ge(k.lat_hi, l + 1)
        vec.tensor_tensor(k.y_lo[:, 2, 0:3, :], k.sq[:, 3:6, :], k.y_hi[:, 2, 0:3, :], ALU.subtract).then_inc(k.lat_ready, 1)
        vec.wait_ge(k.kr_placed, l + 1)
        r = slice(NOPE, QK)
        vec.tensor_tensor(k.tmp[r, 0, :], k.ps[r, 6, 0:T1], k.cos[r, :], ALU.mult)
        vec.tensor_tensor(k.tmp[r, 1, :], k.ps[r, 7, 0:T1], k.sin[r, :], ALU.mult)
        vec.drain()
        vec.tensor_tensor(k.kf[r, :, :], k.tmp[r, 0:1, :].broadcast_to([ROPE, HEADS1, T1]),
                          k.tmp[r, 1:2, :].broadcast_to([ROPE, HEADS1, T1]), ALU.add).then_inc(k.k_full, 1)
        for u, name in enumerate(("uq", "uq", "uk", "uv")):
            g = S1["uq"].first + u
            split(g + AHEAD, q, (S1["uk"].size, S1["uv"].size, S1["branch"].size, S1["branch"].size)[u])
        vec.wait_ge(k.act_evac, l * L_ACT + (S1["uq"].base + 4 + 2))
        vec.tensor_tensor(k.rope_a[r, :, :], k.qf[r, :, :], k.cos[r, :].unsqueeze(1).broadcast_to([ROPE, HEADS1, T1]), ALU.mult)
        for n in range(2):
            vec.drain()
            vec.wait_ge(k.q_turned, l * 2 + n + 1)
            vec.tensor_tensor(k.sq[r, 0:4, :], k.ps[r, 4:8, 0:T1], k.sin[r, :].unsqueeze(1).broadcast_to([ROPE, 4, T1]), ALU.mult).then_inc(k.q_rot_used, 1)
            vec.drain()
            a = vec.tensor_tensor(k.qf[r, 4 * n:4 * n + 4, :], k.rope_a[r, 4 * n:4 * n + 4, :], k.sq[r, 0:4, :], ALU.add)
        a.then_inc(k.q_full, 1)
        heads(l * 24, QB1, HEADS1, mla_mask, softmax_norm)
        for c in range(4):
            vec.wait_ge(k.y_hi_ready, l * 4 + c + 1)
            a = vec.tensor_tensor(k.y_lo[:, 1, c, :], k.ps[:, c, 0:T1], k.y_hi[:, 1, c, :], ALU.subtract)
        a.then_inc(k.y_ready, 1)

        def take_branch(trip, j, g, q):
            m, b = trip * SLOTS + j, 2 * (j % 2)
            unit_used(g, q)
            vec.scalar_tensor_tensor(k.tmp[:, 0:1, :], k.ps[:, b:b + 1, 0:T1], UNW, k.mix1[:, bass.ds(m + 16, 1), :], ALU.mult, ALU.mult)
            vec.scalar_tensor_tensor(k.tmp[:, 1:2, :], k.ps[:, b + 1:b + 2, 0:T1], UNW, k.mix1[:, bass.ds(m + 24, 1), :],
                                     ALU.mult, ALU.mult).then_inc(k.vec_evac, 1)
            vec.drain()
            vec.tensor_tensor(k.tmp[:, 2:3, :], k.tmp[:, 0:1, :], k.tmp[:, 1:2, :], ALU.add)
            vec.drain()
            vec.tensor_copy(k.x_hi[:, bass.ds(m, 1), :], k.tmp[:, 2:3, :])
            vec.drain()
            vec.tensor_tensor(k.x_lo[:, bass.ds(m, 1), :], k.tmp[:, 2:3, :], k.x_hi[:, bass.ds(m, 1), :], ALU.subtract).then_inc(k.merged_ready, 1)
        over_units_ahead(vec, S1["branch"], q, split, take_branch)

        def take_wo(trip, j, g, q):
            c, b = (trip * SLOTS + j) * 2, 2 * (j % 2)
            unit_used(g, q)
            h = k.h[:, bass.ds(c, 2), :]
            vec.scalar_tensor_tensor(h, h, WS * ALPHA, k.ps[:, b:b + 2, 0:T1], ALU.mult, ALU.add).then_inc(k.vec_evac, 1)
        over_units_ahead(vec, S1["wo"], q, split, take_wo)
        vec.drain()
        layer_norm(l * 3 + 1, C1["ln_g"] + KC, C1["ln_b"] + KC)
        up(S1["up2"], q, gates0, T1, 0.5, k.a_hi1, k.a_lo1)
        down(S1["down2"], q, add_scaled)
        vec.drain()
        layer_norm(l * 3 + 2, C1["ln_g"] + 2 * KC, C1["ln_b"] + 2 * KC)

    for l in range(DEPTH):
        s = S20 if l == 0 else S21
        vec.drain()
        rms_norm(2 * l, l, C2["mix_g"], k.sq)
        ahead_only(s["values"], 0)
        ahead_only(s["small"], 0)
        vec.wait_ge(k.act_evac, s["small"].base + 1 + 2)
        vec.tensor_tensor(k.gx[:, :, :], k.gp[:, :, :], k.gbias[:, l, :].unsqueeze(1).broadcast_to([P, 2, 16]), ALU.add).then_inc(k.small_ready, 1)
        ahead_only(s["plain"], 0)
        vec.wait_ge(k.gate_ln, l + 1)
        vec.scalar_tensor_tensor(k.lf[:, :, :], k.gx[:, :, 4:16], 0.0, k.ge[:, :, 4:16], ALU.min, ALU.subtract).then_inc(k.lf_ready, 1)
        ahead_only(s["gated"], 0)
        vec.wait_ge(k.cum_summed, l + 1)
        vec.tensor_copy(k.cum[:, :, :], k.ps[:, 4, 0:32].rearrange("p (b n) -> p b n", n=16)[:, :, 0:12]).then_inc(k.cum_ready, 1)
        split(s["group"].first + AHEAD, 0, s["group"].after[1])
        vec.drain()

        def decay(r, dst, j, b, keys):
            vec.scalar_tensor_tensor(dst, k.ps[:, 4 + b, 256:256 + keys], k.cum[:, j, r:r + 1], k.mask[:, 256 - 128 * j:256 - 128 * j + keys],
                                     ALU.add, ALU.add)

        def ml_mask(h, j, b, first, queries, keys):
            decay(h, k.sc[:, b, 0:keys], j, b, keys)
            vec.drain()
            vec.tensor_reduce(k.stat[:, b, 0:1], k.sc[:, b, 0:keys], AX.X, ALU.max)
            vec.drain()
            vec.tensor_scalar(k.stat[:, b, 1:2], k.stat[:, b, 0:1], k.cum[:, j, h:h + 1], -1.0, ALU.max, ALU.mult).then_inc(k.masked, 1)

        def ml_norm(b, queries, keys):
            pr = k.pr[:, b, 0:keys]
            vec.scalar_tensor_tensor(pr, k.ps[:, 4 + b, 0:keys], float(P) ** -0.5, pr, ALU.mult, ALU.mult, accum_out=k.stat[:, b, 3:4])
            vec.drain()
            vec.scalar_tensor_tensor(k.stat[:, b, 7:8], k.stat[:, b, 3:4], -1.0, k.stat[:, b, 3:4], ALU.mult, ALU.max)
            vec.drain()
            vec.tensor_tensor(k.stat[:, b, 5:6], k.stat[:, b, 7:8], k.stat[:, b, 4:5], ALU.max)
            vec.drain()
            vec.reciprocal(k.stat[:, b, 6:7], k.stat[:, b, 5:6])
            vec.drain()
            vec.tensor_scalar(pr, pr, k.stat[:, b, 6:7], None, ALU.mult).then_inc(k.probs_ready, 1)

        def fox_mask(h, j, b, first, queries, keys):
            decay(4 + h, k.gm[:, b, 0:keys], j, b, keys)
            vec.drain()
            vec.scalar_tensor_tensor(k.sc[:, b, 0:keys], k.ps[:, 4 + b, 0:keys], FOX_DH ** -0.5, k.gm[:, b, 0:keys], ALU.mult, ALU.add)
            softmax_max(b, queries, keys)

        i0 = (DEPTH + l) * 24
        heads(i0, QB2, ML_HEADS, ml_mask, ml_norm)
        vec.wait_ge(k.ml_std, l + 1)
        vec.reciprocal(k.sq[:, 4:8, 0:T2], k.sq[:, 4:8, 0:T2])
        vec.drain()
        for h in range(ML_HEADS):
            vec.scalar_tensor_tensor(k.sq[:, h, 0:T2], k.ps[:, h, 0:T2], k.col2[:, l, C2["ml_g"] + h:C2["ml_g"] + h + 1],
                                     k.sq[:, 4 + h, 0:T2], ALU.mult, ALU.mult)
        vec.drain()
        vec.tensor_tensor(k.sq[:, 0:4, 0:T2], k.sq[:, 0:4, 0:T2], k.mix2[:, 20:24, :], ALU.mult).then_inc(k.ml_ready, 1)
        vec.wait_ge(k.ml_hi, l + 1)
        vec.tensor_tensor(k.y_lo[:, 1, :, 0:T2], k.sq[:, 0:4, 0:T2], k.y_hi[:, 1, :, 0:T2], ALU.subtract).then_inc(k.ml_parts, 1)
        heads(i0 + 2 * ML_HEADS, QB2, FOX_HEADS, fox_mask, softmax_norm)
        vec.wait_ge(k.act_evac, s["group"].base + 2 + 2)
        vec.tensor_copy(k.y_hi[:, 0, :, 0:T2], k.pa[:, :, 0:T2])
        vec.drain()
        vec.tensor_tensor(k.y_lo[:, 0, :, 0:T2], k.pa[:, :, 0:T2], k.y_hi[:, 0, :, 0:T2], ALU.subtract)
        for c in range(4):
            vec.wait_ge(k.y_hi_ready, (DEPTH + l) * 4 + c + 1)
            a = vec.tensor_tensor(k.y_lo[:, 2, c, 0:T2], k.ps[:, c, 0:T2], k.y_hi[:, 2, c, 0:T2], ALU.subtract)
        a.then_inc(k.y_ready, 1)

        def take_branch2(trip, j, g, q):
            m, b = trip * SLOTS + j, 2 * (j % 2)
            unit_used(g, q)
            for n in range(3):
                a = vec.scalar_tensor_tensor(k.tmp[:, n:n + 1, 0:T2], k.ps[:, b + n // 2:b + n // 2 + 1, 256 * (n % 2):256 * (n % 2) + 256], UNW,
                                             k.mix2[:, bass.ds(m + (24 + 8 * n), 1), :], ALU.mult, ALU.mult)
            a.then_inc(k.vec_evac, 1)
            vec.drain()
            vec.tensor_tensor(k.prod[:, 0:1, 0:T2], k.tmp[:, 0:1, 0:T2], k.tmp[:, 1:2, 0:T2], ALU.add)
            vec.drain()
            vec.tensor_tensor(k.prod[:, 1:2, 0:T2], k.prod[:, 0:1, 0:T2], k.tmp[:, 2:3, 0:T2], ALU.add)
            vec.drain()
            vec.tensor_copy(k.x_hi[:, bass.ds(m, 1), 0:T2], k.prod[:, 1:2, 0:T2])
            vec.drain()
            vec.tensor_tensor(k.x_lo[:, bass.ds(m, 1), 0:T2], k.prod[:, 1:2, 0:T2], k.x_hi[:, bass.ds(m, 1), 0:T2], ALU.subtract).then_inc(k.merged_ready, 1)
        over_units_ahead(vec, s["branch"], 0, split, take_branch2)

        def take_wout(trip, j, g, q):
            c, b = (trip * SLOTS + j) * 2, 2 * (j % 2)
            unit_used(g, q)
            x = k.h[:, bass.ds(c, 2), META:T1]
            vec.scalar_tensor_tensor(x, k.ps[:, b:b + 2, 0:T2], UNW, x, ALU.mult, ALU.add).then_inc(k.vec_evac, 1)
        over_units_ahead(vec, s["wout"], 0, split, take_wout)
        vec.drain()
        rms_norm(2 * l + 1, l, C2["ffn_g"], k.sq)
        if l == 0:
            up(s["up"], 0, 0, T2, 1.0, k.a_hi2, k.a_lo2)
            down(s["down"], 0, add_plain)

    vec.wait_ge(k.routed, 1)
    vec.tensor_tensor(k.lg[:, :, :], k.ps[:, 4, 0:2 * EXPERTS].rearrange("p (b e) -> p b e", e=EXPERTS),
                      k.rb[:, :].unsqueeze(1).broadcast_to([P, 2, EXPERTS]), ALU.add)
    vec.drain()
    for b in range(2):
        vec.max(k.top[:, b, :], k.lg[:, b, :])
    vec.drain()
    for b in range(2):
        vec.max_index(k.topi[:, b, :], k.top[:, b, :], k.lg[:, b, :])
    vec.tensor_tensor(k.rt[:, :, 0], k.top[:, :, 1], k.top[:, :, 0], ALU.subtract).then_inc(k.lg_ready, 1)
    vec.drain()
    vec.tensor_copy(k.topf[:, :, :], k.topi[:, :, :])
    vec.wait_ge(k.lg_exped, 1)
    vec.tensor_scalar(k.rt[:, :, 2], k.rt[:, :, 1], 1.0, None, ALU.add)
    vec.drain()
    vec.reciprocal(k.rt[:, :, 3], k.rt[:, :, 2])
    vec.drain()
    vec.tensor_tensor(k.rt[:, :, 4], k.rt[:, :, 1], k.rt[:, :, 3], ALU.mult)
    vec.drain()
    for b in range(2):
        for n, dst in enumerate((k.ga, k.gb)):
            vec.tensor_scalar(dst[:, b, :], k.eidx[:, :], k.topf[:, b, n:n + 1], k.rt[:, b, 3 + n:4 + n], ALU.is_equal, ALU.mult)
    vec.drain()
    vec.tensor_tensor(k.gates[:, :, :], k.ga[:, :, :], k.gb[:, :, :], ALU.add).then_inc(k.gates_ready, 1)
    vec.wait_ge(k.gate_spread, 1)
    vec.tensor_scalar(k.gate_bc[:, :, :], k.ps[:, 4:8, :].rearrange("p b (e t) -> p (b e) t", t=T2), UNW, None, ALU.mult).then_inc(k.gate_bc_ready, 1)
    vec.drain()

    def expert(e, sched):
        q = e * (E_UNITS // SLOTS)
        up(sched["up"], q, e * EC, T2, 1.0, k.a_hi2, k.a_lo2)

        def add_gated(m, acc):
            x = k.h[:, bass.ds(m, 1), META:T1]
            vec.tensor_tensor(k.prod[:, 0:1, 0:T2], acc[:, 0:T2].unsqueeze(1), k.gate_bc[:, bass.ds(e, 1), :], ALU.mult)
            vec.drain()
            vec.tensor_tensor(x, x, k.prod[:, 0:1, 0:T2], ALU.add).then_inc(k.vec_evac, 1)
            vec.drain()
        down(sched["down"], q, add_gated)
    with vec.Fori(0, EXPERTS - 1) as e:
        expert(e, SE)
    expert(EXPERTS - 1, SE_LAST)
    rms_norm(2 * DEPTH, 0, C2["final_g"], k.out_fm, to_parts=False)


def pool_program(pool, k, i, out):
    pool.memset(k.pa[:, :, :], 0.0)
    pool.memset(k.pb[:, :, :], 0.0)
    pool.drain()
    with pool.Fori(0, DEPTH) as l:
        pool.wait_ge(k.act_evac, l * L_ACT + (S1["win"].base + 6 + 2))
        pool.tensor_tensor(k.pa[:, :, 2:2 + T1], k.mix1[:, 4:8, :], k.mix1[:, 8:12, :], ALU.mult)
        pool.drain()
        c_acc, c_tap = k.mix1[:, 4:8, :], k.mix1[:, 8:12, :]
        for n in range(3):
            for c in range(4):
                w = k.col[:, C1["conv"] + 4 * n + c:C1["conv"] + 4 * n + c + 1]
                pool.tensor_scalar((c_tap if n else c_acc)[:, c, :], k.pa[:, c, n:n + T1], w, None, ALU.mult)
            pool.drain()
            if n:
                pool.tensor_tensor(c_acc, c_acc, c_tap, ALU.add)
                pool.drain()
        pool.tensor_tensor(c_acc, c_acc, k.mix1[:, 0:4, :], ALU.mult)
        pool.drain()
        pool.tensor_copy(k.y_hi[:, 0, :, :], c_acc)
        pool.drain()
        pool.tensor_tensor(k.y_lo[:, 0, :, :], c_acc, k.y_hi[:, 0, :, :], ALU.subtract).then_inc(k.conv_ready, 1)
    for l in range(DEPTH):
        s = S20 if l == 0 else S21
        pool.wait_ge(k.act_evac, s["plain"].base + 10 + 2)
        u = k.mix2[:, 4:12, :]
        for n in (3, 2, 1, 0):
            lag = 3 - n
            for c in range(8):
                w = k.col2[:, l, C2["conv"] + 8 * n + c:C2["conv"] + 8 * n + c + 1]
                pool.tensor_scalar((k.tap if lag else k.qkc)[:, c, :], u[:, c, :], w, None, ALU.mult)
            pool.drain()
            if lag:
                a = pool.tensor_tensor(k.qkc[:, :, lag:T2], k.qkc[:, :, lag:T2], k.tap[:, :, 0:T2 - lag], ALU.add)
                if n:
                    pool.drain()
        a.then_inc(k.taps_ready, 1)
        z = 16
        pool.memset(k.pa[:, :, 0:z], 0.0)
        pool.memset(k.pb[:, :, 0:z], 0.0)
        pool.tensor_copy(k.pa[:, :, z:z + T2], k.mix2[:, 0:4, :])
        a, b = k.pa, k.pb
        for n in range(4):
            pool.drain()
            w = 1 << n
            pool.tensor_tensor(b[:, n:4, z:z + T2], a[:, n:4, z:z + T2], a[:, n:4, z - w:z - w + T2], ALU.add)
            a, b = b, a
        pool.drain()
        for n in range(4):
            src = (k.pb, k.pa)[n % 2]
            pool.tensor_tensor(src[:, n, z:2 * z], src[:, n, z:2 * z], k.icnt[:, n, :], ALU.mult)
            pool.tensor_scalar(src[:, n, 2 * z:z + T2], src[:, n, 2 * z:z + T2], 1.0 / (2 << n), None, ALU.mult)
        pool.drain()
        for n in range(4):
            src = (k.pb, k.pa)[n % 2]
            pool.tensor_tensor(src[:, n, z:z + T2], src[:, n, z:z + T2], k.mix2[:, n, :], ALU.subtract)
        pool.drain()
        for n in range(4):
            src = (k.pb, k.pa)[n % 2]
            pool.tensor_copy(k.y_hi[:, 2, n, 0:T2], src[:, n, z:z + T2])
        pool.drain()
        for n in range(4):
            src = (k.pb, k.pa)[n % 2]
            a = pool.tensor_tensor(k.y_lo[:, 2, n, 0:T2], src[:, n, z:z + T2], k.y_hi[:, 2, n, 0:T2], ALU.subtract)
        a.then_inc(k.pool_ready, 1)


def pe_program(pe, k, i, out):
    def parts(acc, w_hi, w_lo, x_hi, x_lo, first, last):
        pe.matmul(acc, w_hi, x_hi, start=first, stop=False)
        pe.matmul(acc, w_hi, x_lo, start=False, stop=False)
        return pe.matmul(acc, w_lo, x_hi, start=False, stop=last)

    def chain(acc, s, tiles, x_hi, x_lo, first=True, last=True):
        for n, (c, m, kc) in enumerate(tiles):
            a = parts(acc, k.w_hi[:, s, c:c + m], k.w_lo[:, s, c:c + m], x_hi[:, kc, :], x_lo[:, kc, :],
                      first and n == 0, last and n == len(tiles) - 1)
        return a

    def stand_alone():
        pe.sem_inc(k.pe_steps, 1)

    def weights(g, q):
        pe.wait_ge(k.parts_ready, q * SLOTS + (g + 1 + SLOTS))

    def all_out(vec, act):
        pe.wait_ge(k.vec_evac, vec)
        pe.wait_ge(k.act_evac, act)

    def up(phase, q, vec0, x_hi, x_lo, t):
        def unit(trip, j, g, q):
            s, b = g % SLOTS, 2 * (j % 2)
            weights(g, q)
            pe.wait_ge(k.vec_evac, vec0 + (trip * SLOTS + j) + (phase.base + 1))
            for n in range(2):
                a = chain(k.ps[:, b + n, 0:t], s, [(n * D + kc * P, P, kc) for kc in range(KC)], x_hi, x_lo)
            a.then_inc(k.unit_done, 1)
        over_units(pe, phase, q, unit)

    def down(phase, q, vec0, a_hi, a_lo, t, fc):
        half = fc // 2

        def unit(trip, j, g, q):
            second = j % 2
            weights(g, q)
            if not second:
                pe.wait_ge(k.vec_evac, vec0 + (trip * 2 + j // 2) + (phase.base + 1))
            chain(k.ps[:, 2 * (j // 2), 0:t], g % SLOTS, [(c * P, P, second * half + c) for c in range(half)], a_hi, a_lo,
                  first=not second, last=bool(second)).then_inc(k.unit_done, 1)
        over_units(pe, phase, q, unit)

    def wide(phase, q, evac, evac0, x_hi, x_lo, t):
        def unit(trip, j, g, q):
            s, b = g % SLOTS, 2 * (j % 2)
            weights(g, q)
            pe.wait_ge(evac, evac0 + (trip * SLOTS + j) + (phase.base + 1))
            for n in range(2):
                a = chain(k.ps[:, b + n, 0:t], s, [(kc * 256 + n * P, P, kc) for kc in range(KC)], x_hi, x_lo)
            a.then_inc(k.unit_done, 1)
        over_units(pe, phase, q, unit)

    def layer_norm(n, vec):
        pe.wait_ge(k.vec_evac, vec)
        for c in range(KC):
            a = pe.matmul(k.ps[:, 4, 0:T1], k.mean_w[:, :], k.h[:, c, :], start=c == 0, stop=c == KC - 1)
        a.then_inc(k.ln_mean, 1)
        pe.wait_ge(k.ln_squared, n + 1)
        for c in range(KC):
            a = pe.matmul(k.ps[:, 5, 0:T1], k.mean_w[:, :], k.sq[:, c, :], start=c == 0, stop=c == KC - 1)
        a.then_inc(k.ln_var, 1)

    def rms_norm(n):
        pe.wait_ge(k.rms_squared, n + 1)
        for c in range(KC):
            a = pe.matmul(k.ps[:, 4, 0:T2], k.mean_w[:, :], k.sq[:, c, 0:T2], start=c == 0, stop=c == KC - 1)
        a.then_inc(k.rms_mean, 1)

    def heads(items0, heads0, qb, kb, heads, score, value, acc, free):
        nb = len(qb)
        items = heads * nb

        def turn(n):
            h, j = n // nb, n % nb
            first, queries, keys = qb[j]
            pe.wait_ge(k.probs_ready, items0 + n + 1)
            if j == 0 and h >= 2:
                pe.wait_ge(k.pt_ready, heads0 + h - 1)
            if queries < P:
                stand_alone()
            for k0, col, width, q0 in kb[:j + 1]:
                c = col + first - q0
                a = pe.transpose(k.ps[0:width, 6 + h % 2, c:c + queries], k.pr[0:queries, n % 2, k0:k0 + width], k.ident[0:queries, 0:queries])
            a.then_inc(k.pt_written, 1)

        def sum_values(h):
            pe.wait_ge(k.pt_ready, heads0 + h + 1)
            total = qb[-1][0] + qb[-1][1]
            for n, (k0, col, width, q0) in enumerate(kb):
                a = pe.matmul(acc(h, q0, total), value(h, n, width), k.pt[0:width, h % 2, col:col + total - q0],
                              start=n == 0, stop=n == len(kb) - 1)
            a.then_inc(k.heads_summed, 1)

        for n in range(items + 1):
            if n < items:
                if n >= 2:
                    pe.wait_ge(free, items0 + n - 1)
                score(n // nb, n % nb, n % 2, *qb[n % nb]).then_inc(k.scored, 1)
            if n >= 1:
                turn(n - 1)
            if n >= nb + 2 and (n - nb - 2) % nb == 0:
                sum_values((n - nb - 2) // nb)
        sum_values(heads - 1)

    pe.wait_ge(k.const_loaded, 16 * N_CONST)
    pe.wait_ge(k.consts_set, 1)
    pe.wait_ge(k.tokens_loaded, 32)
    for c in range(KC):
        if c >= 4:
            pe.wait_ge(k.turned_out, c - 3)
        for b, (at, n) in enumerate(((0, META), (META, P), (META + P, P))):
            a = pe.transpose(k.ps[:, 4 + c % 4, at:at + n], k.tokens[0:n, b, c * P:(c + 1) * P], k.ident[0:n, 0:n])
        a.then_inc(k.turned, 1)
    pe.wait_ge(k.rows2_loaded, 16 * 8)
    pe.wait_ge(k.turned_out, KC)
    for l in range(DEPTH):
        a = pe.transpose(k.ps[:, 6, l * N2:(l + 1) * N2], k.rows2[:, l, :], k.ident[0:N2, 0:N2])
    a.then_inc(k.cols2_turned, 1)
    pe.wait_ge(k.cols2_ready, 1)

    with pe.Fori(0, DEPTH) as l:
        q, vec0, act0, gates0 = l * (L_UNITS // SLOTS), l * L_VEC, l * L_ACT, l * L_GATES
        pe.wait_ge(k.x_ready, l * 3 + 1)
        stand_alone()
        up(S1["up1"], q, vec0, k.x_hi, k.x_lo, T1)
        pe.wait_ge(k.ff_ready, gates0 + FC)
        all_out(vec0 + (S1["down1"].base + 2), act0 + 2)
        stand_alone()
        down(S1["down1"], q, vec0, k.a_hi1, k.a_lo1, T1, FC)
        pe.wait_ge(k.vec_loaded, l * 96 + 96)
        pe.transpose(k.ps[:, 6, 0:N1], k.rows[:, :], k.ident[0:N1, 0:N1]).then_inc(k.vec_turned, 1)
        layer_norm(l * 3, vec0 + (S1["down1"].base + KC + 2))

        pe.wait_ge(k.x_ready, l * 3 + 2)
        stand_alone()
        wide(S1["win"], q, k.act_evac, act0, k.x_hi, k.x_lo, T1)
        pe.wait_ge(k.lat_squared, l + 1)
        pe.matmul(k.ps[:, 4, 0:T1], k.mean_w[:, :], k.sq[:, 0, :], start=True, stop=False)
        pe.matmul(k.ps[:, 4, 0:T1], k.mean_w[:, :], k.sq[:, 1, :], start=False, stop=True)
        pe.matmul(k.ps[:, 5, 0:T1], k.mean_w[:, :], k.sq[:, 2, :], start=True, stop=True).then_inc(k.lat_mean, 1)
        for n in range(2):
            a = pe.matmul(k.ps[0:QK, 6 + n, 0:T1], k.place[:, n, :], k.mix1[0:ROPE, 15, :], start=True, stop=True)
        a.then_inc(k.kr_placed, 1)
        pe.wait_ge(k.lat_ready, l + 1)
        x_hi, x_lo = k.y_hi[:, 2], k.y_lo[:, 2]
        o = 0

        def acc_free(o):
            pe.wait_ge(k.act_evac, act0 + (S1["uq"].base + o + 1))
        for u in range(2):
            g = S1["uq"].first + u
            weights(g, q)
            for pair in range(2):
                acc_free(o)
                for n in range(2):
                    c = (2 * pair + n) * QK
                    a = chain(k.ps[0:QK, 2 * (o % 2) + n, 0:T1], g % SLOTS, [(kc * 4 * QK + c, QK, kc) for kc in range(2)], x_hi, x_lo)
                a.then_inc(k.unit_done if pair == 1 else k.latent_out, 1)
                o += 1
        g = S1["uk"].first
        weights(g, q)
        for pair in range(4):
            acc_free(o)
            for n in range(2):
                a = chain(k.ps[0:NOPE, 2 * (o % 2) + n, 0:T1], g % SLOTS, [((2 * pair + n) * NOPE, NOPE, 2)], x_hi, x_lo)
            a.then_inc(k.unit_done if pair == 3 else k.latent_out, 1)
            o += 1
        g = S1["uv"].first
        s = g % SLOTS
        weights(g, q)
        for b, (first, n, _) in enumerate(QB1):
            acc_free(o)
            acc, t = k.ps[0:n, 2 * (o % 2), :], slice(first, first + n)
            pe.matmul(acc, x_hi[:, 2, t], k.w_hi[:, s, 0:512], start=True, stop=False)
            pe.matmul(acc, x_lo[:, 2, t], k.w_hi[:, s, 0:512], start=False, stop=False)
            a = pe.matmul(acc, x_hi[:, 2, t], k.w_lo[:, s, 0:512], start=False, stop=True)
            a.then_inc(k.unit_done if b == 2 else k.latent_out, 1)
            o += 1
        pe.wait_ge(k.act_evac, act0 + (S1["uq"].base + 4 + 2))
        pe.wait_ge(k.k_full, l + 1)
        r = slice(NOPE, QK)
        for n in range(2):
            if n:
                pe.wait_ge(k.q_rot_used, l * 2 + 1)
            stand_alone()
            for h in range(4):
                a = pe.matmul(k.ps[r, 4 + h, 0:T1], k.rot[r, :], k.qf[r, 4 * n + h, :], start=True, stop=True)
            a.then_inc(k.q_turned, 1)
        pe.wait_ge(k.q_full, l + 1)
        all_out(vec0 + (S1["branch"].base + 2), act0 + (S1["uv"].base + 3 + 2))

        def mla_score(h, j, b, first, queries, keys):
            return pe.matmul(k.ps[0:queries, 4 + b, 0:keys], k.qf[0:QK, h, first:first + queries], k.kf[0:QK, h, 0:keys], start=True, stop=True)
        heads(l * 24, l * 8, QB1, KB1, HEADS1, mla_score,
              lambda h, n, width: k.vt1[0:width, n, h * VH:(h + 1) * VH],
              lambda h, q0, total: k.ps[VH * (h % 2):VH * (h % 2) + VH, h // 2, q0:total], k.masked)
        pe.wait_ge(k.y_ready, l + 1)
        pe.wait_ge(k.conv_ready, l + 1)
        stand_alone()

        def branch(trip, j, g, q):
            s, b = g % SLOTS, 2 * (j % 2)
            weights(g, q)
            pe.wait_ge(k.vec_evac, vec0 + (trip * SLOTS + j) + (S1["branch"].base + 1))
            for n in range(2):
                a = chain(k.ps[:, b + n, 0:T1], s, [(n * 512 + c * P, P, c) for c in range(4)], k.y_hi[:, n], k.y_lo[:, n])
            a.then_inc(k.unit_done, 1)
        over_units(pe, S1["branch"], q, branch)
        pe.wait_ge(k.merged_ready, l * KC + KC)
        stand_alone()
        wide(S1["wo"], q, k.vec_evac, vec0, k.x_hi, k.x_lo, T1)
        layer_norm(l * 3 + 1, vec0 + (S1["wo"].base + 4 + 2))

        pe.wait_ge(k.x_ready, l * 3 + 3)
        stand_alone()
        up(S1["up2"], q, vec0, k.x_hi, k.x_lo, T1)
        pe.wait_ge(k.ff_ready, gates0 + 2 * FC)
        stand_alone()
        down(S1["down2"], q, vec0, k.a_hi1, k.a_lo1, T1, FC)
        layer_norm(l * 3 + 2, vec0 + (S1["down2"].base + KC + 2))

    x_hi, x_lo = k.x_hi[:, :, 0:T2], k.x_lo[:, :, 0:T2]
    for l in range(DEPTH):
        s = S20 if l == 0 else S21
        rms_norm(2 * l)
        pe.wait_ge(k.x_ready, 3 * DEPTH + 2 * l + 2)
        all_out((DEPTH * L_VEC if l == 0 else V_LAYER1) + 2, s["values"].base + 2)

        def values(trip, j, g, q):
            st, b = g % SLOTS, 2 * (j % 2)
            weights(g, q)
            pe.wait_ge(k.act_evac, s["values"].base + j + 1)
            for t in range(2):
                for kc in range(KC):
                    a = parts_turned(k.ps[:, b + t, 0:256], st, kc * 256, 256, kc, t, kc == 0, kc == KC - 1)
            a.then_inc(k.unit_done, 1)

        def parts_turned(acc, st, c, n, kc, t, first, last):
            tok = slice(t * P, (t + 1) * P)
            pe.matmul(acc, k.x_hi[:, kc, tok], k.w_hi[:, st, c:c + n], start=first, stop=False)
            pe.matmul(acc, k.x_lo[:, kc, tok], k.w_hi[:, st, c:c + n], start=False, stop=False)
            return pe.matmul(acc, k.x_hi[:, kc, tok], k.w_lo[:, st, c:c + n], start=False, stop=last)
        over_units(pe, s["values"], 0, values)
        g = s["small"].first
        weights(g, 0)
        pe.wait_ge(k.act_evac, s["small"].base + 2)
        for t in range(2):
            for half in range(2):
                for kc in range(KC):
                    a = parts_turned(k.ps[:, t, 8 * half:8 * half + 8], g % SLOTS, half * KC * 8 + kc * 8, 8, kc, t, kc == 0, kc == KC - 1)
        a.then_inc(k.unit_done, 1)
        pe.wait_ge(k.act_evac, s["plain"].base + 2)
        wide(s["plain"], 0, k.act_evac, 0, x_hi, x_lo, T2)
        pe.wait_ge(k.lf_ready, l + 1)
        pe.matmul(k.ps[:, 4, 0:12], k.tri[:, :], k.lf[:, 0, :], start=True, stop=True)
        pe.matmul(k.ps[:, 4, 16:28], k.ones[:, :], k.lf[:, 0, :], start=True, stop=False)
        pe.matmul(k.ps[:, 4, 16:28], k.tri[:, :], k.lf[:, 1, :], start=False, stop=True).then_inc(k.cum_summed, 1)
        wide(s["gated"], 0, k.act_evac, 0, x_hi, x_lo, T2)
        g = s["group"].first
        weights(g, 0)
        pe.wait_ge(k.pool_ready, l + 1)
        all_out(s["branch"].base + 2, s["group"].base + 2)
        for n in range(4):
            a = chain(k.ps[:, n, 0:T2], g % SLOTS, [(n * P, P, n)], k.y_hi[:, 2, :, 0:T2], k.y_lo[:, 2, :, 0:T2])
        a.then_inc(k.unit_done, 1)
        pe.wait_ge(k.qk_ready, l + 1)
        pe.wait_ge(k.cum_ready, l + 1)
        all_out(s["branch"].base + 2, s["group"].base + 2 + 2)

        def spread(r, b, keys, log_i):
            for c in range(keys // P):
                col = lambda x, n: x[:, c, n:n + 1].broadcast_to([P, P])
                a = pe.matmul(k.ps[:, 4 + b, 256 + c * P:256 + keys], col(k.lf, r), k.ntri[:, 0:keys - c * P], start=c == 0,
                              stop=not log_i and c == keys // P - 1)
            if log_i:
                for c in range(keys // P):
                    col = lambda x, n: x[:, c, n:n + 1].broadcast_to([P, P])
                    a = pe.matmul(k.ps[:, 4 + b, 256 + c * P:256 + (c + 1) * P], col(k.gx, r), k.ident[:, :], start=False,
                                  stop=c == keys // P - 1)

        def ml_score(h, j, b, first, queries, keys):
            spread(h, b, keys, True)
            return pe.matmul(k.ps[:, 4 + b, 0:keys], k.qkc[:, h, first:first + P], k.qkc[:, 4 + h, 0:keys], start=True, stop=True)

        def fox_score(h, j, b, first, queries, keys):
            spread(4 + h, b, keys, False)
            p = slice(FOX_DH * (h % 2), FOX_DH * (h % 2) + FOX_DH)
            return pe.matmul(k.ps[:, 4 + b, 0:keys], k.mix2[p, 12 + h // 2, first:first + P], k.mix2[p, 16 + h // 2, 0:keys], start=True, stop=True)

        i0, h0 = (DEPTH + l) * 24, DEPTH * 8 + l * 12
        heads(i0, h0, QB2, KB2, ML_HEADS, ml_score, lambda h, n, width: k.vtok[:, n, h * P:(h + 1) * P],
              lambda h, q0, total: k.ps[:, h, q0:total], k.probs_ready)
        pe.wait_ge(k.ml_squared, l + 1)
        for h in range(ML_HEADS):
            a = pe.matmul(k.ps[:, 4 + h // 2, (h % 2) * T2:(h % 2) * T2 + T2], k.mean_w[:, :], k.sq[:, h, 0:T2], start=True, stop=True)
        a.then_inc(k.ml_mean, 1)
        pe.wait_ge(k.ml_ready, l + 1)
        heads(i0 + 2 * ML_HEADS, h0 + ML_HEADS, QB2, KB2, FOX_HEADS, fox_score,
              lambda h, n, width: k.vtok[:, n, 512 + h * FOX_DH:512 + (h + 1) * FOX_DH],
              lambda h, q0, total: k.ps[FOX_DH * (h % 2):FOX_DH * (h % 2) + FOX_DH, h // 2, q0:total], k.probs_ready)
        pe.wait_ge(k.y_ready, DEPTH + l + 1)
        pe.wait_ge(k.ml_parts, l + 1)

        def branch2(trip, j, g, q):
            st, b = g % SLOTS, 2 * (j % 2)
            weights(g, q)
            pe.wait_ge(k.vec_evac, (trip * SLOTS + j) + (s["branch"].base + 1))
            for n in range(3):
                a = chain(k.ps[:, b + n // 2, 256 * (n % 2):256 * (n % 2) + 256], st, [(n * 512 + c * P, P, c) for c in range(4)],
                          k.y_hi[:, n, :, 0:T2], k.y_lo[:, n, :, 0:T2])
            a.then_inc(k.unit_done, 1)
        over_units(pe, s["branch"], 0, branch2)
        pe.wait_ge(k.merged_ready, (DEPTH + l) * KC + KC)
        wide(s["wout"], 0, k.vec_evac, 0, x_hi, x_lo, T2)
        rms_norm(2 * l + 1)
        pe.wait_ge(k.x_ready, 3 * DEPTH + 2 * l + 3)
        if l == 0:
            up(s["up"], 0, 0, x_hi, x_lo, T2)
            pe.wait_ge(k.ff_ready, s["up"].gates + FC)
            down(s["down"], 0, 0, k.a_hi2, k.a_lo2, T2, FC)

    for t in range(2):
        for c in range(KC):
            a = pe.matmul(k.ps[:, 4, t * EXPERTS:(t + 1) * EXPERTS], k.sq[:, c, t * P:(t + 1) * P], k.wr[:, c, :], start=c == 0, stop=c == KC - 1)
    a.then_inc(k.routed, 1)
    pe.wait_ge(k.gates_ready, 1)
    for e in range(EXPERTS):
        for t in range(2):
            a = pe.matmul(k.ps[:, 4 + e // 2, (e % 2) * T2 + t * P:(e % 2) * T2 + (t + 1) * P],
                          k.gates[:, t, e:e + 1].broadcast_to([P, P]), k.ident[:, :], start=True, stop=True)
    a.then_inc(k.gate_spread, 1)

    def expert(e, sched):
        q = e * (E_UNITS // SLOTS)
        up(sched["up"], q, e * E_OUT, x_hi, x_lo, T2)
        pe.wait_ge(k.ff_ready, e * EC + (sched["up"].gates + EC))
        stand_alone()
        down(sched["down"], q, e * E_OUT, k.a_hi2, k.a_lo2, T2, EC)
    with pe.Fori(0, EXPERTS - 1) as e:
        expert(e, SE)
    expert(EXPERTS - 1, SE_LAST)

    rms_norm(2 * DEPTH)
    pe.wait_ge(k.h_ready, 3 * DEPTH + 2 * DEPTH + 1)
    for b in range(4):
        for n in range(4):
            c = (b % 2) * 4 + n
            a = pe.transpose(k.ps[:, 4 + b, n * P:(n + 1) * P], k.out_fm[:, c, (b // 2) * P:(b // 2 + 1) * P], k.ident[:, :])
        a.then_inc(k.out_turned, 1)


def build(nc, i, out):
    with ExitStack() as ctx:
        k = allocate(nc, ctx)
        block = ctx.enter_context(nc.Block())

        @block.sync
        def _(sp):
            sp_program(sp, k, i, out)

        @block.scalar
        def _(act):
            act_program(act, k, i, out)

        @block.vector
        def _(vec):
            vec_program(vec, k, i, out)

        @block.gpsimd
        def _(pool):
            pool_program(pool, k, i, out)

        @block.tensor
        def _(pe):
            pe_program(pe, k, i, out)


def constants():
    t = np.arange(T1, dtype=np.float32)
    freq = (np.float32(1.0) / (np.float32(10000.0) ** (np.arange(0, ROPE, 2, dtype=np.float32) / np.float32(ROPE)))).astype(np.float32)
    ang = (freq[:, None] * t[None, :]).astype(np.float32)
    half = ROPE // 2
    rot = np.zeros((P, ROPE), np.float32)
    place = np.zeros((ROPE, 2, QK), np.float32)
    for m in range(half):
        rot[NOPE + m + half, m], rot[NOPE + m, m + half] = -1.0, 1.0
        place[m + half, 1, NOPE + m], place[m, 1, NOPE + m + half] = -1.0, 1.0
    for m in range(ROPE):
        place[m, 0, NOPE + m] = 1.0
    row = np.arange(P)
    tri = (row[:, None] <= row[None, :]).astype(np.float32)
    mask = np.zeros((P, 3 * P), np.float32)
    mask[:, 2 * P:] = np.where(row[None, :] <= row[:, None], 0.0, NEG)
    pos = np.arange(16)
    icnt = np.stack([1.0 / np.minimum(pos + 1, w) for w in (2, 4, 8, 16)]).astype(np.float32)
    return {
        "c_ident": np.eye(P, dtype=np.float32), "c_tri": tri,
        "c_ntri": np.concatenate([-tri, -np.ones((P, P), np.float32)], 1), "c_mask": mask, "c_rot": rot,
        "c_cos": np.tile(np.cos(ang), (2, 1)), "c_sin": np.tile(np.sin(ang), (2, 1)), "c_place": place, "c_icnt": icnt,
        "c_eidx": np.arange(EXPERTS, dtype=np.float32)[None, :],
    }


def kernel(**inputs):
    import concourse.bacc as bacc
    from concourse.bass_utils import run_bass_kernel_spmd

    nc = bacc.Bacc("TRN2", target_bir_lowering=False, num_devices=1)
    arrays, aps = {}, {}
    for name, a in {**inputs, **constants()}.items():
        a = np.ascontiguousarray(a)
        arrays[f"in_{name}"] = a
        aps[name] = nc.dram_tensor(f"in_{name}", a.shape, mybir.dt.from_np(a.dtype), kind="ExternalInput").ap()
    out = nc.dram_tensor("out", (1, SEQ, D), F32, kind="ExternalOutput").ap()
    build(nc, aps, out)
    r = run_bass_kernel_spmd(nc, [arrays], core_ids=[0])
    return r.results[0]["out"]
```

```python
from contextlib import ExitStack

import numpy as np

import concourse.bass as bass
from concourse import mybir

F32 = mybir.dt.float32
F16 = mybir.dt.float16
U32 = mybir.dt.uint32
I32 = mybir.dt.int32
ALU = mybir.AluOpType
ACT = mybir.ActivationFunctionType
AX = mybir.AxisListType

P = 128
D = 1024
KC = D // P
SEQ = 256
META = 16
T1 = SEQ + META
T2 = SEQ
DEPTH = 2
FF = 2816
FC = FF // P
FFE = 3584
EC = FFE // P
EXPERTS = 8
HEADS1 = 8
NOPE, ROPE, VH = 64, 32, 64
QK = NOPE + ROPE
ML_HEADS = 4
FOX_HEADS, FOX_DH = 8, 64
ALPHA = (2 * DEPTH) ** 0.25
LN_EPS, RMS_EPS = 1e-5, 1e-6
NEG = -1e30
WS = 64.0
UNW = 1.0 / WS
SLOTS = 4
AHEAD = 2
UNIT = 16 * P


DOWN_COLS = 256
DOWN_BLOCKS = D // DOWN_COLS
DOWN_GROUPS = 4
HI_GATHERED, HI_TAKEN, LO_GATHERED, LO_TAKEN = (0, 3), (1, 0), (1, 3), (2, 0)


class Phase:

    def __init__(self, first, units, size, base, after, gates):
        self.first, self.units, self.size, self.base, self.after, self.gates = first, units, size, base, after, gates


def schedule(rows, first, vec, act, gates, behind):
    out = {}
    sizes = [size for _, units, size, _, _, _ in rows for _ in range(units)] + behind
    at = 0
    for name, units, size, who, outputs, up in rows:
        out[name] = Phase(first + at, units, size, vec if who == "vec" else act, sizes[at + units:at + units + 2], gates)
        at += units
        vec += outputs if who == "vec" else 0
        act += outputs if who == "act" else 0
        gates += outputs if up else 0
    return out, first + at, vec, act, gates


ROWS1 = [
    ("up1", FC, UNIT, "vec", FC, True),
    ("down1", 2 * KC, FC // 2 * P, "vec", KC, False),
    ("win", 16, UNIT, "act", 16, False),
    ("uq", 2, 2 * 4 * QK, "act", 4, False),
    ("uk", 1, HEADS1 * NOPE, "act", 4, False),
    ("uv", 1, HEADS1 * VH, "act", 3, False),
    ("branch", KC, 8 * P, "vec", KC, False),
    ("wo", 4, UNIT, "vec", 4, False),
    ("up2", FC, UNIT, "vec", FC, True),
    ("down2", 2 * KC, FC // 2 * P, "vec", KC, False),
]
MIX2 = [
    ("values", 4, UNIT, "act", 4, False),
    ("small", 1, KC * 16, "act", 1, False),
    ("plain", 10, UNIT, "act", 10, False),
    ("gated", 14, UNIT, "act", 14, False),
    ("group", 1, 4 * P, "act", 2, False),
    ("branch", KC, 12 * P, "vec", KC, False),
    ("wout", 4, UNIT, "vec", 4, False),
]
DENSE2 = [("up", FC, UNIT, "vec", FC, True), ("down", 2 * KC, FC // 2 * P, "vec", KC, False)]
EXPERT2 = [("up", EC, UNIT, "vec", EC, True), ("down", DOWN_BLOCKS * DOWN_GROUPS, EC // DOWN_GROUPS * DOWN_COLS, "vec", 0, False)]

S1, L_UNITS, L_VEC, L_ACT, L_GATES = schedule(ROWS1, 0, 0, 0, 0, [UNIT, UNIT])
S20, g_, v_, a_, s_ = schedule(MIX2 + DENSE2, DEPTH * L_UNITS, DEPTH * L_VEC, DEPTH * L_ACT, DEPTH * L_GATES, [UNIT, UNIT])
V_LAYER1 = v_
S21, E_FIRST, E_VEC, E_ACT, E_GATES = schedule(MIX2, g_, v_, a_, s_, [UNIT, UNIT])
SE, g_, _, _, _ = schedule(EXPERT2, E_FIRST, E_VEC, E_ACT, E_GATES, [UNIT, UNIT])
E_UNITS = g_ - E_FIRST
SE_LAST, _, _, _, _ = schedule(EXPERT2, E_FIRST, E_VEC, E_ACT, E_GATES, [0, 0])
assert L_UNITS % SLOTS == 0 and E_UNITS % SLOTS == 0
V_END0 = S21["branch"].base
A_PER2 = 4 + 1 + 10 + 14 + 2

C1 = {"ln_g": 0, "ln_b": 24, "gate_b": 48, "conv": 64, "q_g": 76, "kv_g": 78}
N1 = 79
C2 = {"mix_g": 0, "pool_s": 8, "conv": 12, "ml_g": 44, "ffn_g": 48}
N2 = 56
N_CONST = 17
QB2 = [(0, 128, 128), (128, 128, 256)]
KB2 = [(0, 0, 128, 0), (128, 256, 128, 128)]
QB1 = [(0, 128, 128), (128, 128, 256), (256, 16, 272)]
KB1 = [(0, 0, 128, 0), (128, 272, 128, 128), (256, 416, 16, 256)]


def over_units(eng, phase, quads, body, loop=True):
    trips = phase.units // SLOTS if loop else 0
    if trips > 1:
        with eng.Fori(0, trips) as trip:
            for j in range(SLOTS):
                body(trip, j, phase.first + j, quads + trip)
    else:
        trips = 0
    for u in range(trips * SLOTS, phase.units):
        body(u // SLOTS, u % SLOTS, phase.first + u % SLOTS, quads + u // SLOTS)


def over_units_ahead(eng, phase, quads, split, take, loop=True):
    same = phase.after == [phase.size, phase.size]
    inner = phase.units if same else max(phase.units - AHEAD, 0)
    trips = inner // SLOTS if loop else 0

    def step(trip, j, q, size, take_first=False):
        g = phase.first + j
        if take_first:
            take(trip, j, g, q)
        if size:
            split(g + AHEAD, q, size)
        if not take_first:
            take(trip, j, g, q)

    if trips > 1:
        with eng.Fori(0, trips) as trip:
            for j in range(SLOTS):
                step(trip, j, quads + trip, phase.size)
    else:
        trips = 0
    for u in range(trips * SLOTS, phase.units):
        late = u + AHEAD - phase.units
        step(u // SLOTS, u % SLOTS, quads + u // SLOTS, phase.size if late < 0 else phase.after[late], take_first=late == AHEAD - 1)


class Core:
    pass


def allocate(nc, ctx):
    k = Core()

    def sb(name, shape, dt):
        return ctx.enter_context(nc.sbuf_tensor(name, shape, dt))

    def sem(name):
        return ctx.enter_context(nc.semaphore(name))

    k.w32 = sb("w32", [P, SLOTS, UNIT], F32)
    k.w_hi = sb("w_hi", [P, SLOTS, UNIT], F16)
    k.w_lo = sb("w_lo", [P, SLOTS, UNIT], F16)
    k.h = sb("h", [P, KC, T1], F32)
    k.x_hi = sb("x_hi", [P, KC, T1], F16)
    k.x_lo = sb("x_lo", [P, KC, T1], F16)
    k.sq = sb("sq", [P, KC, T1], F32)
    ff = sb("ff", [P, EC * T2], F32)
    k.a_hi1 = ff[:, 0:FC * T1 // 2].bitcast(F16).rearrange("p (c t) -> p c t", t=T1)
    k.a_lo1 = ff[:, FC * T1 // 2:FC * T1].bitcast(F16).rearrange("p (c t) -> p c t", t=T1)
    k.a_hi2 = ff[:, 0:EC * T2 // 2].bitcast(F16).rearrange("p (c t) -> p c t", t=T2)
    k.a_lo2 = ff[:, EC * T2 // 2:EC * T2].bitcast(F16).rearrange("p (c t) -> p c t", t=T2)
    k.a_hi3 = ff[:, 0:EC * P // 2].bitcast(F16).rearrange("p (c t) -> p c t", t=P)
    k.a_lo3 = ff[:, EC * P // 2:EC * P].bitcast(F16).rearrange("p (c t) -> p c t", t=P)
    n = HEADS1 * T1
    k.qf = ff[:, 0:n].rearrange("p (h t) -> p h t", t=T1)
    k.kf = ff[:, n:2 * n].rearrange("p (h t) -> p h t", t=T1)
    k.rope_a = ff[:, 2 * n:3 * n].rearrange("p (h t) -> p h t", t=T1)
    k.qkc = ff[:, 0:8 * T2].rearrange("p (c t) -> p c t", t=T2)
    k.vtok = ff[:, 8 * T2:16 * T2].rearrange("p (t n) -> p t n", n=4 * T2)
    k.tap = ff[:, 16 * T2:24 * T2].rearrange("p (c t) -> p c t", t=T2)
    mix = sb("mix", [P, 48 * T2], F32)
    k.mix1 = mix[:, 0:32 * T1].rearrange("p (c t) -> p c t", t=T1)
    k.vt1 = mix[:, 32 * T1:32 * T1 + 3 * 512].rearrange("p (b n) -> p b n", n=512)
    k.mix2 = mix[:, :].rearrange("p (c t) -> p c t", t=T2)
    k.tokens = mix[:, 0:3 * D].rearrange("p (b n) -> p b n", n=D)
    k.xt_hi = mix[:, 0:D].bitcast(F16).rearrange("p (b n) -> p b n", n=D)
    k.xt_lo = mix[:, D:2 * D].bitcast(F16).rearrange("p (b n) -> p b n", n=D)
    k.to_slot = mix[:, 2 * D:3 * D].bitcast(F16).rearrange("p (b e s) -> p b e s", b=2, s=P)
    k.to_token = mix[:, 3 * D:4 * D].bitcast(F16).rearrange("p (e t) -> p e t", t=T2)
    k.d_hi = mix[:, 4 * D:4 * D + DOWN_COLS // 2].bitcast(F16)
    k.d_lo = mix[:, 4 * D + DOWN_COLS // 2:4 * D + DOWN_COLS].bitcast(F16)
    at = 4 * D + DOWN_COLS
    k.final_g = mix[:, at:at + D]
    k.out_rows = mix[:, at + D:at + 3 * D].rearrange("p (b n) -> p b n", n=D)
    k.squares = mix[:, at + 3 * D:at + 5 * D].rearrange("p (b n) -> p b n", n=D)
    k.zeros = mix[:, at + 5 * D:at + 5 * D + 256].bitcast(F16)
    k.prod = sb("prod", [P, 2, T1], F32)
    k.tmp = sb("tmp", [P, 3, T1], F32)
    k.silu = k.tmp[:, 0:2, :]
    k.y_hi = sb("y_hi", [P, 3, 4, T1], F16)
    k.y_lo = sb("y_lo", [P, 3, 4, T1], F16)
    k.pa = sb("pa", [P, 4, T1 + 2], F32)
    k.pb = sb("pb", [P, 4, T1 + 2], F32)
    at = 2 * n
    k.sc = ff[:, at:at + 2 * T1].rearrange("p (b t) -> p b t", t=T1)
    k.pr = ff[:, at + 2 * T1:at + 4 * T1].rearrange("p (b t) -> p b t", t=T1)
    at += 4 * T1
    k.pt = ff[:, at:at + 2 * 432].rearrange("p (b t) -> p b t", t=432)
    at += 2 * 432
    k.gm = ff[:, at:at + 2 * T2].rearrange("p (b t) -> p b t", t=T2)
    k.stat = sb("stat", [P, 2, 8], F32)
    k.std = k.sq[:, 6:8, :]
    k.rstd = sb("rstd", [P, 2, T1], F32)
    k.gp = sb("gp", [P, 2, 16], F32)
    k.gx = sb("gx", [P, 2, 16], F32)
    k.ge = sb("ge", [P, 2, 16], F32)
    k.gl = sb("gl", [P, 2, 16], F32)
    k.lf = sb("lf", [P, 2, 12], F32)
    k.cum = sb("cum", [P, 2, 12], F32)
    k.gbias = sb("gbias", [P, DEPTH, 16], F32)
    k.wr = sb("wr", [P, KC, EXPERTS], F32)
    k.rb = sb("rb", [P, EXPERTS], F32)
    k.lg = sb("lg", [P, 2, EXPERTS], F32)
    k.top = sb("top", [P, 2, 8], F32)
    k.topi = sb("topi", [P, 2, 8], U32)
    k.topf = sb("topf", [P, 2, 8], F32)
    k.rt = sb("rt", [P, 2, 8], F32)
    k.ga = sb("ga", [P, 2, EXPERTS], F32)
    k.gb = sb("gb", [P, 2, EXPERTS], F32)
    k.gates = sb("gates", [P, 2, EXPERTS], F32)
    k.member = sb("member", [P, 2, EXPERTS], F32)
    k.sel = sb("sel", [P, 2, EXPERTS], F32)
    k.slot_gate = sb("slot_gate", [P, EXPERTS], F32)
    k.gate_now = sb("gate_now", [P, 1], F32)
    k.most = sb("most", [P, 1], F32)
    k.more = sb("more", [P, 1], I32)
    k.slots = sb("slots", [P, P], F32)
    k.slot_col = sb("slot_col", [P, 1], F32)
    k.ms = sb("ms", [P, 2, 4], F32)
    k.rows = sb("rows", [N1, P], F32)
    k.col = sb("col", [P, N1], F32)
    k.rows2 = sb("rows2", [N2, DEPTH, P], F32)
    k.col2 = sb("col2", [P, DEPTH, N2], F32)
    k.pscale = sb("pscale", [P, DEPTH, 4], F32)
    k.ident = sb("ident", [P, P], F32)
    k.tri = sb("tri", [P, P], F32)
    k.ntri = sb("ntri", [P, 2 * P], F32)
    k.mask = sb("mask", [P, 3 * P], F32)
    k.mean_w = sb("mean_w", [P, P], F32)
    k.ones = sb("ones", [P, P], F32)
    k.cos = sb("cos", [P, T1], F32)
    k.sin = sb("sin", [P, T1], F32)
    k.rot = sb("rot", [P, ROPE], F32)
    k.place = sb("place", [ROPE, 2, QK], F32)
    k.icnt = sb("icnt", [P, 4, 16], F32)
    k.eidx = sb("eidx", [P, EXPERTS], F32)
    k.eps = sb("eps", [P, 3], F32)
    k.ps = ctx.enter_context(nc.psum_tensor("ps", [P, 8, 512], F32))

    k.loaded = [sem(f"loaded{j}") for j in range(SLOTS)]
    k.fox_loaded = [sem(f"fox_loaded{j}") for j in range(SLOTS)]
    k.hi_ready = sem("hi_ready")
    k.parts_ready = sem("parts_ready")
    k.unit_done = sem("unit_done")
    k.vec_evac = sem("vec_evac")
    k.act_evac = sem("act_evac")
    k.silu_ready = sem("silu_ready")
    k.ff_ready = sem("ff_ready")
    k.const_loaded = sem("const_loaded")
    k.consts_set = sem("consts_set")
    k.vec_loaded = sem("vec_loaded")
    k.vec_turned = sem("vec_turned")
    k.vec_ready = sem("vec_ready")
    k.tokens_loaded = sem("tokens_loaded")
    k.turned = sem("turned")
    k.turned_out = sem("turned_out")
    k.h_ready = sem("h_ready")
    k.x_hi_ready = sem("x_hi_ready")
    k.x_ready = sem("x_ready")
    k.ln_mean = sem("ln_mean")
    k.ln_centered = sem("ln_centered")
    k.ln_squared = sem("ln_squared")
    k.ln_var = sem("ln_var")
    k.ln_std = sem("ln_std")
    k.lat_squared = sem("lat_squared")
    k.lat_mean = sem("lat_mean")
    k.lat_std = sem("lat_std")
    k.lat_normed = sem("lat_normed")
    k.lat_hi = sem("lat_hi")
    k.lat_ready = sem("lat_ready")
    k.kr_placed = sem("kr_placed")
    k.q_turned = sem("q_turned")
    k.q_rot_used = sem("q_rot_used")
    k.k_full = sem("k_full")
    k.q_full = sem("q_full")
    k.conv_ready = sem("conv_ready")
    k.scored = sem("scored")
    k.masked = sem("masked")
    k.exped = sem("exped")
    k.probs_ready = sem("probs_ready")
    k.pt_written = sem("pt_written")
    k.pt_ready = sem("pt_ready")
    k.heads_summed = sem("heads_summed")
    k.y_hi_ready = sem("y_hi_ready")
    k.y_ready = sem("y_ready")
    k.merged_ready = sem("merged_ready")
    k.small_ready = sem("small_ready")
    k.gate_ln = sem("gate_ln")
    k.lf_ready = sem("lf_ready")
    k.cum_summed = sem("cum_summed")
    k.cum_ready = sem("cum_ready")
    k.pool_ready = sem("pool_ready")
    k.taps_ready = sem("taps_ready")
    k.qk_ready = sem("qk_ready")
    k.ml_squared = sem("ml_squared")
    k.ml_mean = sem("ml_mean")
    k.ml_std = sem("ml_std")
    k.ml_ready = sem("ml_ready")
    k.rms_squared = sem("rms_squared")
    k.rms_mean = sem("rms_mean")
    k.rms_std = sem("rms_std")
    k.zeros_set = sem("zeros_set")
    k.routed = sem("routed")
    k.xt_turned = sem("xt_turned")
    k.xt_hi_ready = sem("xt_hi_ready")
    k.xt_ready = sem("xt_ready")
    k.member_ready = sem("member_ready")
    k.rank_summed = sem("rank_summed")
    k.sel_ready = sem("sel_ready")
    k.sel_spread = sem("sel_spread")
    k.choice_ready = sem("choice_ready")
    k.more_ready = sem("more_ready")
    k.slots_ready = sem("slots_ready")
    k.hi_gathered = sem("hi_gathered")
    k.lo_gathered = sem("lo_gathered")
    k.xe_hi_ready = sem("xe_hi_ready")
    k.xe_ready = sem("xe_ready")
    k.down_hi_ready = sem("down_hi_ready")
    k.down_ready = sem("down_ready")
    k.all_added = sem("all_added")
    k.final_g_loaded = sem("final_g_loaded")
    k.final_std = sem("final_std")
    k.row_ready = sem("row_ready")
    k.lg_ready = sem("lg_ready")
    k.lg_exped = sem("lg_exped")
    k.gates_ready = sem("gates_ready")
    k.gate_spread = sem("gate_spread")
    k.stored = sem("stored")
    k.rows2_loaded = sem("rows2_loaded")
    k.cols2_turned = sem("cols2_turned")
    k.cols2_ready = sem("cols2_ready")
    k.pe_steps = sem("pe_steps")
    k.pool_steps = sem("pool_steps")
    k.latent_out = sem("latent_out")
    k.ml_hi = sem("ml_hi")
    k.ml_parts = sem("ml_parts")
    return k


def sp_program(sp, k, i, out):
    def slot(g, q, shape_a, src_a, shape_b=None, src_b=None):
        s = g % SLOTS
        sp.wait_ge(k.parts_ready, q * SLOTS + (g + 1))
        lo = 0
        for (c, n), src in ((shape_a, src_a), (shape_b, src_b)):
            dst = k.w32[:, s, lo:lo + c * n].rearrange("p (c n) -> p c n", n=n)
            sp.dma_start(dst, src).then_inc(k.loaded[s], 16)
            lo += c * n

    def chunks(w, c0, c, n0, n):
        return w[c0 * P:(c0 + c) * P, :][:, bass.ds(n0, n)].rearrange("(c p) n -> p c n", p=P)

    def up(phase, q, w_gate, w_up, gate0, up0):
        def unit(trip, j, g, q):
            u = (trip * SLOTS + j) * P
            slot(g, q, (KC, P), chunks(w_gate, 0, KC, u + gate0, P), (KC, P), chunks(w_up, 0, KC, u + up0, P))
        over_units(sp, phase, q, unit)

    def down(phase, q, w, fc):
        half, part = fc // 2, fc // 4
        cut = [(0, part), (part, half - part)]

        def unit(trip, j, g, q):
            m = (trip * 2 + j // 2) * P
            at = (j % 2) * half
            (a0, an), (b0, bn) = cut
            slot(g, q, (an, P), chunks(w, at + a0, an, m, P), (bn, P), chunks(w, at + b0, bn, m, P))
        over_units(sp, phase, q, unit)

    def wide(phase, q, w, col):
        def unit(trip, j, g, q):
            c = col(trip, j)
            slot(g, q, (KC // 2, 256), chunks(w, 0, KC // 2, c, 256), (KC // 2, 256), chunks(w, KC // 2, KC // 2, c, 256))
        over_units(sp, phase, q, unit)

    def part(phase, first, units):
        return Phase(phase.first + first, units, phase.size, 0, [], 0)

    with sp.Fori(0, DEPTH) as l:
        q = l * (L_UNITS // SLOTS)
        up(S1["up1"], q, i["ffn1_w_up"][l], i["ffn1_w_up"][l], 0, FF)
        down(S1["down1"], q, i["ffn1_w_down"][l], FC)
        w_in = i["mix_w_in"][l]
        win = S1["win"]
        over = lambda t, j: (t * SLOTS + j) * 256
        for u in range(16):
            c0 = u * 256 if u < 8 else 1952 + (u - 8) * 256
            slot(win.first + u % SLOTS, q + u // SLOTS, (KC // 2, 256), chunks(w_in, 0, KC // 2, c0, 256),
                 (KC // 2, 256), chunks(w_in, KC // 2, KC // 2, c0, 256))
        for u in range(2):
            n = 4 * QK
            slot(S1["uq"].first + u, q, (1, n), chunks(i["w_uq"][l], 0, 1, u * n, n), (1, n), chunks(i["w_uq"][l], 1, 1, u * n, n))
        kv = i["w_ukv"][l].rearrange("p (h n) -> p h n", n=NOPE + VH)
        for u, name in enumerate(("uk", "uv")):
            slot(S1[name].first, q, (4, NOPE), kv[:, 0:4, u * NOPE:(u + 1) * NOPE], (4, NOPE), kv[:, 4:8, u * NOPE:(u + 1) * NOPE])

        def branch(trip, j, g, q):
            m = (trip * SLOTS + j) * P
            slot(g, q, (4, P), chunks(i["w_br_conv"][l], 0, 4, m, P), (4, P), chunks(i["w_br_mla"][l], 0, 4, m, P))
        over_units(sp, S1["branch"], q, branch)
        wide(S1["wo"], q, i["w_o"][l], over)
        up(S1["up2"], q, i["ffn2_w_up"][l], i["ffn2_w_up"][l], 0, FF)
        down(S1["down2"], q, i["ffn2_w_down"][l], FC)

    for l in range(DEPTH):
        s = S20 if l == 0 else S21
        w_in = i["w_in_2"][l]
        wide(s["values"], 0, w_in, lambda t, j: 1536 + 256 * j if j < 2 else 3592 + 256 * (j - 2))
        g = s["small"].first
        slot(g, 0, (KC, 8), chunks(w_in, 0, KC, 2560, 8), (KC, 8), chunks(w_in, 0, KC, 4104, 8))
        wide(part(s["plain"], 0, 6), 0, w_in, lambda t, j: (t * SLOTS + j) * 256)
        wide(part(s["plain"], 6, 4), 0, w_in, lambda t, j: 2568 + (t * SLOTS + j) * 256)
        wide(part(s["gated"], 0, 2), 0, w_in, lambda t, j: 2048 + (t * SLOTS + j) * 256)
        wide(part(s["gated"], 2, 12), 0, w_in, lambda t, j: 4112 + (t * SLOTS + j) * 256)
        grp = i["pool_w_grp_2"][l].rearrange("g c n -> c g n")
        slot(s["group"].first, 0, (2, P), grp[:, 0:2, :], (2, P), grp[:, 2:4, :])

        def branch2(trip, j, g, q):
            m = (trip * SLOTS + j) * P
            slot(g, q, (4, P), chunks(i["w_br_pool_2"][l], 0, 4, m, P), (4, P), chunks(i["w_br_ml_2"][l], 0, 4, m, P))
            dst = k.w32[:, g % SLOTS, 8 * P:12 * P].rearrange("p (c n) -> p c n", n=P)
            sp.dma_start(dst, chunks(i["w_br_fox_2"][l], 0, 4, m, P)).then_inc(k.fox_loaded[g % SLOTS], 16)
        over_units(sp, s["branch"], 0, branch2)
        wide(s["wout"], 0, i["w_out_2"][l], lambda t, j: (t * SLOTS + j) * 256)
        if l == 0:
            up(s["up"], 0, i["ff_w_gate_2"][0], i["ff_w_up_2"][0], 0, 0)
            down(s["down"], 0, i["ff_w_down_2"][0], FC)

    def moe_round(r):
        with sp.Fori(0, EXPERTS) as e:
            q = (e + r * EXPERTS) * (E_UNITS // SLOTS)
            up(SE["up"], q, i["moe_w_gate_2"][0][e], i["moe_w_up_2"][0][e], 0, 0)
            w = i["moe_w_down_2"][0][e]
            n = EC // DOWN_GROUPS

            def unit(trip, j, g, q):
                c, col = n * j, trip * DOWN_COLS
                slot(g, q, (n // 2, DOWN_COLS), chunks(w, c, n // 2, col, DOWN_COLS),
                     (n - n // 2, DOWN_COLS), chunks(w, c + n // 2, n - n // 2, col, DOWN_COLS))
            over_units(sp, SE["down"], q, unit)
    moe_round(0)
    sp.wait_ge(k.more_ready, 1)
    more = sp.value_load(k.more[0:1, 0:1], min_val=0, max_val=1)
    with sp.If(more > 0):
        moe_round(1)


def act_program(act, k, i, out):
    def split(g, q, size):
        s = g % SLOTS
        act.wait_ge(k.loaded[s], (q + g // SLOTS) * 32 + 32)
        if size == 12 * P:
            layer = 0 if g < S21["values"].first else 1
            first = (S20, S21)[layer]["branch"].first
            act.wait_ge(k.fox_loaded[s], (q + (g - first) // SLOTS + 2 * layer) * 16 + 16)
        act.wait_ge(k.unit_done, q * SLOTS + (g + 1))
        act.activation(k.w_hi[:, s, 0:size], k.w32[:, s, 0:size], ACT.Copy, scale=WS).then_inc(k.hi_ready, 1)

    def unit_used(g, q):
        act.wait_ge(k.unit_done, q * SLOTS + (g + 1 + SLOTS))

    def up(phase, q, vec0, gates0, t):
        def take(trip, j, g, q):
            o = trip * SLOTS + j
            unit_used(g, q)
            act.wait_ge(k.vec_evac, vec0 + o + (phase.base + 1))
            act.activation(k.silu[:, j % 2, 0:t], k.ps[:, 2 * (j % 2), 0:t], ACT.Silu, scale=UNW).then_inc(k.silu_ready, 1)
        over_units_ahead(act, phase, q, split, take)

    def ahead_only(phase, q):
        over_units_ahead(act, phase, q, split, lambda trip, j, g, q: None)

    def layer_norm(n):
        act.wait_ge(k.ln_centered, n + 1)
        act.activation(k.sq[:, :, :], k.h[:, :, :], ACT.Square).then_inc(k.ln_squared, 1)
        act.wait_ge(k.ln_var, n + 1)
        act.activation(k.std[:, 0, :], k.ps[:, 5, 0:T1], ACT.Sqrt, bias=k.eps[:, 0:1]).then_inc(k.ln_std, 1)
        act.wait_ge(k.h_ready, n + 1)
        act.activation(k.x_hi[:, :, :], k.h[:, :, :], ACT.Copy).then_inc(k.x_hi_ready, 1)

    def rms_norm(n, to_parts=True):
        act.activation(k.sq[:, :, 0:T2], k.h[:, :, META:T1], ACT.Square).then_inc(k.rms_squared, 1)
        act.wait_ge(k.rms_mean, n + 1)
        act.activation(k.std[:, 0, 0:T2], k.ps[:, 4, 0:T2], ACT.Sqrt, bias=k.eps[:, 1:2]).then_inc(k.rms_std, 1)
        if to_parts:
            act.wait_ge(k.h_ready, 3 * DEPTH + n + 1)
            act.activation(k.x_hi[:, :, 0:T2], k.sq[:, :, 0:T2], ACT.Copy).then_inc(k.x_hi_ready, 1)

    def heads(items0, heads0, blocks, heads, exp, last_rows):
        nb = len(blocks)
        items = heads * nb

        def copy(h):
            act.wait_ge(k.pt_written, items0 + nb * (h + 1))
            if h >= 2:
                act.wait_ge(k.heads_summed, heads0 + h - 1)
            if last_rows:
                act.activation(k.pt[:, h % 2, 0:416], k.ps[:, 6 + h % 2, 0:416], ACT.Copy)
                act.activation(k.pt[0:last_rows, h % 2, 416:432], k.ps[0:last_rows, 6 + h % 2, 416:432], ACT.Copy).then_inc(k.pt_ready, 1)
            else:
                act.activation(k.pt[:, h % 2, 0:384], k.ps[:, 6 + h % 2, 0:384], ACT.Copy).then_inc(k.pt_ready, 1)

        for n in range(items):
            act.wait_ge(k.masked, items0 + n + 1)
            if n >= 2:
                act.wait_ge(k.pt_written, items0 + n - 1)
            exp(n % 2, *blocks[n % nb][1:])
            if n >= nb + 1 and (n - nb - 1) % nb == 0:
                copy((n - nb - 1) // nb)
        copy(heads - 1)

    def softmax_exp(b, queries, keys):
        act.activation(k.pr[0:queries, b, 0:keys], k.sc[0:queries, b, 0:keys], ACT.Exp, bias=k.stat[0:queries, b, 0:1],
                       accum_out=k.stat[0:queries, b, 1:2]).then_inc(k.exped, 1)

    def ml_exp(b, queries, keys):
        act.activation(k.pr[:, b, 0:keys], k.sc[:, b, 0:keys], ACT.Exp, bias=k.stat[:, b, 1:2])
        act.activation(k.stat[:, b, 4:5], k.stat[:, b, 1:2], ACT.Exp).then_inc(k.exped, 1)

    n_const = 0
    for dst, src in ((k.ident, "c_ident"), (k.tri, "c_tri"), (k.ntri, "c_ntri"), (k.mask, "c_mask"), (k.rot, "c_rot")):
        act.dma_start(dst[:, :], i[src]).then_inc(k.const_loaded, 16)
        n_const += 1
    act.dma_start(k.tokens[0:META, 0, :], i["meta_tokens"]).then_inc(k.tokens_loaded, 16)
    act.dma_start(k.tokens[:, 1:3, :], i["x"][0].rearrange("(b p) d -> p b d", p=P)).then_inc(k.tokens_loaded, 16)
    for dst, src in ((k.cos[64:96, :], i["c_cos"]), (k.sin[64:96, :], i["c_sin"]), (k.place[:, :, :], i["c_place"]),
                     (k.icnt[:, :, :], i["c_icnt"].rearrange("(a g) t -> a g t", a=1).broadcast_to([P, 4, 16])),
                     (k.eidx[:, :], i["c_eidx"].broadcast_to([P, EXPERTS])),
                     (k.slots[:, :], i["c_slots"].broadcast_to([P, P])),
                     (k.slot_col[:, :], i["c_slots"].rearrange("a s -> s a")),
                     (k.rb[:, :], i["moe_b_router_2"].broadcast_to([P, EXPERTS])),
                     (k.wr[:, :, :], i["moe_w_router_2"][0].rearrange("(c p) e -> p c e", p=P))):
        act.dma_start(dst, src).then_inc(k.const_loaded, 16)
        n_const += 1
    for name, c0, n in (("ml_b_i_2", 0, 4), ("ml_b_f_2", 4, 4), ("fox_b_f_2", 8, 8)):
        act.dma_start(k.gbias[:, :, c0:c0 + n], i[name].rearrange("(a l) n -> a l n", a=1).broadcast_to([P, DEPTH, n])).then_inc(k.const_loaded, 16)
        n_const += 1
    assert n_const == N_CONST
    for name, n in (("mix_g", 8), ("pool_s", 4), ("ml_g", 4), ("ffn_g", 8)):
        src = {"mix_g": "mix_norm_g_2", "pool_s": "pool_scale_2", "ml_g": "ml_norm_g_2", "ffn_g": "ffn_norm_g_2"}[name]
        act.dma_start(k.rows2[C2[name]:C2[name] + n, :, :], i[src].rearrange("l (c p) -> c l p", p=P)).then_inc(k.rows2_loaded, 16)
    for l in range(DEPTH):
        act.dma_start(k.rows2[C2["conv"]:C2["conv"] + 32, l, :], i["ml_conv_w_2"][l].rearrange("k (c p) -> (k c) p", p=P)).then_inc(k.rows2_loaded, 16)

    for c in range(KC):
        act.wait_ge(k.turned, c + 1)
        act.activation(k.h[:, c, :], k.ps[:, 4 + c % 4, 0:T1], ACT.Copy).then_inc(k.turned_out, 1)
    act.drain()
    act.activation(k.x_hi[:, :, :], k.h[:, :, :], ACT.Copy).then_inc(k.x_hi_ready, 1)
    act.wait_ge(k.cols2_turned, 1)
    for l in range(DEPTH):
        cp = act.activation(k.col2[:, l, :], k.ps[:, 6, l * N2:(l + 1) * N2], ACT.Copy)
    cp.then_inc(k.cols2_ready, 1)
    split(0, 0, UNIT)
    split(1, 0, UNIT)

    with act.Fori(0, DEPTH) as l:
        q, vec0, act0, gates0 = l * (L_UNITS // SLOTS), l * L_VEC, l * L_ACT, l * L_GATES
        act.wait_ge(k.vec_turned, l + 1)
        for name, src, n in (("ln_g", i["ln_g"][l].rearrange("i (c p) -> (i c) p", p=P), 24),
                             ("ln_b", i["ln_b"][l].rearrange("i (c p) -> (i c) p", p=P), 24),
                             ("gate_b", i["mix_b_gate"][l].rearrange("i (c p) -> (i c) p", p=P), 16),
                             ("conv", i["conv_w"][l].rearrange("i (c p) -> (i c) p", p=P), 12),
                             ("q_g", i["q_norm_g"][l].rearrange("(c p) -> c p", p=P), 2),
                             ("kv_g", i["kv_norm_g"][l].rearrange("(c p) -> c p", p=P), 1)):
            act.dma_start(k.rows[C1[name]:C1[name] + n, :], src).then_inc(k.vec_loaded, 16)
        up(S1["up1"], q, vec0, gates0 + S1["up1"].gates, T1)
        ahead_only(S1["down1"], q)
        act.wait_ge(k.vec_turned, l + 2)
        act.activation(k.col[:, :], k.ps[:, 6, 0:N1], ACT.Copy).then_inc(k.vec_ready, 1)
        act.drain()
        layer_norm(l * 3)

        def take_win(u, g, q):
            unit_used(g, q)
            b = 2 * (u % 2)
            if u < 8:
                act.activation(k.mix1[:, 2 * u:2 * u + 2, :], k.ps[:, b:b + 2, 0:T1], ACT.Copy, scale=UNW).then_inc(k.act_evac, 1)
            else:
                for c in range(2):
                    n = 2 * (u - 8) + c
                    a = act.activation(k.mix1[:, 16 + n, :], k.ps[:, b + c, 0:T1], ACT.Sigmoid, scale=UNW,
                                       bias=k.col[:, C1["gate_b"] + n:C1["gate_b"] + n + 1])
                a.then_inc(k.act_evac, 1)
        win = S1["win"]
        for u in range(win.units):
            late = u + AHEAD - win.units
            split(win.first + u + AHEAD, q, win.size if late < 0 else win.after[late])
            take_win(u, win.first + u, q)
        act.drain()
        act.activation(k.sq[:, 0:3, :], k.mix1[:, 12:15, :], ACT.Square).then_inc(k.lat_squared, 1)
        act.wait_ge(k.lat_mean, l + 1)
        act.activation(k.std[:, 0, :], k.ps[:, 4, 0:T1], ACT.Sqrt, bias=k.eps[:, 1:2], scale=float(D) / 256)
        act.activation(k.std[:, 1, :], k.ps[:, 5, 0:T1], ACT.Sqrt, bias=k.eps[:, 1:2], scale=float(D) / 128).then_inc(k.lat_std, 1)
        act.wait_ge(k.lat_normed, l + 1)
        act.activation(k.y_hi[:, 2, 0:3, :], k.sq[:, 3:6, :], ACT.Copy).then_inc(k.lat_hi, 1)
        outs = 0
        lat0 = l * 7
        later = [S1["uk"].size, S1["uv"].size, S1["branch"].size, S1["branch"].size]
        for u, (name, n_out) in enumerate((("uq", 2), ("uq", 2), ("uk", 4), ("uv", 3))):
            g = S1["uq"].first + u
            split(g + AHEAD, q, later[u])
            for o in range(n_out):
                if o < n_out - 1:
                    act.wait_ge(k.latent_out, lat0 + outs + 1)
                    outs += 1
                else:
                    unit_used(g, q)
                b = 2 * (o % 2)
                if name == "uq":
                    h = 4 * u + 2 * o
                    a = act.activation(k.qf[0:QK, h:h + 2, :], k.ps[0:QK, b:b + 2, 0:T1], ACT.Copy, scale=UNW)
                elif name == "uk":
                    a = act.activation(k.kf[0:NOPE, 2 * o:2 * o + 2, :], k.ps[0:NOPE, b:b + 2, 0:T1], ACT.Copy, scale=UNW)
                else:
                    n = QB1[o][1]
                    a = act.activation(k.vt1[0:n, o, :], k.ps[0:n, b, :], ACT.Copy, scale=UNW)
                a.then_inc(k.act_evac, 1)
        heads(l * 24, l * 8, QB1, HEADS1, softmax_exp, META)
        for c in range(4):
            act.wait_ge(k.heads_summed, l * 8 + 2 * c + 2)
            act.activation(k.y_hi[:, 1, c, :], k.ps[:, c, 0:T1], ACT.Copy).then_inc(k.y_hi_ready, 1)
        ahead_only(S1["branch"], q)
        ahead_only(S1["wo"], q)
        layer_norm(l * 3 + 1)
        up(S1["up2"], q, vec0, gates0 + S1["up2"].gates, T1)
        ahead_only(S1["down2"], q)
        layer_norm(l * 3 + 2)

    for l in range(DEPTH):
        s = S20 if l == 0 else S21
        if l == 0:
            act.wait_ge(k.h_ready, 3 * DEPTH)
        else:
            act.wait_ge(k.vec_evac, V_LAYER1 + 2)
        rms_norm(2 * l)

        def take_values(trip, j, g, q):
            unit_used(g, q)
            b = 2 * (j % 2)
            act.activation(k.vtok[:, :, 256 * j:256 * j + 256], k.ps[:, b:b + 2, 0:256], ACT.Copy, scale=UNW).then_inc(k.act_evac, 1)
        over_units_ahead(act, s["values"], 0, split, take_values)

        def take_small(trip, j, g, q):
            unit_used(g, q)
            act.activation(k.gp[:, :, :], k.ps[:, 0:2, 0:16], ACT.Copy, scale=UNW).then_inc(k.act_evac, 1)
        over_units_ahead(act, s["small"], 0, split, take_small)

        def take_plain(trip, j, g, q):
            c = (trip * SLOTS + j) * 2
            unit_used(g, q)
            b = 2 * (j % 2)
            act.activation(k.mix2[:, bass.ds(c, 2), :], k.ps[:, b:b + 2, 0:T2], ACT.Copy, scale=UNW).then_inc(k.act_evac, 1)
        over_units_ahead(act, s["plain"], 0, split, take_plain)
        act.wait_ge(k.small_ready, l + 1)
        act.activation(k.ge[:, :, :], k.gx[:, :, :], ACT.Abs)
        act.drain()
        act.activation(k.gl[:, :, :], k.ge[:, :, :], ACT.Exp, scale=-1.0)
        act.drain()
        act.activation(k.ge[:, :, :], k.gl[:, :, :], ACT.Ln, bias=1.0).then_inc(k.gate_ln, 1)

        def take_gated(trip, j, g, q):
            c = (trip * SLOTS + j) * 2 + 20
            unit_used(g, q)
            b = 2 * (j % 2)
            act.activation(k.mix2[:, bass.ds(c, 2), :], k.ps[:, b:b + 2, 0:T2], ACT.Sigmoid, scale=UNW).then_inc(k.act_evac, 1)
        over_units_ahead(act, s["gated"], 0, split, take_gated)
        act.wait_ge(k.taps_ready, l + 1)
        act.activation(k.qkc[:, :, :], k.qkc[:, :, :], ACT.Silu).then_inc(k.qk_ready, 1)

        g = s["group"].first
        split(g + AHEAD, 0, s["group"].after[1])
        act.wait_ge(k.unit_done, g + 1 + SLOTS)
        for o in range(2):
            for c in range(2):
                n = 2 * o + c
                a = act.activation(k.pa[:, n, 0:T2], k.ps[:, 2 * o + c, 0:T2], ACT.Copy, scale=k.pscale[:, l, n:n + 1])
            a.then_inc(k.act_evac, 1)

        i0 = (DEPTH + l) * 24
        h0 = DEPTH * 8 + l * 12
        heads(i0, h0, QB2, ML_HEADS, ml_exp, 0)
        act.wait_ge(k.heads_summed, h0 + ML_HEADS)
        act.activation(k.sq[:, 0:4, 0:T2], k.ps[:, 0:4, 0:T2], ACT.Square).then_inc(k.ml_squared, 1)
        act.wait_ge(k.ml_mean, l + 1)
        act.activation(k.sq[:, 4:8, 0:T2], k.ps[:, 4:6, :].rearrange("p b (h t) -> p (b h) t", t=T2), ACT.Sqrt, bias=k.eps[:, 1:2],
                       scale=float(D) / P).then_inc(k.ml_std, 1)
        act.wait_ge(k.ml_ready, l + 1)
        act.activation(k.y_hi[:, 1, :, 0:T2], k.sq[:, 0:4, 0:T2], ACT.Copy).then_inc(k.ml_hi, 1)
        heads(i0 + 8, h0 + ML_HEADS, QB2, FOX_HEADS, softmax_exp, 0)
        for c in range(4):
            act.wait_ge(k.heads_summed, h0 + ML_HEADS + 2 * c + 2)
            act.activation(k.y_hi[:, 2, c, 0:T2], k.ps[:, c, 0:T2], ACT.Copy).then_inc(k.y_hi_ready, 1)
        ahead_only(s["branch"], 0)
        ahead_only(s["wout"], 0)
        act.wait_ge(k.vec_evac, s["wout"].base + 4 + 2)
        rms_norm(2 * l + 1, to_parts=l == 0)
        if l == 0:
            up(s["up"], 0, 0, s["up"].gates, T2)
            ahead_only(s["down"], 0)
    act.dma_start(k.final_g, i["final_norm_g_2"].rearrange("(a n) -> a n", a=1).broadcast_to([P, D])).then_inc(k.final_g_loaded, 16)
    act.wait_ge(k.xt_turned, 1)
    act.activation(k.xt_hi[:, :, :], k.ps[:, 0:4, :].rearrange("p (b c) n -> p b (c n)", b=2), ACT.Copy).then_inc(k.xt_hi_ready, 1)
    act.wait_ge(k.lg_ready, 1)
    act.activation(k.rt[:, :, 1], k.rt[:, :, 0], ACT.Exp).then_inc(k.lg_exped, 1)

    def take_gathered(n):
        act.wait_ge(k.hi_gathered, n + 1)
        act.activation(k.x_hi[:, :, 0:P], k.ps[:, 2:4, :].rearrange("p b (c s) -> p (b c) s", s=P), ACT.Copy).then_inc(k.xe_hi_ready, 1)

    def expert(r, e, sched, last):
        n = e + r * EXPERTS
        q = n * (E_UNITS // SLOTS)
        up(sched["up"], q, n * EC, None, P)
        act.activation(k.gate_now[:, :], k.slot_gate[:, bass.ds(e, 1)], ACT.Copy)
        act.drain()

        def take_block(trip, j, g, q):
            if (trip, j) == HI_TAKEN and not last:
                take_gathered(n + 1)
            if j == DOWN_GROUPS - 1:
                unit_used(g, q)
                act.activation(k.d_hi, k.ps[:, trip % 2, 0:DOWN_COLS], ACT.Copy, scale=k.gate_now[:, 0:1]).then_inc(k.down_hi_ready, 1)
        over_units_ahead(act, sched["down"], q, split, take_block, loop=False)

    def moe_round(r):
        take_gathered(r * EXPERTS)
        act.wait_ge(k.slots_ready, r + 1)
        with act.Fori(0, EXPERTS - 1) as e:
            expert(r, e, SE, last=False)
        expert(r, EXPERTS - 1, SE_LAST, last=True)
    moe_round(0)
    act.wait_ge(k.more_ready, 1)
    more = act.value_load(k.more[0:1, 0:1], min_val=0, max_val=1)
    with act.If(more > 0):
        q1 = EXPERTS * (E_UNITS // SLOTS)
        split(E_FIRST, q1, UNIT)
        split(E_FIRST + 1, q1, UNIT)
        moe_round(1)

    act.wait_ge(k.all_added, 1)
    y = k.ps[:, 4:8, :].rearrange("p (b c) n -> p b (c n)", b=2)
    for b in range(2):
        act.activation(k.squares[:, b, :], y[:, b, :], ACT.Square, accum_out=k.ms[:, b, 0:1])
    act.drain()
    act.activation(k.ms[:, :, 1], k.ms[:, :, 0], ACT.Sqrt, bias=k.eps[:, 1:2], scale=1.0 / D).then_inc(k.final_std, 1)
    for b in range(2):
        act.wait_ge(k.row_ready, b + 1)
        act.dma_start(out[0, b * P:(b + 1) * P, :], k.out_rows[:, b, :]).then_inc(k.stored, 16)
    act.wait_ge(k.stored, 32)


def vec_program(vec, k, i, out):
    def split(g, q, size):
        s = g % SLOTS
        vec.wait_ge(k.hi_ready, q * SLOTS + (g + 1))
        vec.scalar_tensor_tensor(k.w_lo[:, s, 0:size], k.w32[:, s, 0:size], WS, k.w_hi[:, s, 0:size],
                                 ALU.mult, ALU.subtract).then_inc(k.parts_ready, 1)

    def unit_used(g, q):
        vec.wait_ge(k.unit_done, q * SLOTS + (g + 1 + SLOTS))

    def ahead_only(phase, q):
        over_units_ahead(vec, phase, q, split, lambda trip, j, g, q: None)

    def up(phase, q, gates0, t, factor):
        def take(trip, j, g, q):
            o, b = trip * SLOTS + j, j % 2
            vec.wait_ge(k.silu_ready, gates0 + o + (phase.gates + 1))
            vec.wait_ge(k.ff_ready, gates0 + o + (phase.gates + 1))
            vec.scalar_tensor_tensor(k.prod[:, b, 0:t], k.silu[:, b, 0:t], factor * UNW, k.ps[:, 2 * b + 1, 0:t],
                                     ALU.mult, ALU.mult).then_inc(k.vec_evac, 1)
        over_units_ahead(vec, phase, q, split, take)

    def down(phase, q, add):
        def take(trip, j, g, q):
            if (j % 2) == 1:
                unit_used(g, q)
                add(trip * 2 + j // 2, k.ps[:, 2 * (j // 2), :])
        over_units_ahead(vec, phase, q, split, take)

    def add_scaled(m, acc):
        vec.scalar_tensor_tensor(k.h[:, bass.ds(m, 1), :], k.h[:, bass.ds(m, 1), :], WS * ALPHA, acc[:, 0:T1].unsqueeze(1),
                                 ALU.mult, ALU.add).then_inc(k.vec_evac, 1)

    def add_plain(m, acc):
        x = k.h[:, bass.ds(m, 1), META:T1]
        vec.scalar_tensor_tensor(x, acc[:, 0:T2].unsqueeze(1), UNW, x, ALU.mult, ALU.add).then_inc(k.vec_evac, 1)

    def per_chunk(x, t, n):
        return x[:, 0:t].unsqueeze(1).broadcast_to([P, n, t])

    def layer_norm(n, g0, b0):
        vec.wait_ge(k.ln_mean, n + 1)
        vec.tensor_tensor(k.h[:, :, :], k.h[:, :, :], per_chunk(k.ps[:, 4, :], T1, KC), ALU.subtract).then_inc(k.ln_centered, 1)
        vec.wait_ge(k.ln_std, n + 1)
        vec.reciprocal(k.rstd[:, 0, :], k.std[:, 0, :])
        vec.drain()
        vec.tensor_tensor(k.h[:, :, :], k.h[:, :, :], per_chunk(k.rstd[:, 0, :], T1, KC), ALU.mult)
        vec.drain()
        for c in range(KC):
            a = vec.tensor_scalar(k.h[:, c, :], k.h[:, c, :], k.col[:, g0 + c:g0 + c + 1], k.col[:, b0 + c:b0 + c + 1], ALU.mult, ALU.add)
        a.then_inc(k.h_ready, 1)
        vec.wait_ge(k.x_hi_ready, n + 2)
        vec.tensor_tensor(k.x_lo[:, :, :], k.h[:, :, :], k.x_hi[:, :, :], ALU.subtract).then_inc(k.x_ready, 1)

    def rms_norm(n, l, g0, dst, to_parts=True):
        vec.wait_ge(k.rms_std, n + 1)
        vec.reciprocal(k.rstd[:, 0, 0:T2], k.std[:, 0, 0:T2])
        vec.drain()
        for c in range(KC):
            a = vec.scalar_tensor_tensor(dst[:, c, 0:T2], k.h[:, c, META:T1], k.col2[:, l, g0 + c:g0 + c + 1], k.rstd[:, 0, 0:T2],
                                         ALU.mult, ALU.mult)
        a.then_inc(k.h_ready, 1)
        if to_parts:
            vec.wait_ge(k.x_hi_ready, 3 * DEPTH + n + 2)
            vec.tensor_tensor(k.x_lo[:, :, 0:T2], dst[:, :, 0:T2], k.x_hi[:, :, 0:T2], ALU.subtract).then_inc(k.x_ready, 1)

    def heads(items0, blocks, heads, mask, norm):
        nb = len(blocks)
        items = heads * nb
        for n in range(items + 1):
            if n < items:
                vec.wait_ge(k.scored, items0 + n + 1)
                if n >= 2:
                    vec.wait_ge(k.exped, items0 + n - 1)
                mask(n // nb, n % nb, n % 2, *blocks[n % nb])
            if n >= 1:
                m = n - 1
                vec.wait_ge(k.exped, items0 + m + 1)
                norm(m % 2, *blocks[m % nb][1:])

    def softmax_max(b, queries, keys):
        vec.drain()
        vec.tensor_reduce(k.stat[0:queries, b, 0:1], k.sc[0:queries, b, 0:keys], AX.X, ALU.max, negate=True).then_inc(k.masked, 1)

    def softmax_norm(b, queries, keys):
        vec.reciprocal(k.stat[0:queries, b, 2:3], k.stat[0:queries, b, 1:2])
        vec.drain()
        vec.tensor_scalar(k.pr[0:queries, b, 0:keys], k.pr[0:queries, b, 0:keys], k.stat[0:queries, b, 2:3], None, ALU.mult).then_inc(k.probs_ready, 1)

    def mla_mask(h, j, b, first, queries, keys):
        vec.scalar_tensor_tensor(k.sc[0:queries, b, 0:keys], k.ps[0:queries, 4 + b, 0:keys], QK ** -0.5,
                                 k.mask[0:queries, 256 - first:256 - first + keys], ALU.mult, ALU.add)
        softmax_max(b, queries, keys)

    vec.memset(k.mean_w[:, :], 1.0 / D)
    vec.memset(k.ones[:, :], 1.0)
    vec.memset(k.eps[:, 0:1], LN_EPS * WS * WS)
    vec.memset(k.eps[:, 1:2], RMS_EPS).then_inc(k.consts_set, 1)
    vec.sem_inc(k.parts_ready, SLOTS)
    vec.sem_inc(k.unit_done, SLOTS)
    vec.sem_inc(k.vec_evac, 2)
    vec.sem_inc(k.vec_turned, 1)
    vec.sem_inc(k.act_evac, 2)
    vec.sem_inc(k.ff_ready, 2)
    vec.wait_ge(k.const_loaded, 16 * N_CONST)
    vec.wait_ge(k.x_hi_ready, 1)
    vec.tensor_tensor(k.x_lo[:, :, :], k.h[:, :, :], k.x_hi[:, :, :], ALU.subtract).then_inc(k.x_ready, 1)
    vec.wait_ge(k.cols2_ready, 1)
    vec.tensor_scalar(k.pscale[:, :, :], k.col2[:, :, C2["pool_s"]:C2["pool_s"] + 4], UNW, None, ALU.mult).then_inc(k.consts_set, 1)
    split(0, 0, UNIT)
    split(1, 0, UNIT)

    with vec.Fori(0, DEPTH) as l:
        q, gates0 = l * (L_UNITS // SLOTS), l * L_GATES
        up(S1["up1"], q, gates0, T1, 0.5)
        down(S1["down1"], q, add_scaled)
        vec.drain()
        vec.wait_ge(k.vec_ready, l + 1)
        layer_norm(l * 3, C1["ln_g"], C1["ln_b"])
        ahead_only(S1["win"], q)
        vec.wait_ge(k.lat_std, l + 1)
        vec.reciprocal(k.rstd[:, :, :], k.std[:, :, :])
        vec.drain()
        for c in range(3):
            a = vec.scalar_tensor_tensor(k.sq[:, 3 + c, :], k.mix1[:, 12 + c, :], k.col[:, C1["q_g"] + c:C1["q_g"] + c + 1],
                                         k.rstd[:, c // 2, :], ALU.mult, ALU.mult)
        a.then_inc(k.lat_normed, 1)
        vec.wait_ge(k.lat_hi, l + 1)
        vec.tensor_tensor(k.y_lo[:, 2, 0:3, :], k.sq[:, 3:6, :], k.y_hi[:, 2, 0:3, :], ALU.subtract).then_inc(k.lat_ready, 1)
        vec.wait_ge(k.kr_placed, l + 1)
        r = slice(NOPE, QK)
        vec.tensor_tensor(k.tmp[r, 0, :], k.ps[r, 6, 0:T1], k.cos[r, :], ALU.mult)
        vec.tensor_tensor(k.tmp[r, 1, :], k.ps[r, 7, 0:T1], k.sin[r, :], ALU.mult)
        vec.drain()
        vec.tensor_tensor(k.kf[r, :, :], k.tmp[r, 0:1, :].broadcast_to([ROPE, HEADS1, T1]),
                          k.tmp[r, 1:2, :].broadcast_to([ROPE, HEADS1, T1]), ALU.add).then_inc(k.k_full, 1)
        for u, name in enumerate(("uq", "uq", "uk", "uv")):
            g = S1["uq"].first + u
            split(g + AHEAD, q, (S1["uk"].size, S1["uv"].size, S1["branch"].size, S1["branch"].size)[u])
        vec.wait_ge(k.act_evac, l * L_ACT + (S1["uq"].base + 4 + 2))
        vec.tensor_tensor(k.rope_a[r, :, :], k.qf[r, :, :], k.cos[r, :].unsqueeze(1).broadcast_to([ROPE, HEADS1, T1]), ALU.mult)
        for n in range(2):
            vec.drain()
            vec.wait_ge(k.q_turned, l * 2 + n + 1)
            vec.tensor_tensor(k.sq[r, 0:4, :], k.ps[r, 4:8, 0:T1], k.sin[r, :].unsqueeze(1).broadcast_to([ROPE, 4, T1]), ALU.mult).then_inc(k.q_rot_used, 1)
            vec.drain()
            a = vec.tensor_tensor(k.qf[r, 4 * n:4 * n + 4, :], k.rope_a[r, 4 * n:4 * n + 4, :], k.sq[r, 0:4, :], ALU.add)
        a.then_inc(k.q_full, 1)
        heads(l * 24, QB1, HEADS1, mla_mask, softmax_norm)
        for c in range(4):
            vec.wait_ge(k.y_hi_ready, l * 4 + c + 1)
            a = vec.tensor_tensor(k.y_lo[:, 1, c, :], k.ps[:, c, 0:T1], k.y_hi[:, 1, c, :], ALU.subtract)
        a.then_inc(k.y_ready, 1)

        def take_branch(trip, j, g, q):
            m, b = trip * SLOTS + j, 2 * (j % 2)
            unit_used(g, q)
            vec.scalar_tensor_tensor(k.tmp[:, 0:1, :], k.ps[:, b:b + 1, 0:T1], UNW, k.mix1[:, bass.ds(m + 16, 1), :], ALU.mult, ALU.mult)
            vec.scalar_tensor_tensor(k.tmp[:, 1:2, :], k.ps[:, b + 1:b + 2, 0:T1], UNW, k.mix1[:, bass.ds(m + 24, 1), :],
                                     ALU.mult, ALU.mult).then_inc(k.vec_evac, 1)
            vec.drain()
            vec.tensor_tensor(k.tmp[:, 2:3, :], k.tmp[:, 0:1, :], k.tmp[:, 1:2, :], ALU.add)
            vec.drain()
            vec.tensor_copy(k.x_hi[:, bass.ds(m, 1), :], k.tmp[:, 2:3, :])
            vec.drain()
            vec.tensor_tensor(k.x_lo[:, bass.ds(m, 1), :], k.tmp[:, 2:3, :], k.x_hi[:, bass.ds(m, 1), :], ALU.subtract).then_inc(k.merged_ready, 1)
        over_units_ahead(vec, S1["branch"], q, split, take_branch)

        def take_wo(trip, j, g, q):
            c, b = (trip * SLOTS + j) * 2, 2 * (j % 2)
            unit_used(g, q)
            h = k.h[:, bass.ds(c, 2), :]
            vec.scalar_tensor_tensor(h, h, WS * ALPHA, k.ps[:, b:b + 2, 0:T1], ALU.mult, ALU.add).then_inc(k.vec_evac, 1)
        over_units_ahead(vec, S1["wo"], q, split, take_wo)
        vec.drain()
        layer_norm(l * 3 + 1, C1["ln_g"] + KC, C1["ln_b"] + KC)
        up(S1["up2"], q, gates0, T1, 0.5)
        down(S1["down2"], q, add_scaled)
        vec.drain()
        layer_norm(l * 3 + 2, C1["ln_g"] + 2 * KC, C1["ln_b"] + 2 * KC)

    for l in range(DEPTH):
        s = S20 if l == 0 else S21
        vec.drain()
        rms_norm(2 * l, l, C2["mix_g"], k.sq)
        ahead_only(s["values"], 0)
        ahead_only(s["small"], 0)
        vec.wait_ge(k.act_evac, s["small"].base + 1 + 2)
        vec.tensor_tensor(k.gx[:, :, :], k.gp[:, :, :], k.gbias[:, l, :].unsqueeze(1).broadcast_to([P, 2, 16]), ALU.add).then_inc(k.small_ready, 1)
        ahead_only(s["plain"], 0)
        vec.wait_ge(k.gate_ln, l + 1)
        vec.scalar_tensor_tensor(k.lf[:, :, :], k.gx[:, :, 4:16], 0.0, k.ge[:, :, 4:16], ALU.min, ALU.subtract).then_inc(k.lf_ready, 1)
        ahead_only(s["gated"], 0)
        vec.wait_ge(k.cum_summed, l + 1)
        vec.tensor_copy(k.cum[:, :, :], k.ps[:, 4, 0:32].rearrange("p (b n) -> p b n", n=16)[:, :, 0:12]).then_inc(k.cum_ready, 1)
        split(s["group"].first + AHEAD, 0, s["group"].after[1])
        vec.drain()

        def decay(r, dst, j, b, keys):
            vec.scalar_tensor_tensor(dst, k.ps[:, 4 + b, 256:256 + keys], k.cum[:, j, r:r + 1], k.mask[:, 256 - 128 * j:256 - 128 * j + keys],
                                     ALU.add, ALU.add)

        def ml_mask(h, j, b, first, queries, keys):
            decay(h, k.sc[:, b, 0:keys], j, b, keys)
            vec.drain()
            vec.tensor_reduce(k.stat[:, b, 0:1], k.sc[:, b, 0:keys], AX.X, ALU.max)
            vec.drain()
            vec.tensor_scalar(k.stat[:, b, 1:2], k.stat[:, b, 0:1], k.cum[:, j, h:h + 1], -1.0, ALU.max, ALU.mult).then_inc(k.masked, 1)

        def ml_norm(b, queries, keys):
            pr = k.pr[:, b, 0:keys]
            vec.scalar_tensor_tensor(pr, k.ps[:, 4 + b, 0:keys], float(P) ** -0.5, pr, ALU.mult, ALU.mult, accum_out=k.stat[:, b, 3:4])
            vec.drain()
            vec.scalar_tensor_tensor(k.stat[:, b, 7:8], k.stat[:, b, 3:4], -1.0, k.stat[:, b, 3:4], ALU.mult, ALU.max)
            vec.drain()
            vec.tensor_tensor(k.stat[:, b, 5:6], k.stat[:, b, 7:8], k.stat[:, b, 4:5], ALU.max)
            vec.drain()
            vec.reciprocal(k.stat[:, b, 6:7], k.stat[:, b, 5:6])
            vec.drain()
            vec.tensor_scalar(pr, pr, k.stat[:, b, 6:7], None, ALU.mult).then_inc(k.probs_ready, 1)

        def fox_mask(h, j, b, first, queries, keys):
            decay(4 + h, k.gm[:, b, 0:keys], j, b, keys)
            vec.drain()
            vec.scalar_tensor_tensor(k.sc[:, b, 0:keys], k.ps[:, 4 + b, 0:keys], FOX_DH ** -0.5, k.gm[:, b, 0:keys], ALU.mult, ALU.add)
            softmax_max(b, queries, keys)

        i0 = (DEPTH + l) * 24
        heads(i0, QB2, ML_HEADS, ml_mask, ml_norm)
        vec.wait_ge(k.ml_std, l + 1)
        vec.reciprocal(k.sq[:, 4:8, 0:T2], k.sq[:, 4:8, 0:T2])
        vec.drain()
        for h in range(ML_HEADS):
            vec.scalar_tensor_tensor(k.sq[:, h, 0:T2], k.ps[:, h, 0:T2], k.col2[:, l, C2["ml_g"] + h:C2["ml_g"] + h + 1],
                                     k.sq[:, 4 + h, 0:T2], ALU.mult, ALU.mult)
        vec.drain()
        vec.tensor_tensor(k.sq[:, 0:4, 0:T2], k.sq[:, 0:4, 0:T2], k.mix2[:, 20:24, :], ALU.mult).then_inc(k.ml_ready, 1)
        vec.wait_ge(k.ml_hi, l + 1)
        vec.tensor_tensor(k.y_lo[:, 1, :, 0:T2], k.sq[:, 0:4, 0:T2], k.y_hi[:, 1, :, 0:T2], ALU.subtract).then_inc(k.ml_parts, 1)
        heads(i0 + 2 * ML_HEADS, QB2, FOX_HEADS, fox_mask, softmax_norm)
        vec.wait_ge(k.act_evac, s["group"].base + 2 + 2)
        vec.tensor_copy(k.y_hi[:, 0, :, 0:T2], k.pa[:, :, 0:T2])
        vec.drain()
        vec.tensor_tensor(k.y_lo[:, 0, :, 0:T2], k.pa[:, :, 0:T2], k.y_hi[:, 0, :, 0:T2], ALU.subtract)
        for c in range(4):
            vec.wait_ge(k.y_hi_ready, (DEPTH + l) * 4 + c + 1)
            a = vec.tensor_tensor(k.y_lo[:, 2, c, 0:T2], k.ps[:, c, 0:T2], k.y_hi[:, 2, c, 0:T2], ALU.subtract)
        a.then_inc(k.y_ready, 1)

        def take_branch2(trip, j, g, q):
            m, b = trip * SLOTS + j, 2 * (j % 2)
            unit_used(g, q)
            for n in range(3):
                a = vec.scalar_tensor_tensor(k.tmp[:, n:n + 1, 0:T2], k.ps[:, b + n // 2:b + n // 2 + 1, 256 * (n % 2):256 * (n % 2) + 256], UNW,
                                             k.mix2[:, bass.ds(m + (24 + 8 * n), 1), :], ALU.mult, ALU.mult)
            a.then_inc(k.vec_evac, 1)
            vec.drain()
            vec.tensor_tensor(k.prod[:, 0:1, 0:T2], k.tmp[:, 0:1, 0:T2], k.tmp[:, 1:2, 0:T2], ALU.add)
            vec.drain()
            vec.tensor_tensor(k.prod[:, 1:2, 0:T2], k.prod[:, 0:1, 0:T2], k.tmp[:, 2:3, 0:T2], ALU.add)
            vec.drain()
            vec.tensor_copy(k.x_hi[:, bass.ds(m, 1), 0:T2], k.prod[:, 1:2, 0:T2])
            vec.drain()
            vec.tensor_tensor(k.x_lo[:, bass.ds(m, 1), 0:T2], k.prod[:, 1:2, 0:T2], k.x_hi[:, bass.ds(m, 1), 0:T2], ALU.subtract).then_inc(k.merged_ready, 1)
        over_units_ahead(vec, s["branch"], 0, split, take_branch2)

        def take_wout(trip, j, g, q):
            c, b = (trip * SLOTS + j) * 2, 2 * (j % 2)
            unit_used(g, q)
            x = k.h[:, bass.ds(c, 2), META:T1]
            vec.scalar_tensor_tensor(x, k.ps[:, b:b + 2, 0:T2], UNW, x, ALU.mult, ALU.add).then_inc(k.vec_evac, 1)
        over_units_ahead(vec, s["wout"], 0, split, take_wout)
        vec.drain()
        rms_norm(2 * l + 1, l, C2["ffn_g"], k.sq, to_parts=l == 0)
        if l == 0:
            up(s["up"], 0, 0, T2, 1.0)
            down(s["down"], 0, add_plain)

    vec.memset(k.zeros, 0.0).then_inc(k.zeros_set, 1)
    vec.wait_ge(k.routed, 1)
    vec.tensor_tensor(k.lg[:, :, :], k.ps[:, 4, 0:2 * EXPERTS].rearrange("p (b e) -> p b e", e=EXPERTS),
                      k.rb[:, :].unsqueeze(1).broadcast_to([P, 2, EXPERTS]), ALU.add)
    vec.drain()
    for b in range(2):
        vec.max(k.top[:, b, :], k.lg[:, b, :])
    vec.drain()
    for b in range(2):
        vec.max_index(k.topi[:, b, :], k.top[:, b, :], k.lg[:, b, :])
    vec.tensor_tensor(k.rt[:, :, 0], k.top[:, :, 1], k.top[:, :, 0], ALU.subtract).then_inc(k.lg_ready, 1)
    vec.drain()
    vec.tensor_copy(k.topf[:, :, :], k.topi[:, :, :])
    vec.drain()
    for b in range(2):
        for n, dst in enumerate((k.ga, k.gb)):
            vec.tensor_scalar(dst[:, b, :], k.eidx[:, :], k.topf[:, b, n:n + 1], None, ALU.is_equal)
    vec.drain()
    vec.tensor_tensor(k.member[:, :, :], k.ga[:, :, :], k.gb[:, :, :], ALU.add).then_inc(k.member_ready, 1)
    vec.wait_ge(k.lg_exped, 1)
    vec.tensor_scalar(k.rt[:, :, 2], k.rt[:, :, 1], 1.0, None, ALU.add)
    vec.drain()
    vec.reciprocal(k.rt[:, :, 3], k.rt[:, :, 2])
    vec.drain()
    vec.tensor_tensor(k.rt[:, :, 4], k.rt[:, :, 1], k.rt[:, :, 3], ALU.mult)
    vec.drain()
    for b in range(2):
        vec.tensor_scalar(k.ga[:, b, :], k.ga[:, b, :], k.rt[:, b, 3:4], None, ALU.mult)
    vec.drain()
    for b in range(2):
        vec.scalar_tensor_tensor(k.gates[:, b, :], k.gb[:, b, :], k.rt[:, b, 4:5], k.ga[:, b, :], ALU.mult, ALU.add)
    vec.wait_ge(k.rank_summed, 1)
    vec.tensor_tensor(k.sel[:, :, :], k.member[:, :, :], k.ps[:, 5, 0:2 * EXPERTS].rearrange("p (b e) -> p b e", e=EXPERTS), ALU.mult).then_inc(k.sel_ready, 1)
    vec.wait_ge(k.xt_hi_ready, 1)
    vec.tensor_tensor(k.xt_lo[:, :, :], k.ps[:, 0:4, :].rearrange("p (b c) n -> p b (c n)", b=2), k.xt_hi[:, :, :], ALU.subtract).then_inc(k.xt_ready, 1)

    def dispatch(r):
        spread = k.ps[:, 0:4, :].rearrange("p b (e t) -> p (b e) t", t=T2)
        vec.wait_ge(k.sel_spread, r + 1)
        if r == 0:
            vec.tensor_reduce(k.most[:, :], spread, AX.XY, ALU.max)
            vec.drain()
            vec.tensor_scalar(k.more[:, :], k.most[:, :], float(P), None, ALU.is_gt).then_inc(k.more_ready, 1)
        vec.tensor_scalar(k.to_token[:, :, :], spread, -float(P * r), k.slot_col[:, 0:1], ALU.add, ALU.is_equal).then_inc(k.choice_ready, 1)
        for b in range(2):
            for e in range(EXPERTS):
                vec.tensor_scalar(k.to_slot[:, b, e, :], k.slots[:, :], float(P * r), k.sel[:, b, e:e + 1], ALU.add, ALU.is_equal)
        vec.wait_ge(k.gate_spread, r + 1)
        for e in range(EXPERTS):
            a = vec.scalar_tensor_tensor(k.squares[:, 0, e * P:e * P + T2 // 2].bitcast(F16), k.to_token[:, e, :], UNW, spread[:, e, :],
                                         ALU.mult, ALU.mult, accum_out=k.slot_gate[:, e:e + 1])
        a.then_inc(k.slots_ready, 1)

    def take_gathered(n):
        vec.wait_ge(k.lo_gathered, n + 1)
        vec.tensor_copy(k.x_lo[:, :, 0:P], k.ps[:, 2:4, :].rearrange("p b (c s) -> p (b c) s", s=P)).then_inc(k.xe_ready, 1)

    def expert(r, e, sched, last):
        n = e + r * EXPERTS
        q = n * (E_UNITS // SLOTS)
        up(sched["up"], q, n * EC, P, 1.0)

        def take_block(trip, j, g, q):
            if (trip, j) == LO_TAKEN and not last:
                take_gathered(n + 1)
            if j == DOWN_GROUPS - 1:
                vec.wait_ge(k.down_hi_ready, n * DOWN_BLOCKS + trip + 1)
                vec.scalar_tensor_tensor(k.d_lo, k.ps[:, trip % 2, 0:DOWN_COLS], k.slot_gate[:, bass.ds(e, 1)], k.d_hi,
                                         ALU.mult, ALU.subtract).then_inc(k.down_ready, 1)
        over_units_ahead(vec, sched["down"], q, split, take_block, loop=False)

    def moe_round(r):
        dispatch(r)
        take_gathered(r * EXPERTS)
        with vec.Fori(0, EXPERTS - 1) as e:
            expert(r, e, SE, last=False)
        expert(r, EXPERTS - 1, SE_LAST, last=True)
    moe_round(0)
    more = vec.value_load(k.more[0:1, 0:1], min_val=0, max_val=1)
    with vec.If(more > 0):
        q1 = EXPERTS * (E_UNITS // SLOTS)
        split(E_FIRST, q1, UNIT)
        split(E_FIRST + 1, q1, UNIT)
        moe_round(1)

    vec.wait_ge(k.final_g_loaded, 16)
    vec.wait_ge(k.final_std, 1)
    vec.reciprocal(k.ms[:, :, 2], k.ms[:, :, 1])
    vec.drain()
    y = k.ps[:, 4:8, :].rearrange("p (b c) n -> p b (c n)", b=2)
    for b in range(2):
        vec.scalar_tensor_tensor(k.out_rows[:, b, :], y[:, b, :], k.ms[:, b, 2:3], k.final_g, ALU.mult, ALU.mult).then_inc(k.row_ready, 1)


def pool_program(pool, k, i, out):
    def up(phase, vec0, t, a_hi, a_lo):
        def take(trip, j, g, q):
            o, b = trip * SLOTS + j, j % 2
            pool.wait_ge(k.vec_evac, vec0 + o + (phase.base + 2 + 1))
            pool.sem_inc(k.pool_steps, 1)
            pool.tensor_copy(a_hi[:, bass.ds(o, 1), :], k.prod[:, b:b + 1, 0:t])
            pool.drain()
            pool.tensor_tensor(a_lo[:, bass.ds(o, 1), :], k.prod[:, b:b + 1, 0:t], a_hi[:, bass.ds(o, 1), :], ALU.subtract).then_inc(k.ff_ready, 1)
        over_units(pool, phase, 0, take)

    pool.memset(k.pa[:, :, :], 0.0)
    pool.memset(k.pb[:, :, :], 0.0)
    pool.drain()
    with pool.Fori(0, DEPTH) as l:
        up(S1["up1"], l * L_VEC, T1, k.a_hi1, k.a_lo1)
        pool.wait_ge(k.act_evac, l * L_ACT + (S1["win"].base + 6 + 2))
        pool.tensor_tensor(k.pa[:, :, 2:2 + T1], k.mix1[:, 4:8, :], k.mix1[:, 8:12, :], ALU.mult)
        pool.drain()
        c_acc, c_tap = k.mix1[:, 4:8, :], k.mix1[:, 8:12, :]
        for n in range(3):
            for c in range(4):
                w = k.col[:, C1["conv"] + 4 * n + c:C1["conv"] + 4 * n + c + 1]
                pool.tensor_scalar((c_tap if n else c_acc)[:, c, :], k.pa[:, c, n:n + T1], w, None, ALU.mult)
            pool.drain()
            if n:
                pool.tensor_tensor(c_acc, c_acc, c_tap, ALU.add)
                pool.drain()
        pool.tensor_tensor(c_acc, c_acc, k.mix1[:, 0:4, :], ALU.mult)
        pool.drain()
        pool.tensor_copy(k.y_hi[:, 0, :, :], c_acc)
        pool.drain()
        pool.tensor_tensor(k.y_lo[:, 0, :, :], c_acc, k.y_hi[:, 0, :, :], ALU.subtract).then_inc(k.conv_ready, 1)
        up(S1["up2"], l * L_VEC, T1, k.a_hi1, k.a_lo1)
    for l in range(DEPTH):
        s = S20 if l == 0 else S21
        pool.wait_ge(k.act_evac, s["plain"].base + 10 + 2)
        u = k.mix2[:, 4:12, :]
        for n in (3, 2, 1, 0):
            lag = 3 - n
            for c in range(8):
                w = k.col2[:, l, C2["conv"] + 8 * n + c:C2["conv"] + 8 * n + c + 1]
                pool.tensor_scalar((k.tap if lag else k.qkc)[:, c, :], u[:, c, :], w, None, ALU.mult)
            pool.drain()
            if lag:
                a = pool.tensor_tensor(k.qkc[:, :, lag:T2], k.qkc[:, :, lag:T2], k.tap[:, :, 0:T2 - lag], ALU.add)
                if n:
                    pool.drain()
        a.then_inc(k.taps_ready, 1)
        z = 16
        pool.memset(k.pa[:, :, 0:z], 0.0)
        pool.memset(k.pb[:, :, 0:z], 0.0)
        pool.tensor_copy(k.pa[:, :, z:z + T2], k.mix2[:, 0:4, :])
        a, b = k.pa, k.pb
        for n in range(4):
            pool.drain()
            w = 1 << n
            pool.tensor_tensor(b[:, n:4, z:z + T2], a[:, n:4, z:z + T2], a[:, n:4, z - w:z - w + T2], ALU.add)
            a, b = b, a
        pool.drain()
        for n in range(4):
            src = (k.pb, k.pa)[n % 2]
            pool.tensor_tensor(src[:, n, z:2 * z], src[:, n, z:2 * z], k.icnt[:, n, :], ALU.mult)
            pool.tensor_scalar(src[:, n, 2 * z:z + T2], src[:, n, 2 * z:z + T2], 1.0 / (2 << n), None, ALU.mult)
        pool.drain()
        for n in range(4):
            src = (k.pb, k.pa)[n % 2]
            pool.tensor_tensor(src[:, n, z:z + T2], src[:, n, z:z + T2], k.mix2[:, n, :], ALU.subtract)
        pool.drain()
        for n in range(4):
            src = (k.pb, k.pa)[n % 2]
            pool.tensor_copy(k.y_hi[:, 2, n, 0:T2], src[:, n, z:z + T2])
        pool.drain()
        for n in range(4):
            src = (k.pb, k.pa)[n % 2]
            a = pool.tensor_tensor(k.y_lo[:, 2, n, 0:T2], src[:, n, z:z + T2], k.y_hi[:, 2, n, 0:T2], ALU.subtract)
        a.then_inc(k.pool_ready, 1)
        if l == 0:
            up(s["up"], 0, T2, k.a_hi2, k.a_lo2)

    def moe_round(r):
        with pool.Fori(0, EXPERTS) as e:
            up(SE["up"], (e + r * EXPERTS) * EC, P, k.a_hi3, k.a_lo3)
    moe_round(0)
    pool.wait_ge(k.more_ready, 1)
    more = pool.value_load(k.more[0:1, 0:1], min_val=0, max_val=1)
    with pool.If(more > 0):
        moe_round(1)


def pe_program(pe, k, i, out):
    def parts(acc, w_hi, w_lo, x_hi, x_lo, first, last):
        pe.matmul(acc, w_hi, x_hi, start=first, stop=False)
        pe.matmul(acc, w_hi, x_lo, start=False, stop=False)
        return pe.matmul(acc, w_lo, x_hi, start=False, stop=last)

    def chain(acc, s, tiles, x_hi, x_lo, first=True, last=True):
        for n, (c, m, kc) in enumerate(tiles):
            a = parts(acc, k.w_hi[:, s, c:c + m], k.w_lo[:, s, c:c + m], x_hi[:, kc, :], x_lo[:, kc, :],
                      first and n == 0, last and n == len(tiles) - 1)
        return a

    def stand_alone():
        pe.sem_inc(k.pe_steps, 1)

    def weights(g, q):
        pe.wait_ge(k.parts_ready, q * SLOTS + (g + 1 + SLOTS))

    def all_out(vec, act):
        pe.wait_ge(k.vec_evac, vec)
        pe.wait_ge(k.act_evac, act)

    def up(phase, q, vec0, x_hi, x_lo, t):
        def unit(trip, j, g, q):
            s, b = g % SLOTS, 2 * (j % 2)
            weights(g, q)
            pe.wait_ge(k.vec_evac, vec0 + (trip * SLOTS + j) + (phase.base + 1))
            for n in range(2):
                a = chain(k.ps[:, b + n, 0:t], s, [(n * D + kc * P, P, kc) for kc in range(KC)], x_hi, x_lo)
            a.then_inc(k.unit_done, 1)
        over_units(pe, phase, q, unit)

    def down(phase, q, vec0, gates, a_hi, a_lo, t, fc):
        half = fc // 2

        def unit(trip, j, g, q):
            second = j % 2
            weights(g, q)
            pe.wait_ge(k.ff_ready, gates + (2 + (1 + second) * half))
            if not second:
                pe.wait_ge(k.vec_evac, vec0 + (trip * 2 + j // 2) + (phase.base + 1))
            chain(k.ps[:, 2 * (j // 2), 0:t], g % SLOTS, [(c * P, P, second * half + c) for c in range(half)], a_hi, a_lo,
                  first=not second, last=bool(second)).then_inc(k.unit_done, 1)
        over_units(pe, phase, q, unit)

    def wide(phase, q, evac, evac0, x_hi, x_lo, t):
        def unit(trip, j, g, q):
            s, b = g % SLOTS, 2 * (j % 2)
            weights(g, q)
            pe.wait_ge(evac, evac0 + (trip * SLOTS + j) + (phase.base + 1))
            for n in range(2):
                a = chain(k.ps[:, b + n, 0:t], s, [(kc * 256 + n * P, P, kc) for kc in range(KC)], x_hi, x_lo)
            a.then_inc(k.unit_done, 1)
        over_units(pe, phase, q, unit)

    def layer_norm(n, vec):
        pe.wait_ge(k.vec_evac, vec)
        for c in range(KC):
            a = pe.matmul(k.ps[:, 4, 0:T1], k.mean_w[:, :], k.h[:, c, :], start=c == 0, stop=c == KC - 1)
        a.then_inc(k.ln_mean, 1)
        pe.wait_ge(k.ln_squared, n + 1)
        for c in range(KC):
            a = pe.matmul(k.ps[:, 5, 0:T1], k.mean_w[:, :], k.sq[:, c, :], start=c == 0, stop=c == KC - 1)
        a.then_inc(k.ln_var, 1)

    def rms_norm(n):
        pe.wait_ge(k.rms_squared, n + 1)
        for c in range(KC):
            a = pe.matmul(k.ps[:, 4, 0:T2], k.mean_w[:, :], k.sq[:, c, 0:T2], start=c == 0, stop=c == KC - 1)
        a.then_inc(k.rms_mean, 1)

    def heads(items0, heads0, qb, kb, heads, score, value, acc, free):
        nb = len(qb)
        items = heads * nb

        def turn(n):
            h, j = n // nb, n % nb
            first, queries, keys = qb[j]
            pe.wait_ge(k.probs_ready, items0 + n + 1)
            if j == 0 and h >= 2:
                pe.wait_ge(k.pt_ready, heads0 + h - 1)
            if queries < P:
                stand_alone()
            for k0, col, width, q0 in kb[:j + 1]:
                c = col + first - q0
                a = pe.transpose(k.ps[0:width, 6 + h % 2, c:c + queries], k.pr[0:queries, n % 2, k0:k0 + width], k.ident[0:queries, 0:queries])
            a.then_inc(k.pt_written, 1)

        def sum_values(h):
            pe.wait_ge(k.pt_ready, heads0 + h + 1)
            total = qb[-1][0] + qb[-1][1]
            for n, (k0, col, width, q0) in enumerate(kb):
                a = pe.matmul(acc(h, q0, total), value(h, n, width), k.pt[0:width, h % 2, col:col + total - q0],
                              start=n == 0, stop=n == len(kb) - 1)
            a.then_inc(k.heads_summed, 1)

        def score_next(n):
            if n >= 2:
                pe.wait_ge(free, items0 + n - 1)
            score(n // nb, n % nb, n % 2, *qb[n % nb]).then_inc(k.scored, 1)

        score_next(0)
        score_next(1)
        for n in range(items):
            if n + 2 < items:
                score_next(n + 2)
            turn(n)
            if n >= nb + 1 and (n - nb - 1) % nb == 0:
                sum_values((n - nb - 1) // nb)
        sum_values(heads - 1)

    pe.wait_ge(k.const_loaded, 16 * N_CONST)
    pe.wait_ge(k.consts_set, 1)
    pe.wait_ge(k.tokens_loaded, 32)
    for c in range(KC):
        if c >= 4:
            pe.wait_ge(k.turned_out, c - 3)
        for b, (at, n) in enumerate(((0, META), (META, P), (META + P, P))):
            a = pe.transpose(k.ps[:, 4 + c % 4, at:at + n], k.tokens[0:n, b, c * P:(c + 1) * P], k.ident[0:n, 0:n])
        a.then_inc(k.turned, 1)
    pe.wait_ge(k.rows2_loaded, 16 * 6)
    pe.wait_ge(k.turned_out, KC)
    for l in range(DEPTH):
        a = pe.transpose(k.ps[:, 6, l * N2:(l + 1) * N2], k.rows2[:, l, :], k.ident[0:N2, 0:N2])
    a.then_inc(k.cols2_turned, 1)
    pe.wait_ge(k.cols2_ready, 1)

    with pe.Fori(0, DEPTH) as l:
        q, vec0, act0, gates0 = l * (L_UNITS // SLOTS), l * L_VEC, l * L_ACT, l * L_GATES
        pe.wait_ge(k.x_ready, l * 3 + 1)
        stand_alone()
        up(S1["up1"], q, vec0, k.x_hi, k.x_lo, T1)
        down(S1["down1"], q, vec0, gates0, k.a_hi1, k.a_lo1, T1, FC)
        pe.wait_ge(k.vec_loaded, l * 96 + 96)
        pe.transpose(k.ps[:, 6, 0:N1], k.rows[:, :], k.ident[0:N1, 0:N1]).then_inc(k.vec_turned, 1)
        layer_norm(l * 3, vec0 + (S1["down1"].base + KC + 2))

        pe.wait_ge(k.x_ready, l * 3 + 2)
        stand_alone()
        wide(S1["win"], q, k.act_evac, act0, k.x_hi, k.x_lo, T1)
        pe.wait_ge(k.lat_squared, l + 1)
        pe.matmul(k.ps[:, 4, 0:T1], k.mean_w[:, :], k.sq[:, 0, :], start=True, stop=False)
        pe.matmul(k.ps[:, 4, 0:T1], k.mean_w[:, :], k.sq[:, 1, :], start=False, stop=True)
        pe.matmul(k.ps[:, 5, 0:T1], k.mean_w[:, :], k.sq[:, 2, :], start=True, stop=True).then_inc(k.lat_mean, 1)
        for n in range(2):
            a = pe.matmul(k.ps[0:QK, 6 + n, 0:T1], k.place[:, n, :], k.mix1[0:ROPE, 15, :], start=True, stop=True)
        a.then_inc(k.kr_placed, 1)
        pe.wait_ge(k.lat_ready, l + 1)
        x_hi, x_lo = k.y_hi[:, 2], k.y_lo[:, 2]
        o = 0

        def acc_free(o):
            pe.wait_ge(k.act_evac, act0 + (S1["uq"].base + o + 1))
        for u in range(2):
            g = S1["uq"].first + u
            weights(g, q)
            for pair in range(2):
                acc_free(o)
                for n in range(2):
                    c = (2 * pair + n) * QK
                    a = chain(k.ps[0:QK, 2 * (o % 2) + n, 0:T1], g % SLOTS, [(kc * 4 * QK + c, QK, kc) for kc in range(2)], x_hi, x_lo)
                a.then_inc(k.unit_done if pair == 1 else k.latent_out, 1)
                o += 1
        g = S1["uk"].first
        weights(g, q)
        for pair in range(4):
            acc_free(o)
            for n in range(2):
                a = chain(k.ps[0:NOPE, 2 * (o % 2) + n, 0:T1], g % SLOTS, [((2 * pair + n) * NOPE, NOPE, 2)], x_hi, x_lo)
            a.then_inc(k.unit_done if pair == 3 else k.latent_out, 1)
            o += 1
        g = S1["uv"].first
        s = g % SLOTS
        weights(g, q)
        for b, (first, n, _) in enumerate(QB1):
            acc_free(o)
            acc, t = k.ps[0:n, 2 * (o % 2), :], slice(first, first + n)
            pe.matmul(acc, x_hi[:, 2, t], k.w_hi[:, s, 0:512], start=True, stop=False)
            pe.matmul(acc, x_lo[:, 2, t], k.w_hi[:, s, 0:512], start=False, stop=False)
            a = pe.matmul(acc, x_hi[:, 2, t], k.w_lo[:, s, 0:512], start=False, stop=True)
            a.then_inc(k.unit_done if b == 2 else k.latent_out, 1)
            o += 1
        pe.wait_ge(k.act_evac, act0 + (S1["uq"].base + 4 + 2))
        pe.wait_ge(k.k_full, l + 1)
        r = slice(NOPE, QK)
        for n in range(2):
            if n:
                pe.wait_ge(k.q_rot_used, l * 2 + 1)
            stand_alone()
            for h in range(4):
                a = pe.matmul(k.ps[r, 4 + h, 0:T1], k.rot[r, :], k.qf[r, 4 * n + h, :], start=True, stop=True)
            a.then_inc(k.q_turned, 1)
        pe.wait_ge(k.q_full, l + 1)
        all_out(vec0 + (S1["branch"].base + 2), act0 + (S1["uv"].base + 3 + 2))

        def mla_score(h, j, b, first, queries, keys):
            return pe.matmul(k.ps[0:queries, 4 + b, 0:keys], k.qf[0:QK, h, first:first + queries], k.kf[0:QK, h, 0:keys], start=True, stop=True)
        heads(l * 24, l * 8, QB1, KB1, HEADS1, mla_score,
              lambda h, n, width: k.vt1[0:width, n, h * VH:(h + 1) * VH],
              lambda h, q0, total: k.ps[VH * (h % 2):VH * (h % 2) + VH, h // 2, q0:total], k.masked)
        pe.wait_ge(k.y_ready, l + 1)
        pe.wait_ge(k.conv_ready, l + 1)
        stand_alone()

        def branch(trip, j, g, q):
            s, b = g % SLOTS, 2 * (j % 2)
            weights(g, q)
            pe.wait_ge(k.vec_evac, vec0 + (trip * SLOTS + j) + (S1["branch"].base + 1))
            for n in range(2):
                a = chain(k.ps[:, b + n, 0:T1], s, [(n * 512 + c * P, P, c) for c in range(4)], k.y_hi[:, n], k.y_lo[:, n])
            a.then_inc(k.unit_done, 1)
        over_units(pe, S1["branch"], q, branch)
        pe.wait_ge(k.merged_ready, l * KC + KC)
        stand_alone()
        wide(S1["wo"], q, k.vec_evac, vec0, k.x_hi, k.x_lo, T1)
        layer_norm(l * 3 + 1, vec0 + (S1["wo"].base + 4 + 2))

        pe.wait_ge(k.x_ready, l * 3 + 3)
        stand_alone()
        up(S1["up2"], q, vec0, k.x_hi, k.x_lo, T1)
        down(S1["down2"], q, vec0, gates0 + FC, k.a_hi1, k.a_lo1, T1, FC)
        layer_norm(l * 3 + 2, vec0 + (S1["down2"].base + KC + 2))

    x_hi, x_lo = k.x_hi[:, :, 0:T2], k.x_lo[:, :, 0:T2]
    for l in range(DEPTH):
        s = S20 if l == 0 else S21
        rms_norm(2 * l)
        pe.wait_ge(k.x_ready, 3 * DEPTH + 2 * l + 2)
        all_out((DEPTH * L_VEC if l == 0 else V_LAYER1) + 2, s["values"].base + 2)

        def values(trip, j, g, q):
            st, b = g % SLOTS, 2 * (j % 2)
            weights(g, q)
            pe.wait_ge(k.act_evac, s["values"].base + j + 1)
            for t in range(2):
                for kc in range(KC):
                    a = parts_turned(k.ps[:, b + t, 0:256], st, kc * 256, 256, kc, t, kc == 0, kc == KC - 1)
            a.then_inc(k.unit_done, 1)

        def parts_turned(acc, st, c, n, kc, t, first, last):
            tok = slice(t * P, (t + 1) * P)
            pe.matmul(acc, k.x_hi[:, kc, tok], k.w_hi[:, st, c:c + n], start=first, stop=False)
            pe.matmul(acc, k.x_lo[:, kc, tok], k.w_hi[:, st, c:c + n], start=False, stop=False)
            return pe.matmul(acc, k.x_hi[:, kc, tok], k.w_lo[:, st, c:c + n], start=False, stop=last)
        over_units(pe, s["values"], 0, values)
        g = s["small"].first
        weights(g, 0)
        pe.wait_ge(k.act_evac, s["small"].base + 2)
        for t in range(2):
            for half in range(2):
                for kc in range(KC):
                    a = parts_turned(k.ps[:, t, 8 * half:8 * half + 8], g % SLOTS, half * KC * 8 + kc * 8, 8, kc, t, kc == 0, kc == KC - 1)
        a.then_inc(k.unit_done, 1)
        pe.wait_ge(k.act_evac, s["plain"].base + 2)
        wide(s["plain"], 0, k.act_evac, 0, x_hi, x_lo, T2)
        pe.wait_ge(k.lf_ready, l + 1)
        pe.matmul(k.ps[:, 4, 0:12], k.tri[:, :], k.lf[:, 0, :], start=True, stop=True)
        pe.matmul(k.ps[:, 4, 16:28], k.ones[:, :], k.lf[:, 0, :], start=True, stop=False)
        pe.matmul(k.ps[:, 4, 16:28], k.tri[:, :], k.lf[:, 1, :], start=False, stop=True).then_inc(k.cum_summed, 1)
        wide(s["gated"], 0, k.act_evac, 0, x_hi, x_lo, T2)
        g = s["group"].first
        weights(g, 0)
        pe.wait_ge(k.pool_ready, l + 1)
        all_out(s["branch"].base + 2, s["group"].base + 2)
        for n in range(4):
            a = chain(k.ps[:, n, 0:T2], g % SLOTS, [(n * P, P, n)], k.y_hi[:, 2, :, 0:T2], k.y_lo[:, 2, :, 0:T2])
        a.then_inc(k.unit_done, 1)
        pe.wait_ge(k.qk_ready, l + 1)
        pe.wait_ge(k.cum_ready, l + 1)
        all_out(s["branch"].base + 2, s["group"].base + 2 + 2)

        def spread(r, b, keys, log_i):
            for c in range(keys // P):
                col = lambda x, n: x[:, c, n:n + 1].broadcast_to([P, P])
                a = pe.matmul(k.ps[:, 4 + b, 256 + c * P:256 + keys], col(k.lf, r), k.ntri[:, 0:keys - c * P], start=c == 0,
                              stop=not log_i and c == keys // P - 1)
            if log_i:
                for c in range(keys // P):
                    col = lambda x, n: x[:, c, n:n + 1].broadcast_to([P, P])
                    a = pe.matmul(k.ps[:, 4 + b, 256 + c * P:256 + (c + 1) * P], col(k.gx, r), k.ident[:, :], start=False,
                                  stop=c == keys // P - 1)

        def ml_score(h, j, b, first, queries, keys):
            spread(h, b, keys, True)
            return pe.matmul(k.ps[:, 4 + b, 0:keys], k.qkc[:, h, first:first + P], k.qkc[:, 4 + h, 0:keys], start=True, stop=True)

        def fox_score(h, j, b, first, queries, keys):
            spread(4 + h, b, keys, False)
            p = slice(FOX_DH * (h % 2), FOX_DH * (h % 2) + FOX_DH)
            return pe.matmul(k.ps[:, 4 + b, 0:keys], k.mix2[p, 12 + h // 2, first:first + P], k.mix2[p, 16 + h // 2, 0:keys], start=True, stop=True)

        i0, h0 = (DEPTH + l) * 24, DEPTH * 8 + l * 12
        heads(i0, h0, QB2, KB2, ML_HEADS, ml_score, lambda h, n, width: k.vtok[:, n, h * P:(h + 1) * P],
              lambda h, q0, total: k.ps[:, h, q0:total], k.probs_ready)
        pe.wait_ge(k.ml_squared, l + 1)
        for h in range(ML_HEADS):
            a = pe.matmul(k.ps[:, 4 + h // 2, (h % 2) * T2:(h % 2) * T2 + T2], k.mean_w[:, :], k.sq[:, h, 0:T2], start=True, stop=True)
        a.then_inc(k.ml_mean, 1)
        pe.wait_ge(k.ml_ready, l + 1)
        heads(i0 + 2 * ML_HEADS, h0 + ML_HEADS, QB2, KB2, FOX_HEADS, fox_score,
              lambda h, n, width: k.vtok[:, n, 512 + h * FOX_DH:512 + (h + 1) * FOX_DH],
              lambda h, q0, total: k.ps[FOX_DH * (h % 2):FOX_DH * (h % 2) + FOX_DH, h // 2, q0:total], k.masked)
        pe.wait_ge(k.y_ready, DEPTH + l + 1)
        pe.wait_ge(k.ml_parts, l + 1)

        def branch2(trip, j, g, q):
            st, b = g % SLOTS, 2 * (j % 2)
            weights(g, q)
            pe.wait_ge(k.vec_evac, (trip * SLOTS + j) + (s["branch"].base + 1))
            for n in range(3):
                a = chain(k.ps[:, b + n // 2, 256 * (n % 2):256 * (n % 2) + 256], st, [(n * 512 + c * P, P, c) for c in range(4)],
                          k.y_hi[:, n, :, 0:T2], k.y_lo[:, n, :, 0:T2])
            a.then_inc(k.unit_done, 1)
        over_units(pe, s["branch"], 0, branch2)
        pe.wait_ge(k.merged_ready, (DEPTH + l) * KC + KC)
        wide(s["wout"], 0, k.vec_evac, 0, x_hi, x_lo, T2)
        rms_norm(2 * l + 1)
        if l == 0:
            pe.wait_ge(k.x_ready, 3 * DEPTH + 2 * l + 3)
            up(s["up"], 0, 0, x_hi, x_lo, T2)
            down(s["down"], 0, 0, s["up"].gates, k.a_hi2, k.a_lo2, T2, FC)

    pe.wait_ge(k.h_ready, 3 * DEPTH + 2 * DEPTH)
    for t in range(2):
        for c in range(KC):
            a = pe.matmul(k.ps[:, 4, t * EXPERTS:(t + 1) * EXPERTS], k.sq[:, c, t * P:(t + 1) * P], k.wr[:, c, :], start=c == 0, stop=c == KC - 1)
    a.then_inc(k.routed, 1)
    for t in range(2):
        for c in range(KC):
            a = pe.transpose(k.ps[:, 2 * t + c // 4, (c % 4) * P:(c % 4 + 1) * P], k.sq[:, c, t * P:(t + 1) * P], k.ident[:, :])
    a.then_inc(k.xt_turned, 1)
    pe.wait_ge(k.member_ready, 1)
    pe.matmul(k.ps[:, 5, 0:EXPERTS], k.tri[:, :], k.member[:, 0, :], start=True, stop=True)
    pe.matmul(k.ps[:, 5, EXPERTS:2 * EXPERTS], k.ones[:, :], k.member[:, 0, :], start=True, stop=False)
    pe.matmul(k.ps[:, 5, EXPERTS:2 * EXPERTS], k.tri[:, :], k.member[:, 1, :], start=False, stop=True).then_inc(k.rank_summed, 1)
    pe.wait_ge(k.sel_ready, 1)
    pe.wait_ge(k.zeros_set, 1)
    for b in range(4):
        pe.matmul(k.ps[:, 4 + b, :], k.zeros[:, 0:P], k.zeros, start=True, stop=False)
    for t in range(2):
        for c in range(KC):
            pe.matmul(k.ps[:, 4 + 2 * t + c // 4, (c % 4) * P:(c % 4 + 1) * P], k.h[:, c, META + t * P:META + (t + 1) * P], k.ident[:, :],
                      start=False, stop=False)
    pe.wait_ge(k.xt_ready, 1)

    def spread_columns(x):
        for e in range(EXPERTS):
            for t in range(2):
                a = pe.matmul(k.ps[:, e // 2, (e % 2) * T2 + t * P:(e % 2) * T2 + (t + 1) * P],
                              x[:, t, e:e + 1].broadcast_to([P, P]), k.ident[:, :], start=True, stop=True)
        return a

    y = k.ps[:, 4:8, :].rearrange("p b n -> p (b n)")

    def gather(x, e):
        for c in range(KC):
            for t in range(2):
                a = pe.matmul(k.ps[:, 2 + c // 4, (c % 4) * P:(c % 4 + 1) * P], x[:, t, c * P:(c + 1) * P],
                              k.to_slot[:, t, bass.ds(e, 1), :], start=t == 0, stop=t == 1)
        return a

    def expert(r, e, sched, last):
        n = e + r * EXPERTS
        q = n * (E_UNITS // SLOTS)
        pe.wait_ge(k.xe_ready, n + 1)
        stand_alone()
        up(sched["up"], q, n * EC, k.x_hi[:, :, 0:P], k.x_lo[:, :, 0:P], P)
        chunks = EC // DOWN_GROUPS

        def unit(trip, j, g, q):
            s = g % SLOTS
            weights(g, q)
            if trip == 0:
                pe.wait_ge(k.ff_ready, n * EC + (sched["up"].gates + 2 + (j + 1) * chunks))
            if trip < 2 and j == 0:
                pe.wait_ge(k.vec_evac, n * EC + (sched["down"].base + 1))
            acc = k.ps[:, trip % 2, 0:DOWN_COLS]
            for c in range(chunks):
                ff, w = j * chunks + c, slice(c * DOWN_COLS, (c + 1) * DOWN_COLS)
                pe.matmul(acc, k.a_hi3[:, ff, :], k.w_hi[:, s, w], start=ff == 0, stop=False)
                pe.matmul(acc, k.a_lo3[:, ff, :], k.w_hi[:, s, w], start=False, stop=False)
                a = pe.matmul(acc, k.a_hi3[:, ff, :], k.w_lo[:, s, w], start=False, stop=ff == EC - 1)
            a.then_inc(k.unit_done, 1)
            if trip and j == 0:
                add_block(trip - 1)
            if (trip, j) == HI_GATHERED and not last:
                gather(k.xt_hi, e + 1).then_inc(k.hi_gathered, 1)
            if (trip, j) == LO_GATHERED and not last:
                pe.wait_ge(k.xe_hi_ready, n + 2)
                stand_alone()
                gather(k.xt_lo, e + 1).then_inc(k.lo_gathered, 1)

        def add_block(block):
            pe.wait_ge(k.down_ready, n * DOWN_BLOCKS + block + 1)
            for t in range(2):
                for x in (k.d_hi, k.d_lo):
                    pe.matmul(y[:, block * DOWN_COLS + t * D:(block + 1) * DOWN_COLS + t * D],
                              k.to_token[:, bass.ds(e, 1), t * P:(t + 1) * P].rearrange("p a t -> p (a t)"), x, start=False, stop=False)
        over_units(pe, sched["down"], q, unit, loop=False)
        add_block(DOWN_BLOCKS - 1)

    def moe_round(r):
        spread_columns(k.sel).then_inc(k.sel_spread, 1)
        pe.wait_ge(k.choice_ready, r + 1)
        spread_columns(k.gates).then_inc(k.gate_spread, 1)
        pe.wait_ge(k.slots_ready, r + 1)
        gather(k.xt_hi, 0).then_inc(k.hi_gathered, 1)
        pe.wait_ge(k.xe_hi_ready, r * EXPERTS + 1)
        gather(k.xt_lo, 0).then_inc(k.lo_gathered, 1)
        with pe.Fori(0, EXPERTS - 1) as e:
            expert(r, e, SE, last=False)
        expert(r, EXPERTS - 1, SE_LAST, last=True)
    moe_round(0)
    pe.wait_ge(k.more_ready, 1)
    more = pe.value_load(k.more[0:1, 0:1], min_val=0, max_val=1)
    with pe.If(more > 0):
        moe_round(1)
    for b in range(4):
        a = pe.matmul(k.ps[:, 4 + b, :], k.zeros[:, 0:P], k.zeros, start=False, stop=True)
    a.then_inc(k.all_added, 1)


def build(nc, i, out):
    with ExitStack() as ctx:
        k = allocate(nc, ctx)
        block = ctx.enter_context(nc.Block())

        @block.sync
        def _(sp):
            sp_program(sp, k, i, out)

        @block.scalar
        def _(act):
            act_program(act, k, i, out)

        @block.vector
        def _(vec):
            vec_program(vec, k, i, out)

        @block.gpsimd
        def _(pool):
            pool_program(pool, k, i, out)

        @block.tensor
        def _(pe):
            pe_program(pe, k, i, out)


def constants():
    t = np.arange(T1, dtype=np.float32)
    freq = (np.float32(1.0) / (np.float32(10000.0) ** (np.arange(0, ROPE, 2, dtype=np.float32) / np.float32(ROPE)))).astype(np.float32)
    ang = (freq[:, None] * t[None, :]).astype(np.float32)
    half = ROPE // 2
    rot = np.zeros((P, ROPE), np.float32)
    place = np.zeros((ROPE, 2, QK), np.float32)
    for m in range(half):
        rot[NOPE + m + half, m], rot[NOPE + m, m + half] = -1.0, 1.0
        place[m + half, 1, NOPE + m], place[m, 1, NOPE + m + half] = -1.0, 1.0
    for m in range(ROPE):
        place[m, 0, NOPE + m] = 1.0
    row = np.arange(P)
    tri = (row[:, None] <= row[None, :]).astype(np.float32)
    mask = np.zeros((P, 3 * P), np.float32)
    mask[:, 2 * P:] = np.where(row[None, :] <= row[:, None], 0.0, NEG)
    pos = np.arange(16)
    icnt = np.stack([1.0 / np.minimum(pos + 1, w) for w in (2, 4, 8, 16)]).astype(np.float32)
    return {
        "c_ident": np.eye(P, dtype=np.float32), "c_tri": tri,
        "c_ntri": np.concatenate([-tri, -np.ones((P, P), np.float32)], 1), "c_mask": mask, "c_rot": rot,
        "c_cos": np.tile(np.cos(ang), (2, 1)), "c_sin": np.tile(np.sin(ang), (2, 1)), "c_place": place, "c_icnt": icnt,
        "c_eidx": np.arange(EXPERTS, dtype=np.float32)[None, :],
        "c_slots": np.arange(1, P + 1, dtype=np.float32)[None, :],
    }


def kernel(**inputs):
    import concourse.bacc as bacc
    from concourse.bass_utils import run_bass_kernel_spmd

    nc = bacc.Bacc("TRN2", target_bir_lowering=False, num_devices=1)
    arrays, aps = {}, {}
    for name, a in {**inputs, **constants()}.items():
        a = np.ascontiguousarray(a)
        arrays[f"in_{name}"] = a
        aps[name] = nc.dram_tensor(f"in_{name}", a.shape, mybir.dt.from_np(a.dtype), kind="ExternalInput").ap()
    out = nc.dram_tensor("out", (1, SEQ, D), F32, kind="ExternalOutput").ap()
    build(nc, aps, out)
    r = run_bass_kernel_spmd(nc, [arrays], core_ids=[0])
    return r.results[0]["out"]
```

```python
from contextlib import ExitStack

import numpy as np

import concourse.bass as bass
from concourse import mybir

F32 = mybir.dt.float32
F16 = mybir.dt.float16
U32 = mybir.dt.uint32
I32 = mybir.dt.int32
ALU = mybir.AluOpType
ACT = mybir.ActivationFunctionType
AX = mybir.AxisListType

P = 128
D = 1024
KC = D // P
SEQ = 256
META = 16
T1 = SEQ + META
T2 = SEQ
DEPTH = 2
FF = 2816
FC = FF // P
FFE = 3584
EC = FFE // P
EXPERTS = 8
HEADS1 = 8
NOPE, ROPE, VH = 64, 32, 64
QK = NOPE + ROPE
ML_HEADS = 4
FOX_HEADS, FOX_DH = 8, 64
ALPHA = (2 * DEPTH) ** 0.25
LN_EPS, RMS_EPS = 1e-5, 1e-6
NEG = -1e30
WS = 64.0
UNW = 1.0 / WS
SLOTS = 4
AHEAD = 2
BUFS = 3
UNIT = 16 * P


DOWN_COLS = 256
DOWN_BLOCKS = D // DOWN_COLS
DOWN_GROUPS = 4
HI_GATHERED, HI_TAKEN, LO_GATHERED, LO_TAKEN = (0, 3), (1, 0), (1, 3), (2, 0)


SPREAD = (4, 0)


class Phase:

    def __init__(self, first, units, size, base, after, gates):
        self.first, self.units, self.size, self.base, self.after, self.gates = first, units, size, base, after, gates


def schedule(rows, first, vec, act, gates, behind):
    out = {}
    sizes = [size for _, units, size, _, _, _ in rows for _ in range(units)] + behind
    at = 0
    for name, units, size, who, outputs, up in rows:
        out[name] = Phase(first + at, units, size, vec if who == "vec" else act, sizes[at + units:at + units + 2], gates)
        at += units
        vec += outputs if who == "vec" else 0
        act += outputs if who == "act" else 0
        gates += outputs if up else 0
    return out, first + at, vec, act, gates


ROWS1 = [
    ("up1", FC, UNIT, "vec", FC, True),
    ("down1", 2 * KC, FC // 2 * P, "vec", KC, False),
    ("win", 16, UNIT, "act", 16, False),
    ("uq", 2, 2 * 4 * QK, "act", 4, False),
    ("uk", 1, HEADS1 * NOPE, "act", 4, False),
    ("uv", 1, HEADS1 * VH, "act", 3, False),
    ("branch", KC, 8 * P, "vec", KC, False),
    ("wo", 4, UNIT, "vec", 4, False),
    ("up2", FC, UNIT, "vec", FC, True),
    ("down2", 2 * KC, FC // 2 * P, "vec", KC, False),
]
MIX2 = [
    ("values", 4, UNIT, "act", 4, False),
    ("small", 1, KC * 16, "act", 1, False),
    ("plain", 10, UNIT, "act", 10, False),
    ("gated", 14, UNIT, "act", 14, False),
    ("group", 1, 4 * P, "act", 2, False),
    ("branch", KC, 12 * P, "vec", KC, False),
    ("wout", 4, UNIT, "vec", 4, False),
]
DENSE2 = [("up", FC, UNIT, "vec", FC, True), ("down", 2 * KC, FC // 2 * P, "vec", KC, False)]
EXPERT2 = [("up", EC, UNIT, "vec", EC, True), ("down", DOWN_BLOCKS * DOWN_GROUPS, EC // DOWN_GROUPS * DOWN_COLS, "vec", 0, False)]

S1, L_UNITS, L_VEC, L_ACT, L_GATES = schedule(ROWS1, 0, 0, 0, 0, [UNIT, UNIT])
S20, g_, v_, a_, s_ = schedule(MIX2 + DENSE2, DEPTH * L_UNITS, DEPTH * L_VEC, DEPTH * L_ACT, DEPTH * L_GATES, [UNIT, UNIT])
V_LAYER1 = v_
S21, E_FIRST, E_VEC, E_ACT, E_GATES = schedule(MIX2, g_, v_, a_, s_, [UNIT, UNIT])
SE, g_, _, _, _ = schedule(EXPERT2, E_FIRST, E_VEC, E_ACT, E_GATES, [UNIT, UNIT])
E_UNITS = g_ - E_FIRST
SE_LAST, _, _, _, _ = schedule(EXPERT2, E_FIRST, E_VEC, E_ACT, E_GATES, [0, 0])
assert L_UNITS % SLOTS == 0 and E_UNITS % SLOTS == 0
V_END0 = S21["branch"].base
A_PER2 = 4 + 1 + 10 + 14 + 2

WIN_ORDER = [6, 7, 0, 1, 2, 3, 4, 5, 8, 9, 10, 11, 12, 13, 14, 15]
LAT_SQUARED, LAT_SUMMED, LAT_ROOT, LAT_NORMED, LAT_HI, LAT_LO = 2, 3, 5, 6, 8, 9

C1 = {"ln_g": 0, "ln_b": 24, "gate_b": 48, "conv": 64, "q_g": 76, "kv_g": 78}
N1 = 79
C2 = {"mix_g": 0, "pool_s": 8, "conv": 12, "ml_g": 44, "ffn_g": 48}
N2 = 56
N_CONST = 16
QB2 = [(0, 128, 128), (128, 128, 256)]
KB2 = [(0, 0, 128, 0), (128, 256, 128, 128)]
QB1 = [(0, 128, 128), (128, 128, 256), (256, 16, 272)]
KB1 = [(0, 0, 128, 0), (128, 272, 128, 128), (256, 416, 16, 256)]


ML_INVERTED, ML_SCALED, ML_HI, ML_LO = (2, 4, 6, 8), 10, 12, 14


def over_units(eng, phase, quads, body, loop=True):
    trips = phase.units // SLOTS if loop else 0
    if trips > 1:
        with eng.Fori(0, trips) as trip:
            for j in range(SLOTS):
                body(trip, j, phase.first + j, quads + trip)
    else:
        trips = 0
    for u in range(trips * SLOTS, phase.units):
        body(u // SLOTS, u % SLOTS, phase.first + u % SLOTS, quads + u // SLOTS)


def over_units_ahead(eng, phase, quads, split, take, loop=True):
    same = phase.after == [phase.size, phase.size]
    inner = phase.units if same else max(phase.units - AHEAD, 0)
    trips = inner // SLOTS if loop else 0

    def step(trip, j, q, size, take_first=False):
        g = phase.first + j
        if take_first:
            take(trip, j, g, q)
        if size:
            split(g + AHEAD, q, size)
        if not take_first:
            take(trip, j, g, q)

    if trips > 1:
        with eng.Fori(0, trips) as trip:
            for j in range(SLOTS):
                step(trip, j, quads + trip, phase.size)
    else:
        trips = 0
    for u in range(trips * SLOTS, phase.units):
        late = u + AHEAD - phase.units
        step(u // SLOTS, u % SLOTS, quads + u // SLOTS, phase.size if late < 0 else phase.after[late], take_first=late == AHEAD - 1)


def halves(banks):
    return banks.rearrange("p b (h t) -> p (b h) t", t=T2)


class Core:
    pass


def allocate(nc, ctx):
    k = Core()

    def sb(name, shape, dt):
        return ctx.enter_context(nc.sbuf_tensor(name, shape, dt))

    def sem(name):
        return ctx.enter_context(nc.semaphore(name))

    k.w32 = sb("w32", [P, SLOTS, UNIT], F32)
    k.w_hi = sb("w_hi", [P, SLOTS, UNIT], F16)
    k.w_lo = sb("w_lo", [P, SLOTS, UNIT], F16)
    k.h = sb("h", [P, KC, T1], F32)
    k.x_hi = sb("x_hi", [P, KC, T1], F16)
    k.x_lo = sb("x_lo", [P, KC, T1], F16)
    k.sq = sb("sq", [P, KC, T1], F32)
    ff = sb("ff", [P, EC * T2], F32)
    k.a_hi1 = ff[:, 0:FC * T1 // 2].bitcast(F16).rearrange("p (c t) -> p c t", t=T1)
    k.a_lo1 = ff[:, FC * T1 // 2:FC * T1].bitcast(F16).rearrange("p (c t) -> p c t", t=T1)
    k.a_hi2 = ff[:, 0:EC * T2 // 2].bitcast(F16).rearrange("p (c t) -> p c t", t=T2)
    k.a_lo2 = ff[:, EC * T2 // 2:EC * T2].bitcast(F16).rearrange("p (c t) -> p c t", t=T2)
    k.a_hi3 = ff[:, 0:EC * P // 2].bitcast(F16).rearrange("p (c t) -> p c t", t=P)
    k.a_lo3 = ff[:, EC * P // 2:EC * P].bitcast(F16).rearrange("p (c t) -> p c t", t=P)
    n = HEADS1 * T1
    k.qf = ff[:, 0:n].rearrange("p (h t) -> p h t", t=T1)
    k.kf = ff[:, n:2 * n].rearrange("p (h t) -> p h t", t=T1)
    k.rope_a = ff[:, 2 * n:3 * n].rearrange("p (h t) -> p h t", t=T1)
    k.qkc = ff[:, 0:8 * T2].rearrange("p (c t) -> p c t", t=T2)
    k.vtok = ff[:, 8 * T2:16 * T2].rearrange("p (t n) -> p t n", n=4 * T2)
    k.tap = ff[:, 16 * T2:24 * T2].rearrange("p (c t) -> p c t", t=T2)
    mix = sb("mix", [P, 48 * T2], F32)
    k.mix1 = mix[:, 0:32 * T1].rearrange("p (c t) -> p c t", t=T1)
    k.vt1 = mix[:, 32 * T1:32 * T1 + 3 * 512].rearrange("p (b n) -> p b n", n=512)
    k.mix2 = mix[:, :].rearrange("p (c t) -> p c t", t=T2)
    k.tokens = mix[:, 0:3 * D].rearrange("p (b n) -> p b n", n=D)
    k.xt_hi = mix[:, 0:D].bitcast(F16).rearrange("p (b n) -> p b n", n=D)
    k.xt_lo = mix[:, D:2 * D].bitcast(F16).rearrange("p (b n) -> p b n", n=D)
    k.to_slot = mix[:, 2 * D:3 * D].bitcast(F16).rearrange("p (b e s) -> p b e s", b=2, s=P)
    k.to_token = mix[:, 3 * D:4 * D].bitcast(F16).rearrange("p (e t) -> p e t", t=T2)
    k.d_hi = mix[:, 4 * D:4 * D + DOWN_COLS // 2].bitcast(F16)
    k.d_lo = mix[:, 4 * D + DOWN_COLS // 2:4 * D + DOWN_COLS].bitcast(F16)
    at = 4 * D + DOWN_COLS
    k.final_g = mix[:, at:at + D]
    k.out_rows = mix[:, at + D:at + 3 * D].rearrange("p (b n) -> p b n", n=D)
    k.squares = mix[:, at + 3 * D:at + 5 * D].rearrange("p (b n) -> p b n", n=D)
    k.zeros = mix[:, at + 5 * D:at + 5 * D + 256].bitcast(F16)
    k.prod = sb("prod", [P, 2, T1], F32)
    k.tmp = sb("tmp", [P, 3, T1], F32)
    k.silu = k.tmp[:, 0:2, :]
    k.y_hi = sb("y_hi", [P, 3, 4, T1], F16)
    k.y_lo = sb("y_lo", [P, 3, 4, T1], F16)
    k.pa = sb("pa", [P, 4, T1 + 2], F32)
    k.pb = sb("pb", [P, 4, T1 + 2], F32)
    at = 2 * n
    k.sc = ff[:, at:at + BUFS * T1].rearrange("p (b t) -> p b t", t=T1)
    at += BUFS * T1
    k.pr = ff[:, at:at + BUFS * T1].rearrange("p (b t) -> p b t", t=T1)
    at += BUFS * T1
    k.pt = ff[:, at:at + 2 * 432].rearrange("p (b t) -> p b t", t=432)
    k.stat = sb("stat", [P, BUFS, 8], F32)
    k.std = k.sq[:, 6:8, :]
    k.rstd = sb("rstd", [P, 2, T1], F32)
    k.gp = sb("gp", [P, 2, 16], F32)
    k.gx = sb("gx", [P, 2, 16], F32)
    k.ge = sb("ge", [P, 2, 16], F32)
    k.gl = sb("gl", [P, 2, 16], F32)
    k.lf = sb("lf", [P, 2, 12], F32)
    k.lf_fox = sb("lf_fox", [P, 2, FOX_HEADS], F32)
    k.cum = sb("cum", [P, 2, 12], F32)
    k.gbias = sb("gbias", [P, DEPTH, 16], F32)
    k.wr = sb("wr", [P, KC, EXPERTS], F32)
    k.rb = sb("rb", [P, EXPERTS], F32)
    k.lg = sb("lg", [P, 2, EXPERTS], F32)
    k.top = sb("top", [P, 2, 8], F32)
    k.topi = sb("topi", [P, 2, 8], U32)
    k.topf = sb("topf", [P, 2, 8], F32)
    k.rt = sb("rt", [P, 2, 8], F32)
    k.ga = sb("ga", [P, 2, EXPERTS], F32)
    k.gb = sb("gb", [P, 2, EXPERTS], F32)
    k.gates = sb("gates", [P, 2, EXPERTS], F32)
    k.member = sb("member", [P, 2, EXPERTS], F32)
    k.sel = sb("sel", [P, 2, EXPERTS], F32)
    k.slot_gate = sb("slot_gate", [P, EXPERTS], F32)
    k.gate_now = sb("gate_now", [P, 1], F32)
    k.most = sb("most", [P, 1], F32)
    k.more = sb("more", [P, 1], I32)
    k.slots = sb("slots", [P, P], F32)
    k.slot_col = sb("slot_col", [P, 1], F32)
    k.ms = sb("ms", [P, 2, 4], F32)
    k.rows = sb("rows", [N1, P], F32)
    k.col = sb("col", [P, N1], F32)
    k.rows2 = sb("rows2", [N2, DEPTH, P], F32)
    k.col2 = sb("col2", [P, DEPTH, N2], F32)
    k.pscale = sb("pscale", [P, DEPTH, 4], F32)
    k.ident = sb("ident", [P, P], F32)
    k.tri = sb("tri", [P, P], F32)
    k.ntri = sb("ntri", [P, 2 * P], F32)
    k.mask = sb("mask", [P, 3 * P], F32)
    k.mean_w = sb("mean_w", [P, P], F32)
    k.ones = sb("ones", [P, P], F32)
    k.cos = sb("cos", [P, T1], F32)
    k.sin = sb("sin", [P, T1], F32)
    k.rot = sb("rot", [P, ROPE], F32)
    k.place = sb("place", [ROPE, 2, QK], F32)
    k.icnt = sb("icnt", [P, 4, 16], F32)
    k.eidx = sb("eidx", [P, EXPERTS], F32)
    k.eps = sb("eps", [P, 3], F32)
    k.warm = sb("warm", [P, 1], F32)
    k.ps = ctx.enter_context(nc.psum_tensor("ps", [P, 8, 512], F32))

    k.loaded = [sem(f"loaded{j}") for j in range(SLOTS)]
    k.fox_loaded = [sem(f"fox_loaded{j}") for j in range(SLOTS)]
    k.hi_ready = sem("hi_ready")
    k.parts_ready = sem("parts_ready")
    k.unit_done = sem("unit_done")
    k.vec_evac = sem("vec_evac")
    k.act_evac = sem("act_evac")
    k.silu_ready = sem("silu_ready")
    k.ff_ready = sem("ff_ready")
    k.const_loaded = sem("const_loaded")
    k.consts_set = sem("consts_set")
    k.vec_loaded = sem("vec_loaded")
    k.vec_turned = sem("vec_turned")
    k.vec_ready = sem("vec_ready")
    k.tokens_loaded = sem("tokens_loaded")
    k.turned = sem("turned")
    k.turned_out = sem("turned_out")
    k.h_ready = sem("h_ready")
    k.sum_added = sem("sum_added")
    k.ln_scaled = sem("ln_scaled")
    k.rms_scaled = sem("rms_scaled")
    k.x_hi_ready = sem("x_hi_ready")
    k.x_ready = sem("x_ready")
    k.ln_mean = sem("ln_mean")
    k.ln_centered = sem("ln_centered")
    k.ln_squared = sem("ln_squared")
    k.ln_var = sem("ln_var")
    k.ln_std = sem("ln_std")
    k.lat_squared = sem("lat_squared")
    k.lat_mean = sem("lat_mean")
    k.lat_std = sem("lat_std")
    k.lat_normed = sem("lat_normed")
    k.lat_hi = sem("lat_hi")
    k.lat_ready = sem("lat_ready")
    k.kr_placed = sem("kr_placed")
    k.q_turned = sem("q_turned")
    k.q_rot_used = sem("q_rot_used")
    k.k_full = sem("k_full")
    k.q_full = sem("q_full")
    k.conv_ready = sem("conv_ready")
    k.scored = sem("scored")
    k.masked = sem("masked")
    k.exped = sem("exped")
    k.sum_inverted = sem("sum_inverted")
    k.probs_ready = sem("probs_ready")
    k.pt_written = sem("pt_written")
    k.pt_ready = sem("pt_ready")
    k.heads_summed = sem("heads_summed")
    k.y_hi_ready = sem("y_hi_ready")
    k.y_ready = sem("y_ready")
    k.merged_ready = sem("merged_ready")
    k.small_ready = sem("small_ready")
    k.gate_ln = sem("gate_ln")
    k.lf_ready = sem("lf_ready")
    k.lf_fox_ready = sem("lf_fox_ready")
    k.cum_summed = sem("cum_summed")
    k.cum_ready = sem("cum_ready")
    k.pool_ready = sem("pool_ready")
    k.taps_ready = sem("taps_ready")
    k.qk_ready = sem("qk_ready")
    k.ml_squared = sem("ml_squared")
    k.ml_mean = sem("ml_mean")
    k.ml_std = sem("ml_std")
    k.ml_ready = sem("ml_ready")
    k.rms_squared = sem("rms_squared")
    k.rms_mean = sem("rms_mean")
    k.rms_std = sem("rms_std")
    k.zeros_set = sem("zeros_set")
    k.routed = sem("routed")
    k.xt_turned = sem("xt_turned")
    k.xt_hi_ready = sem("xt_hi_ready")
    k.xt_ready = sem("xt_ready")
    k.member_ready = sem("member_ready")
    k.rank_summed = sem("rank_summed")
    k.sel_ready = sem("sel_ready")
    k.sel_spread = sem("sel_spread")
    k.choice_ready = sem("choice_ready")
    k.more_ready = sem("more_ready")
    k.slots_ready = sem("slots_ready")
    k.hi_gathered = sem("hi_gathered")
    k.lo_gathered = sem("lo_gathered")
    k.xe_hi_ready = sem("xe_hi_ready")
    k.xe_ready = sem("xe_ready")
    k.down_hi_ready = sem("down_hi_ready")
    k.down_ready = sem("down_ready")
    k.all_added = sem("all_added")
    k.final_g_loaded = sem("final_g_loaded")
    k.final_std = sem("final_std")
    k.row_ready = sem("row_ready")
    k.lg_ready = sem("lg_ready")
    k.lg_exped = sem("lg_exped")
    k.gate_spread = sem("gate_spread")
    k.stored = sem("stored")
    k.rows2_loaded = sem("rows2_loaded")
    k.cols2_turned = sem("cols2_turned")
    k.cols2_ready = sem("cols2_ready")
    k.pe_steps = sem("pe_steps")
    k.sp_steps = sem("sp_steps")
    k.pool_steps = sem("pool_steps")
    k.latent_out = sem("latent_out")
    k.ml_hi = sem("ml_hi")
    k.ml_parts = sem("ml_parts")
    return k


def sp_program(sp, k, i, out):
    def slot(g, q, shape_a, src_a, shape_b=None, src_b=None):
        s = g % SLOTS
        sp.wait_ge(k.parts_ready, q * SLOTS + (g + 1))
        sp.sem_inc(k.sp_steps, 1)
        lo = 0
        for (c, n), src in ((shape_a, src_a), (shape_b, src_b)):
            dst = k.w32[:, s, lo:lo + c * n].rearrange("p (c n) -> p c n", n=n)
            sp.dma_start(dst, src).then_inc(k.loaded[s], 16)
            lo += c * n

    def chunks(w, c0, c, n0, n):
        return w[c0 * P:(c0 + c) * P, :][:, bass.ds(n0, n)].rearrange("(c p) n -> p c n", p=P)

    def up(phase, q, w_gate, w_up, gate0, up0):
        def unit(trip, j, g, q):
            u = (trip * SLOTS + j) * P
            slot(g, q, (KC, P), chunks(w_gate, 0, KC, u + gate0, P), (KC, P), chunks(w_up, 0, KC, u + up0, P))
        over_units(sp, phase, q, unit)

    def down(phase, q, w, fc):
        half, part = fc // 2, fc // 4
        cut = [(0, part), (part, half - part)]

        def unit(trip, j, g, q):
            m = (trip * 2 + j // 2) * P
            at = (j % 2) * half
            (a0, an), (b0, bn) = cut
            slot(g, q, (an, P), chunks(w, at + a0, an, m, P), (bn, P), chunks(w, at + b0, bn, m, P))
        over_units(sp, phase, q, unit)

    def wide(phase, q, w, col):
        def unit(trip, j, g, q):
            c = col(trip, j)
            slot(g, q, (KC // 2, 256), chunks(w, 0, KC // 2, c, 256), (KC // 2, 256), chunks(w, KC // 2, KC // 2, c, 256))
        over_units(sp, phase, q, unit)

    def part(phase, first, units):
        return Phase(phase.first + first, units, phase.size, 0, [], 0)

    with sp.Fori(0, DEPTH) as l:
        q = l * (L_UNITS // SLOTS)
        up(S1["up1"], q, i["ffn1_w_up"][l], i["ffn1_w_up"][l], 0, FF)
        down(S1["down1"], q, i["ffn1_w_down"][l], FC)
        w_in = i["mix_w_in"][l]
        win = S1["win"]
        over = lambda t, j: (t * SLOTS + j) * 256
        for at, u in enumerate(WIN_ORDER):
            c0 = u * 256 if u < 8 else 1952 + (u - 8) * 256
            slot(win.first + at % SLOTS, q + at // SLOTS, (KC // 2, 256), chunks(w_in, 0, KC // 2, c0, 256),
                 (KC // 2, 256), chunks(w_in, KC // 2, KC // 2, c0, 256))
        for u in range(2):
            n = 4 * QK
            slot(S1["uq"].first + u, q, (1, n), chunks(i["w_uq"][l], 0, 1, u * n, n), (1, n), chunks(i["w_uq"][l], 1, 1, u * n, n))
        kv = i["w_ukv"][l].rearrange("p (h n) -> p h n", n=NOPE + VH)
        for u, name in enumerate(("uk", "uv")):
            slot(S1[name].first, q, (4, NOPE), kv[:, 0:4, u * NOPE:(u + 1) * NOPE], (4, NOPE), kv[:, 4:8, u * NOPE:(u + 1) * NOPE])

        def branch(trip, j, g, q):
            m = (trip * SLOTS + j) * P
            slot(g, q, (4, P), chunks(i["w_br_conv"][l], 0, 4, m, P), (4, P), chunks(i["w_br_mla"][l], 0, 4, m, P))
        over_units(sp, S1["branch"], q, branch)
        wide(S1["wo"], q, i["w_o"][l], over)
        up(S1["up2"], q, i["ffn2_w_up"][l], i["ffn2_w_up"][l], 0, FF)
        down(S1["down2"], q, i["ffn2_w_down"][l], FC)

    for l in range(DEPTH):
        s = S20 if l == 0 else S21
        w_in = i["w_in_2"][l]
        wide(s["values"], 0, w_in, lambda t, j: 1536 + 256 * j if j < 2 else 3592 + 256 * (j - 2))
        g = s["small"].first
        slot(g, 0, (KC, 8), chunks(w_in, 0, KC, 2560, 8), (KC, 8), chunks(w_in, 0, KC, 4104, 8))
        wide(part(s["plain"], 0, 6), 0, w_in, lambda t, j: (t * SLOTS + j) * 256)
        wide(part(s["plain"], 6, 4), 0, w_in, lambda t, j: 2568 + (t * SLOTS + j) * 256)
        wide(part(s["gated"], 0, 2), 0, w_in, lambda t, j: 2048 + (t * SLOTS + j) * 256)
        wide(part(s["gated"], 2, 12), 0, w_in, lambda t, j: 4112 + (t * SLOTS + j) * 256)
        grp = i["pool_w_grp_2"][l].rearrange("g c n -> c g n")
        slot(s["group"].first, 0, (2, P), grp[:, 0:2, :], (2, P), grp[:, 2:4, :])

        def branch2(trip, j, g, q):
            m = (trip * SLOTS + j) * P
            slot(g, q, (4, P), chunks(i["w_br_pool_2"][l], 0, 4, m, P), (4, P), chunks(i["w_br_ml_2"][l], 0, 4, m, P))
            dst = k.w32[:, g % SLOTS, 8 * P:12 * P].rearrange("p (c n) -> p c n", n=P)
            sp.dma_start(dst, chunks(i["w_br_fox_2"][l], 0, 4, m, P)).then_inc(k.fox_loaded[g % SLOTS], 16)
        over_units(sp, s["branch"], 0, branch2)
        wide(s["wout"], 0, i["w_out_2"][l], lambda t, j: (t * SLOTS + j) * 256)
        if l == 0:
            up(s["up"], 0, i["ff_w_gate_2"][0], i["ff_w_up_2"][0], 0, 0)
            down(s["down"], 0, i["ff_w_down_2"][0], FC)

    def moe_round(r):
        with sp.Fori(0, EXPERTS) as e:
            q = (e + r * EXPERTS) * (E_UNITS // SLOTS)
            up(SE["up"], q, i["moe_w_gate_2"][0][e], i["moe_w_up_2"][0][e], 0, 0)
            w = i["moe_w_down_2"][0][e]
            n = EC // DOWN_GROUPS

            def unit(trip, j, g, q):
                c, col = n * j, trip * DOWN_COLS
                slot(g, q, (n // 2, DOWN_COLS), chunks(w, c, n // 2, col, DOWN_COLS),
                     (n - n // 2, DOWN_COLS), chunks(w, c + n // 2, n - n // 2, col, DOWN_COLS))
            over_units(sp, SE["down"], q, unit)
    moe_round(0)
    sp.wait_ge(k.more_ready, 1)
    more = sp.value_load(k.more[0:1, 0:1], min_val=0, max_val=1)
    with sp.If(more > 0):
        moe_round(1)


def act_program(act, k, i, out):
    def split(g, q, size):
        s = g % SLOTS
        act.wait_ge(k.loaded[s], (q + g // SLOTS) * 32 + 32)
        if size == 12 * P:
            layer = 0 if g < S21["values"].first else 1
            first = (S20, S21)[layer]["branch"].first
            act.wait_ge(k.fox_loaded[s], (q + (g - first) // SLOTS + 2 * layer) * 16 + 16)
        act.wait_ge(k.unit_done, q * SLOTS + (g + 1))
        act.activation(k.w_hi[:, s, 0:size], k.w32[:, s, 0:size], ACT.Copy, scale=WS).then_inc(k.hi_ready, 1)

    def unit_used(g, q):
        act.wait_ge(k.unit_done, q * SLOTS + (g + 1 + SLOTS))

    def up(phase, q, vec0, gates0, t, loop=True):
        def take(trip, j, g, q):
            o = trip * SLOTS + j
            unit_used(g, q)
            act.wait_ge(k.vec_evac, vec0 + o + (phase.base + 1))
            act.activation(k.silu[:, j % 2, 0:t], k.ps[:, 2 * (j % 2), 0:t], ACT.Silu, scale=UNW).then_inc(k.silu_ready, 1)
        over_units_ahead(act, phase, q, split, take, loop)

    def ahead_only(phase, q):
        over_units_ahead(act, phase, q, split, lambda trip, j, g, q: None)

    def root_ready():
        act.activation(k.warm[:, :], k.eps[:, 0:1], ACT.Sqrt)

    def layer_norm(n, b0):
        root_ready()
        for c in range(KC):
            act.wait_ge(k.ln_centered, n * KC + (c + 1))
            act.activation(k.sq[:, c, :], k.h[:, c, :], ACT.Square).then_inc(k.ln_squared, 1)
        act.wait_ge(k.ln_var, n + 1)
        act.activation(k.std[:, 0, :], k.ps[:, 5, 0:T1], ACT.Sqrt, bias=k.eps[:, 0:1]).then_inc(k.ln_std, 1)
        for c in range(KC):
            act.wait_ge(k.ln_scaled, n * KC + (c + 1))
            act.activation(k.x_hi[:, c, :], k.sq[:, c, :], ACT.Identity, bias=k.col[:, b0 + c:b0 + c + 1]).then_inc(k.x_hi_ready, 1)
        for c in range(KC):
            a = act.activation(k.h[:, c, :], k.sq[:, c, :], ACT.Identity, bias=k.col[:, b0 + c:b0 + c + 1])
        a.then_inc(k.h_ready, 1)

    def rms_norm(n, to_parts=True):
        root_ready()
        for c in range(KC):
            act.activation(k.sq[:, c, 0:T2], k.h[:, c, META:T1], ACT.Square).then_inc(k.rms_squared, 1)
        act.wait_ge(k.rms_mean, n + 1)
        act.activation(k.std[:, 0, 0:T2], k.ps[:, 4, 0:T2], ACT.Sqrt, bias=k.eps[:, 1:2]).then_inc(k.rms_std, 1)
        if to_parts:
            for c in range(KC):
                act.wait_ge(k.rms_scaled, n * KC + c + 1)
                act.activation(k.x_hi[:, c, 0:T2], k.sq[:, c, 0:T2], ACT.Copy).then_inc(k.x_hi_ready, 1)

    def heads(items0, heads0, blocks, heads, exp, last_rows, norm=None, norm0=0, behind=None):
        nb = len(blocks)
        items = heads * nb

        def copy(h):
            act.wait_ge(k.pt_written, items0 + nb * (h + 1))
            if h >= 2:
                act.wait_ge(k.heads_summed, heads0 + h - 1)
            if last_rows:
                act.activation(k.pt[:, h % 2, 0:416], k.ps[:, 6 + h % 2, 0:416], ACT.Copy)
                act.activation(k.pt[0:last_rows, h % 2, 416:432], k.ps[0:last_rows, 6 + h % 2, 416:432], ACT.Copy).then_inc(k.pt_ready, 1)
            else:
                act.activation(k.pt[:, h % 2, 0:384], k.ps[:, 6 + h % 2, 0:384], ACT.Copy).then_inc(k.pt_ready, 1)

        for n in range(items):
            act.wait_ge(k.masked, items0 + n + 1)
            if n >= BUFS:
                act.wait_ge(k.pt_written, items0 + n - BUFS + 1)
            exp(n % BUFS, *blocks[n % nb][1:])
            if norm and n >= 1:
                act.wait_ge(k.sum_inverted, norm0 + n)
                norm((n - 1) % BUFS, *blocks[(n - 1) % nb][1:])
            if n >= nb + 1 and (n - nb - 1) % nb == 0:
                copy((n - nb - 1) // nb)
            if behind:
                behind(n)
        if norm:
            act.wait_ge(k.sum_inverted, norm0 + items)
            norm((items - 1) % BUFS, *blocks[(items - 1) % nb][1:])
        copy(heads - 1)

    def softmax_exp(b, queries, keys):
        act.activation(k.pr[0:queries, b, 0:keys], k.sc[0:queries, b, 0:keys], ACT.Exp, bias=k.stat[0:queries, b, 0:1],
                       accum_out=k.stat[0:queries, b, 1:2]).then_inc(k.exped, 1)

    def softmax_norm(b, queries, keys):
        act.activation(k.pr[0:queries, b, 0:keys], k.pr[0:queries, b, 0:keys], ACT.Copy, scale=k.stat[0:queries, b, 2:3]).then_inc(k.probs_ready, 1)

    def ml_exp(b, queries, keys):
        act.activation(k.pr[:, b, 0:keys], k.sc[:, b, 0:keys], ACT.Exp, bias=k.stat[:, b, 1:2])
        act.activation(k.stat[:, b, 4:5], k.stat[:, b, 1:2], ACT.Exp).then_inc(k.exped, 1)

    act.dma_start(k.ident[:, :], i["c_ident"]).then_inc(k.tokens_loaded, 16)
    act.dma_start(k.tokens[0:META, 0, :], i["meta_tokens"]).then_inc(k.tokens_loaded, 16)
    act.dma_start(k.tokens[:, 1:3, :], i["x"][0].rearrange("(b p) d -> p b d", p=P)).then_inc(k.tokens_loaded, 16)
    for c in range(KC):
        act.wait_ge(k.turned, c + 1)
        act.activation(k.h[:, c, :], k.ps[:, 4 + c % 4, 0:T1], ACT.Copy).then_inc(k.turned_out, 1)
    act.drain()
    act.activation(k.x_hi[:, :, :], k.h[:, :, :], ACT.Copy).then_inc(k.x_hi_ready, KC)
    act.sem_inc(k.h_ready, 1)
    split(0, 0, UNIT)
    split(1, 0, UNIT)

    with act.Fori(0, DEPTH) as l:
        q, vec0, act0, gates0 = l * (L_UNITS // SLOTS), l * L_VEC, l * L_ACT, l * L_GATES
        act.wait_ge(k.vec_turned, l + 1)
        for name, src, n in (("ln_g", i["ln_g"][l].rearrange("i (c p) -> (i c) p", p=P), 24),
                             ("ln_b", i["ln_b"][l].rearrange("i (c p) -> (i c) p", p=P), 24),
                             ("gate_b", i["mix_b_gate"][l].rearrange("i (c p) -> (i c) p", p=P), 16),
                             ("conv", i["conv_w"][l].rearrange("i (c p) -> (i c) p", p=P), 12),
                             ("q_g", i["q_norm_g"][l].rearrange("(c p) -> c p", p=P), 2),
                             ("kv_g", i["kv_norm_g"][l].rearrange("(c p) -> c p", p=P), 1)):
            act.dma_start(k.rows[C1[name]:C1[name] + n, :], src).then_inc(k.vec_loaded, 16)
        up(S1["up1"], q, vec0, gates0 + S1["up1"].gates, T1)
        ahead_only(S1["down1"], q)
        act.wait_ge(k.vec_turned, l + 2)
        act.activation(k.col[:, :], k.ps[:, 6, 0:N1], ACT.Copy).then_inc(k.vec_ready, 1)
        act.drain()
        layer_norm(l * 3, C1["ln_b"])

        def take_win(at, g, q):
            unit_used(g, q)
            u, b = WIN_ORDER[at], 2 * (at % 2)
            if u < 8:
                act.activation(k.mix1[:, 2 * u:2 * u + 2, :], k.ps[:, b:b + 2, 0:T1], ACT.Copy, scale=UNW).then_inc(k.act_evac, 1)
            else:
                for c in range(2):
                    n = 2 * (u - 8) + c
                    a = act.activation(k.mix1[:, 16 + n, :], k.ps[:, b + c, 0:T1], ACT.Sigmoid, scale=UNW,
                                       bias=k.col[:, C1["gate_b"] + n:C1["gate_b"] + n + 1])
                a.then_inc(k.act_evac, 1)
        win = S1["win"]
        for u in range(win.units):
            late = u + AHEAD - win.units
            split(win.first + u + AHEAD, q, win.size if late < 0 else win.after[late])
            if u == LAT_SQUARED:
                act.drain()
                act.activation(k.sq[:, 0:3, :], k.mix1[:, 12:15, :], ACT.Square).then_inc(k.lat_squared, 1)
            if u == LAT_ROOT:
                act.wait_ge(k.lat_mean, l + 1)
                act.activation(k.std[:, 0, :], k.ps[:, 4, 0:T1], ACT.Sqrt, bias=k.eps[:, 1:2], scale=float(D) / 256)
                act.activation(k.std[:, 1, :], k.ps[:, 5, 0:T1], ACT.Sqrt, bias=k.eps[:, 1:2], scale=float(D) / 128).then_inc(k.lat_std, 1)
            if u == LAT_HI:
                act.wait_ge(k.lat_normed, l + 1)
                act.activation(k.y_hi[:, 2, 0:3, :], k.sq[:, 3:6, :], ACT.Copy).then_inc(k.lat_hi, 1)
            take_win(u, win.first + u, q)
        outs = 0
        lat0 = l * 7
        later = [S1["uk"].size, S1["uv"].size, S1["branch"].size, S1["branch"].size]
        for u, (name, n_out) in enumerate((("uq", 2), ("uq", 2), ("uk", 4), ("uv", 3))):
            g = S1["uq"].first + u
            split(g + AHEAD, q, later[u])
            for o in range(n_out):
                if o < n_out - 1:
                    act.wait_ge(k.latent_out, lat0 + outs + 1)
                    outs += 1
                else:
                    unit_used(g, q)
                b = 2 * (o % 2)
                if name == "uq":
                    h = 4 * u + 2 * o
                    a = act.activation(k.qf[0:QK, h:h + 2, :], k.ps[0:QK, b:b + 2, 0:T1], ACT.Copy, scale=UNW)
                elif name == "uk":
                    a = act.activation(k.kf[0:NOPE, 2 * o:2 * o + 2, :], k.ps[0:NOPE, b:b + 2, 0:T1], ACT.Copy, scale=UNW)
                else:
                    n = QB1[o][1]
                    a = act.activation(k.vt1[0:n, o, :], k.ps[0:n, b, :], ACT.Copy, scale=UNW)
                a.then_inc(k.act_evac, 1)
        heads(l * 24, l * 8, QB1, HEADS1, softmax_exp, META, softmax_norm, l * 24)
        for c in range(4):
            act.wait_ge(k.heads_summed, l * 8 + 2 * c + 2)
            act.activation(k.y_hi[:, 1, c, :], k.ps[:, c, 0:T1], ACT.Copy).then_inc(k.y_hi_ready, 1)
        ahead_only(S1["branch"], q)
        ahead_only(S1["wo"], q)
        layer_norm(l * 3 + 1, C1["ln_b"] + KC)
        up(S1["up2"], q, vec0, gates0 + S1["up2"].gates, T1)
        ahead_only(S1["down2"], q)
        layer_norm(l * 3 + 2, C1["ln_b"] + 2 * KC)

    act.wait_ge(k.cols2_turned, 1)
    for l in range(DEPTH):
        cp = act.activation(k.col2[:, l, :], k.ps[:, 6, l * N2:(l + 1) * N2], ACT.Copy)
    cp.then_inc(k.cols2_ready, 1)
    for l in range(DEPTH):
        s = S20 if l == 0 else S21
        if l == 0:
            act.drain()
            act.wait_ge(k.x_ready, (3 * DEPTH + 1) * KC)
        else:
            act.wait_ge(k.vec_evac, V_LAYER1 + 2)
        rms_norm(2 * l)

        def take_values(trip, j, g, q):
            unit_used(g, q)
            b = 2 * (j % 2)
            act.activation(k.vtok[:, :, 256 * j:256 * j + 256], k.ps[:, b:b + 2, 0:256], ACT.Copy, scale=UNW).then_inc(k.act_evac, 1)
        over_units_ahead(act, s["values"], 0, split, take_values)

        def take_small(trip, j, g, q):
            unit_used(g, q)
            act.activation(k.gp[:, :, :], k.ps[:, 0:2, 0:16], ACT.Copy, scale=UNW).then_inc(k.act_evac, 1)
        over_units_ahead(act, s["small"], 0, split, take_small)

        def take_plain(trip, j, g, q):
            c = (trip * SLOTS + j) * 2
            unit_used(g, q)
            b = 2 * (j % 2)
            act.activation(k.mix2[:, bass.ds(c, 2), :], k.ps[:, b:b + 2, 0:T2], ACT.Copy, scale=UNW).then_inc(k.act_evac, 1)
        over_units_ahead(act, s["plain"], 0, split, take_plain)
        act.wait_ge(k.small_ready, l + 1)
        act.activation(k.ge[:, :, :], k.gx[:, :, :], ACT.Abs)
        act.drain()
        act.activation(k.gl[:, :, :], k.ge[:, :, :], ACT.Exp, scale=-1.0)
        act.drain()
        act.activation(k.ge[:, :, :], k.gl[:, :, :], ACT.Ln, bias=1.0).then_inc(k.gate_ln, 1)

        def take_gated(trip, j, g, q):
            c = (trip * SLOTS + j) * 2 + 20
            unit_used(g, q)
            b = 2 * (j % 2)
            act.activation(k.mix2[:, bass.ds(c, 2), :], k.ps[:, b:b + 2, 0:T2], ACT.Sigmoid, scale=UNW).then_inc(k.act_evac, 1)
        over_units_ahead(act, s["gated"], 0, split, take_gated)
        act.wait_ge(k.taps_ready, l + 1)
        act.activation(k.qkc[:, :, :], k.qkc[:, :, :], ACT.Silu).then_inc(k.qk_ready, 1)

        g = s["group"].first
        split(g + AHEAD, 0, s["group"].after[1])
        act.wait_ge(k.unit_done, g + 1 + SLOTS)
        for o in range(2):
            for c in range(2):
                n = 2 * o + c
                a = act.activation(k.pa[:, n, 0:T2], k.ps[:, 2 * o + c, 0:T2], ACT.Copy, scale=k.pscale[:, l, n:n + 1])
            a.then_inc(k.act_evac, 1)

        i0 = (DEPTH + l) * 24
        h0 = DEPTH * 8 + l * 12
        heads(i0, h0, QB2, ML_HEADS, ml_exp, 0)
        act.wait_ge(k.heads_summed, h0 + ML_HEADS)
        act.activation(k.sq[:, 0:4, 0:T2], halves(k.ps[:, 0:2, :]), ACT.Square).then_inc(k.ml_squared, 1)
        act.wait_ge(k.ml_mean, l + 1)
        act.activation(k.sq[:, 4:8, 0:T2], halves(k.ps[:, 6:8, :]), ACT.Sqrt, bias=k.eps[:, 1:2], scale=float(D) / P).then_inc(k.ml_std, 1)

        def ml_high(n):
            if n == ML_HI:
                act.wait_ge(k.ml_ready, l + 1)
                act.activation(k.y_hi[:, 1, :, 0:T2], k.sq[:, 0:4, 0:T2], ACT.Copy).then_inc(k.ml_hi, 1)
        heads(i0 + 8, h0 + ML_HEADS, QB2, FOX_HEADS, softmax_exp, 0, softmax_norm, DEPTH * 24 + l * 2 * FOX_HEADS, behind=ml_high)
        for c in range(4):
            act.wait_ge(k.heads_summed, h0 + ML_HEADS + 4 * (c // 2) + 4)
            act.activation(k.y_hi[:, 2, c, 0:T2], k.ps[:, 2 + c // 2, (c % 2) * T2:(c % 2 + 1) * T2], ACT.Copy).then_inc(k.y_hi_ready, 1)
        ahead_only(s["branch"], 0)
        ahead_only(s["wout"], 0)
        act.wait_ge(k.vec_evac, s["wout"].base + 4 + 2)
        rms_norm(2 * l + 1, to_parts=l == 0)
        if l == 0:
            up(s["up"], 0, 0, s["up"].gates, T2)
            ahead_only(s["down"], 0)
    act.dma_start(k.final_g, i["final_norm_g_2"].rearrange("(a n) -> a n", a=1).broadcast_to([P, D])).then_inc(k.final_g_loaded, 16)
    act.activation(k.warm[:, :], k.eps[:, 0:1], ACT.Exp)
    act.wait_ge(k.lg_ready, 1)
    act.activation(k.rt[:, :, 1], k.rt[:, :, 0], ACT.Exp).then_inc(k.lg_exped, 1)
    act.wait_ge(k.xt_turned, 1)
    act.activation(k.xt_hi[:, :, :], k.ps[:, 0:4, :].rearrange("p (b c) n -> p b (c n)", b=2), ACT.Copy).then_inc(k.xt_hi_ready, 1)

    def take_gathered(n):
        act.wait_ge(k.hi_gathered, n + 1)
        act.activation(k.x_hi[:, :, 0:P], k.ps[:, 2:4, :].rearrange("p b (c s) -> p (b c) s", s=P), ACT.Copy).then_inc(k.xe_hi_ready, 1)

    def expert(r, e, sched, last):
        n = e + r * EXPERTS
        q = n * (E_UNITS // SLOTS)
        up(sched["up"], q, n * EC, None, P, loop=False)
        act.activation(k.gate_now[:, :], k.slot_gate[:, bass.ds(e, 1)], ACT.Copy)
        act.drain()

        def take_block(trip, j, g, q):
            if (trip, j) == HI_TAKEN and not last:
                take_gathered(n + 1)
            if j == DOWN_GROUPS - 1:
                unit_used(g, q)
                act.activation(k.d_hi, k.ps[:, trip % 2, 0:DOWN_COLS], ACT.Copy, scale=k.gate_now[:, 0:1]).then_inc(k.down_hi_ready, 1)
        over_units_ahead(act, sched["down"], q, split, take_block, loop=False)

    def moe_round(r):
        take_gathered(r * EXPERTS)
        act.wait_ge(k.slots_ready, r + 1)
        with act.Fori(0, EXPERTS - 1) as e:
            expert(r, e, SE, last=False)
        expert(r, EXPERTS - 1, SE_LAST, last=True)
    moe_round(0)
    act.wait_ge(k.more_ready, 1)
    more = act.value_load(k.more[0:1, 0:1], min_val=0, max_val=1)
    with act.If(more > 0):
        q1 = EXPERTS * (E_UNITS // SLOTS)
        split(E_FIRST, q1, UNIT)
        split(E_FIRST + 1, q1, UNIT)
        moe_round(1)

    act.wait_ge(k.all_added, 1)
    y = k.ps[:, 4:8, :].rearrange("p (b c) n -> p b (c n)", b=2)
    for b in range(2):
        act.activation(k.squares[:, b, :], y[:, b, :], ACT.Square, accum_out=k.ms[:, b, 0:1])
    act.drain()
    act.activation(k.ms[:, :, 1], k.ms[:, :, 0], ACT.Sqrt, bias=k.eps[:, 1:2], scale=1.0 / D).then_inc(k.final_std, 1)
    for b in range(2):
        act.wait_ge(k.row_ready, b + 1)
        act.dma_start(out[0, b * P:(b + 1) * P, :], k.out_rows[:, b, :]).then_inc(k.stored, 16)
    act.wait_ge(k.stored, 32)


def vec_program(vec, k, i, out):
    def split(g, q, size):
        s = g % SLOTS
        vec.wait_ge(k.hi_ready, q * SLOTS + (g + 1))
        vec.scalar_tensor_tensor(k.w_lo[:, s, 0:size], k.w32[:, s, 0:size], WS, k.w_hi[:, s, 0:size],
                                 ALU.mult, ALU.subtract).then_inc(k.parts_ready, 1)

    def unit_used(g, q):
        vec.wait_ge(k.unit_done, q * SLOTS + (g + 1 + SLOTS))

    def ahead_only(phase, q):
        over_units_ahead(vec, phase, q, split, lambda trip, j, g, q: None)

    def up(phase, q, gates0, t, factor):
        def take(trip, j, g, q):
            o, b = trip * SLOTS + j, j % 2
            vec.wait_ge(k.silu_ready, gates0 + o + (phase.gates + 1))
            vec.wait_ge(k.ff_ready, gates0 + o + (phase.gates + 1))
            vec.scalar_tensor_tensor(k.prod[:, b, 0:t], k.silu[:, b, 0:t], factor * UNW, k.ps[:, 2 * b + 1, 0:t],
                                     ALU.mult, ALU.mult).then_inc(k.vec_evac, 1)
        over_units_ahead(vec, phase, q, split, take)

    def down(phase, q, add):
        def take(trip, j, g, q):
            if (j % 2) == 1:
                unit_used(g, q)
                add(trip * 2 + j // 2, k.ps[:, 2 * (j // 2), :])
        over_units_ahead(vec, phase, q, split, take)

    def add_scaled(m, acc):
        vec.scalar_tensor_tensor(k.h[:, bass.ds(m, 1), :], k.h[:, bass.ds(m, 1), :], WS * ALPHA, acc[:, 0:T1].unsqueeze(1),
                                 ALU.mult, ALU.add).then_inc(k.vec_evac, 1)
        vec.drain()
        add_sum(m)

    def start_sum(n):
        vec.drain()
        vec.wait_ge(k.h_ready, n + 1)
        vec.memset(k.tmp[:, 2:3, :], 0.0)
        vec.drain()

    def add_sum(m):
        vec.tensor_tensor(k.tmp[:, 2:3, :], k.tmp[:, 2:3, :], k.h[:, bass.ds(m, 1), :], ALU.add).then_inc(k.sum_added, 1)
        vec.drain()

    def add_plain(m, acc):
        x = k.h[:, bass.ds(m, 1), META:T1]
        vec.scalar_tensor_tensor(x, acc[:, 0:T2].unsqueeze(1), UNW, x, ALU.mult, ALU.add).then_inc(k.vec_evac, 1)

    def scaled(c, t, lo, x_hi0):
        if c < KC:
            t(c)
        if lo and c > 0:
            vec.wait_ge(k.x_hi_ready, x_hi0 + c)
            lo(c - 1).then_inc(k.x_ready, 1)

    def layer_norm(n, g0, b0):
        vec.wait_ge(k.ln_mean, n + 1)
        for c in range(KC):
            vec.tensor_tensor(k.h[:, c, :], k.h[:, c, :], k.ps[:, 4, 0:T1], ALU.subtract).then_inc(k.ln_centered, 1)
        vec.wait_ge(k.ln_std, n + 1)
        vec.reciprocal(k.rstd[:, 0, :], k.std[:, 0, :])
        vec.drain()

        def t(c):
            vec.scalar_tensor_tensor(k.sq[:, c, :], k.h[:, c, :], k.col[:, g0 + c:g0 + c + 1], k.rstd[:, 0, :],
                                     ALU.mult, ALU.mult).then_inc(k.ln_scaled, 1)

        def lo(c):
            return vec.scalar_tensor_tensor(k.x_lo[:, c, :], k.sq[:, c, :], k.col[:, b0 + c:b0 + c + 1], k.x_hi[:, c, :], ALU.add, ALU.subtract)
        for c in range(KC + 1):
            scaled(c, t, lo, (n + 1) * KC)

    def rms_norm(n, l, g0, to_parts=True):
        vec.wait_ge(k.rms_std, n + 1)
        vec.reciprocal(k.rstd[:, 0, 0:T2], k.std[:, 0, 0:T2])
        vec.drain()

        def t(c):
            vec.scalar_tensor_tensor(k.sq[:, c, 0:T2], k.h[:, c, META:T1], k.col2[:, l, g0 + c:g0 + c + 1], k.rstd[:, 0, 0:T2],
                                     ALU.mult, ALU.mult).then_inc(k.rms_scaled, 1)

        def lo(c):
            return vec.tensor_tensor(k.x_lo[:, c, 0:T2], k.sq[:, c, 0:T2], k.x_hi[:, c, 0:T2], ALU.subtract)
        for c in range(KC + 1):
            scaled(c, t, lo if to_parts else None, (3 * DEPTH + n + 1) * KC)

    def heads(items0, blocks, heads, mask, norm, behind=None):
        nb = len(blocks)
        items = heads * nb
        for n in range(items + 1):
            if n < items:
                vec.wait_ge(k.scored, items0 + n + 1)
                if n >= BUFS:
                    vec.wait_ge(k.exped, items0 + n - BUFS + 1)
                mask(n // nb, n % nb, n % 2, n % BUFS, *blocks[n % nb])
            if n >= 1:
                m = n - 1
                vec.wait_ge(k.exped, items0 + m + 1)
                norm(m % 2, m % BUFS, *blocks[m % nb][1:])
            if behind:
                behind(n)

    def softmax_max(b, queries, keys):
        vec.drain()
        vec.tensor_reduce(k.stat[0:queries, b, 0:1], k.sc[0:queries, b, 0:keys], AX.X, ALU.max, negate=True).then_inc(k.masked, 1)

    def softmax_norm(bank, b, queries, keys):
        vec.reciprocal(k.stat[0:queries, b, 2:3], k.stat[0:queries, b, 1:2]).then_inc(k.sum_inverted, 1)

    def mla_mask(h, j, bank, b, first, queries, keys):
        vec.scalar_tensor_tensor(k.sc[0:queries, b, 0:keys], k.ps[0:queries, 4 + bank, 0:keys], QK ** -0.5,
                                 k.mask[0:queries, 256 - first:256 - first + keys], ALU.mult, ALU.add)
        softmax_max(b, queries, keys)

    vec.memset(k.mean_w[:, :], 1.0 / D)
    vec.memset(k.ones[:, :], 1.0)
    vec.memset(k.eps[:, 0:1], LN_EPS * WS * WS)
    vec.memset(k.eps[:, 1:2], RMS_EPS).then_inc(k.consts_set, 1)
    vec.sem_inc(k.parts_ready, SLOTS)
    vec.sem_inc(k.unit_done, SLOTS)
    vec.sem_inc(k.vec_evac, 2)
    vec.sem_inc(k.vec_turned, 1)
    vec.sem_inc(k.act_evac, 2)
    vec.sem_inc(k.ff_ready, 2)
    vec.wait_ge(k.x_hi_ready, KC)
    vec.tensor_tensor(k.x_lo[:, :, :], k.h[:, :, :], k.x_hi[:, :, :], ALU.subtract).then_inc(k.x_ready, KC)
    split(0, 0, UNIT)
    split(1, 0, UNIT)

    with vec.Fori(0, DEPTH) as l:
        q, gates0 = l * (L_UNITS // SLOTS), l * L_GATES
        up(S1["up1"], q, gates0, T1, 0.5)
        vec.wait_ge(k.const_loaded, 16 * N_CONST)
        start_sum(l * 3)
        down(S1["down1"], q, add_scaled)
        vec.wait_ge(k.vec_ready, l + 1)
        layer_norm(l * 3, C1["ln_g"], C1["ln_b"])
        r = slice(NOPE, QK)

        def towards_latents(trip, j, g, q):
            u = trip * SLOTS + j
            if u == LAT_NORMED:
                vec.wait_ge(k.lat_std, l + 1)
                vec.reciprocal(k.rstd[:, :, :], k.std[:, :, :])
                vec.drain()
                for c in range(3):
                    a = vec.scalar_tensor_tensor(k.sq[:, 3 + c, :], k.mix1[:, 12 + c, :], k.col[:, C1["q_g"] + c:C1["q_g"] + c + 1],
                                                 k.rstd[:, c // 2, :], ALU.mult, ALU.mult)
                a.then_inc(k.lat_normed, 1)
                vec.wait_ge(k.kr_placed, l + 1)
                vec.tensor_tensor(k.tmp[r, 0, :], k.ps[r, 6, 0:T1], k.cos[r, :], ALU.mult)
                vec.tensor_tensor(k.tmp[r, 1, :], k.ps[r, 7, 0:T1], k.sin[r, :], ALU.mult)
                vec.drain()
                vec.tensor_tensor(k.kf[r, :, :], k.tmp[r, 0:1, :].broadcast_to([ROPE, HEADS1, T1]),
                                  k.tmp[r, 1:2, :].broadcast_to([ROPE, HEADS1, T1]), ALU.add).then_inc(k.k_full, 1)
            if u == LAT_LO:
                vec.wait_ge(k.lat_hi, l + 1)
                vec.tensor_tensor(k.y_lo[:, 2, 0:3, :], k.sq[:, 3:6, :], k.y_hi[:, 2, 0:3, :], ALU.subtract).then_inc(k.lat_ready, 1)
        over_units_ahead(vec, S1["win"], q, split, towards_latents, loop=False)
        for u in range(2):
            split(S1["uq"].first + u + AHEAD, q, (S1["uk"].size, S1["uv"].size, S1["branch"].size, S1["branch"].size)[u])
        vec.wait_ge(k.act_evac, l * L_ACT + (S1["uq"].base + 4 + 2))
        vec.tensor_tensor(k.rope_a[r, :, :], k.qf[r, :, :], k.cos[r, :].unsqueeze(1).broadcast_to([ROPE, HEADS1, T1]), ALU.mult)
        for n in range(2):
            vec.drain()
            vec.wait_ge(k.q_turned, l * 2 + n + 1)
            vec.tensor_tensor(k.sq[r, 0:4, :], k.ps[r, 4:8, 0:T1], k.sin[r, :].unsqueeze(1).broadcast_to([ROPE, 4, T1]), ALU.mult).then_inc(k.q_rot_used, 1)
            vec.drain()
            a = vec.tensor_tensor(k.qf[r, 4 * n:4 * n + 4, :], k.rope_a[r, 4 * n:4 * n + 4, :], k.sq[r, 0:4, :], ALU.add)
        a.then_inc(k.q_full, 1)
        for u in range(2, 4):
            split(S1["uq"].first + u + AHEAD, q, (S1["uk"].size, S1["uv"].size, S1["branch"].size, S1["branch"].size)[u])
        heads(l * 24, QB1, HEADS1, mla_mask, softmax_norm)
        for c in range(4):
            vec.wait_ge(k.y_hi_ready, l * 4 + c + 1)
            a = vec.tensor_tensor(k.y_lo[:, 1, c, :], k.ps[:, c, 0:T1], k.y_hi[:, 1, c, :], ALU.subtract)
        a.then_inc(k.y_ready, 1)

        def take_branch(trip, j, g, q):
            m, b = trip * SLOTS + j, 2 * (j % 2)
            unit_used(g, q)
            vec.scalar_tensor_tensor(k.tmp[:, 0:1, :], k.ps[:, b:b + 1, 0:T1], UNW, k.mix1[:, bass.ds(m + 16, 1), :], ALU.mult, ALU.mult)
            vec.scalar_tensor_tensor(k.tmp[:, 1:2, :], k.ps[:, b + 1:b + 2, 0:T1], UNW, k.mix1[:, bass.ds(m + 24, 1), :],
                                     ALU.mult, ALU.mult).then_inc(k.vec_evac, 1)
            vec.drain()
            vec.tensor_tensor(k.tmp[:, 2:3, :], k.tmp[:, 0:1, :], k.tmp[:, 1:2, :], ALU.add)
            vec.drain()
            vec.tensor_copy(k.x_hi[:, bass.ds(m, 1), :], k.tmp[:, 2:3, :])
            vec.drain()
            vec.tensor_tensor(k.x_lo[:, bass.ds(m, 1), :], k.tmp[:, 2:3, :], k.x_hi[:, bass.ds(m, 1), :], ALU.subtract).then_inc(k.merged_ready, 1)
        over_units_ahead(vec, S1["branch"], q, split, take_branch)

        def take_wo(trip, j, g, q):
            c, b = (trip * SLOTS + j) * 2, 2 * (j % 2)
            unit_used(g, q)
            h = k.h[:, bass.ds(c, 2), :]
            vec.scalar_tensor_tensor(h, h, WS * ALPHA, k.ps[:, b:b + 2, 0:T1], ALU.mult, ALU.add).then_inc(k.vec_evac, 1)
            vec.drain()
            for n in range(2):
                add_sum(c + n)
        start_sum(l * 3 + 1)
        over_units_ahead(vec, S1["wo"], q, split, take_wo)
        layer_norm(l * 3 + 1, C1["ln_g"] + KC, C1["ln_b"] + KC)
        up(S1["up2"], q, gates0, T1, 0.5)
        start_sum(l * 3 + 2)
        down(S1["down2"], q, add_scaled)
        layer_norm(l * 3 + 2, C1["ln_g"] + 2 * KC, C1["ln_b"] + 2 * KC)

    for l in range(DEPTH):
        s = S20 if l == 0 else S21
        vec.drain()
        if l == 0:
            vec.wait_ge(k.cols2_ready, 1)
            vec.tensor_scalar(k.pscale[:, :, :], k.col2[:, :, C2["pool_s"]:C2["pool_s"] + 4], UNW, None, ALU.mult).then_inc(k.consts_set, 1)
            vec.wait_ge(k.h_ready, 3 * DEPTH + 1)
        rms_norm(2 * l, l, C2["mix_g"])
        ahead_only(s["values"], 0)
        ahead_only(s["small"], 0)
        vec.wait_ge(k.act_evac, s["small"].base + 1 + 2)
        vec.tensor_tensor(k.gx[:, :, :], k.gp[:, :, :], k.gbias[:, l, :].unsqueeze(1).broadcast_to([P, 2, 16]), ALU.add).then_inc(k.small_ready, 1)
        ahead_only(s["plain"], 0)
        vec.wait_ge(k.gate_ln, l + 1)
        vec.scalar_tensor_tensor(k.lf[:, :, :], k.gx[:, :, 4:16], 0.0, k.ge[:, :, 4:16], ALU.min, ALU.subtract).then_inc(k.lf_ready, 1)
        vec.drain()
        vec.tensor_scalar(k.lf_fox[:, :, :], k.lf[:, :, 4:12], FOX_DH ** 0.5, None, ALU.mult).then_inc(k.lf_fox_ready, 1)
        ahead_only(s["gated"], 0)
        vec.wait_ge(k.cum_summed, l + 1)
        vec.tensor_copy(k.cum[:, :, :], k.ps[:, 4, 0:32].rearrange("p (b n) -> p b n", n=16)[:, :, 0:12]).then_inc(k.cum_ready, 1)
        split(s["group"].first + AHEAD, 0, s["group"].after[1])
        vec.drain()

        def ml_mask(h, j, bank, b, first, queries, keys):
            vec.scalar_tensor_tensor(k.sc[:, b, 0:keys], k.ps[:, 4 + bank, 256:256 + keys], k.cum[:, j, h:h + 1],
                                     k.mask[:, 256 - 128 * j:256 - 128 * j + keys], ALU.add, ALU.add)
            vec.drain()
            vec.tensor_reduce(k.stat[:, b, 0:1], k.sc[:, b, 0:keys], AX.X, ALU.max)
            vec.drain()
            vec.tensor_scalar(k.stat[:, b, 1:2], k.stat[:, b, 0:1], k.cum[:, j, h:h + 1], -1.0, ALU.max, ALU.mult).then_inc(k.masked, 1)

        def ml_norm(bank, b, queries, keys):
            pr = k.pr[:, b, 0:keys]
            vec.scalar_tensor_tensor(pr, k.ps[:, 4 + bank, 0:keys], float(P) ** -0.5, pr, ALU.mult, ALU.mult, accum_out=k.stat[:, b, 3:4])
            vec.drain()
            vec.scalar_tensor_tensor(k.stat[:, b, 7:8], k.stat[:, b, 3:4], -1.0, k.stat[:, b, 3:4], ALU.mult, ALU.max)
            vec.drain()
            vec.tensor_tensor(k.stat[:, b, 5:6], k.stat[:, b, 7:8], k.stat[:, b, 4:5], ALU.max)
            vec.drain()
            vec.reciprocal(k.stat[:, b, 6:7], k.stat[:, b, 5:6])
            vec.drain()
            vec.tensor_scalar(pr, pr, k.stat[:, b, 6:7], None, ALU.mult).then_inc(k.probs_ready, 1)

        def fox_mask(h, j, bank, b, first, queries, keys):
            vec.tensor_scalar(k.sc[:, b, 0:keys], k.ps[:, 4 + bank, 0:keys], FOX_DH ** -0.5, k.cum[:, j, 4 + h:5 + h], ALU.mult, ALU.add)
            softmax_max(b, queries, keys)

        i0 = (DEPTH + l) * 24
        heads(i0, QB2, ML_HEADS, ml_mask, ml_norm)

        def ml_outputs(n):
            if n == ML_INVERTED[0]:
                vec.wait_ge(k.ml_std, l + 1)
            if n in ML_INVERTED:
                h = ML_INVERTED.index(n)
                vec.reciprocal(k.sq[:, 4 + h, 0:T2], k.sq[:, 4 + h, 0:T2])
            if n == ML_SCALED:
                vec.drain()
                for h in range(ML_HEADS):
                    vec.scalar_tensor_tensor(k.sq[:, h, 0:T2], k.ps[:, h // 2, (h % 2) * T2:(h % 2 + 1) * T2],
                                             k.col2[:, l, C2["ml_g"] + h:C2["ml_g"] + h + 1], k.sq[:, 4 + h, 0:T2], ALU.mult, ALU.mult)
                vec.drain()
                vec.tensor_tensor(k.sq[:, 0:4, 0:T2], k.sq[:, 0:4, 0:T2], k.mix2[:, 20:24, :], ALU.mult).then_inc(k.ml_ready, 1)
            if n == ML_LO:
                vec.wait_ge(k.ml_hi, l + 1)
                vec.tensor_tensor(k.y_lo[:, 1, :, 0:T2], k.sq[:, 0:4, 0:T2], k.y_hi[:, 1, :, 0:T2], ALU.subtract).then_inc(k.ml_parts, 1)
        heads(i0 + 2 * ML_HEADS, QB2, FOX_HEADS, fox_mask, softmax_norm, behind=ml_outputs)
        vec.wait_ge(k.act_evac, s["group"].base + 2 + 2)
        vec.tensor_copy(k.y_hi[:, 0, :, 0:T2], k.pa[:, :, 0:T2])
        vec.drain()
        vec.tensor_tensor(k.y_lo[:, 0, :, 0:T2], k.pa[:, :, 0:T2], k.y_hi[:, 0, :, 0:T2], ALU.subtract)
        for c in range(4):
            vec.wait_ge(k.y_hi_ready, (DEPTH + l) * 4 + 2 * (c // 2) + 2)
            a = vec.tensor_tensor(k.y_lo[:, 2, c, 0:T2], k.ps[:, 2 + c // 2, (c % 2) * T2:(c % 2 + 1) * T2], k.y_hi[:, 2, c, 0:T2], ALU.subtract)
        a.then_inc(k.y_ready, 1)

        def take_branch2(trip, j, g, q):
            m, b = trip * SLOTS + j, 2 * (j % 2)
            unit_used(g, q)
            for n in range(3):
                a = vec.scalar_tensor_tensor(k.tmp[:, n:n + 1, 0:T2], k.ps[:, b + n // 2:b + n // 2 + 1, 256 * (n % 2):256 * (n % 2) + 256], UNW,
                                             k.mix2[:, bass.ds(m + (24 + 8 * n), 1), :], ALU.mult, ALU.mult)
            a.then_inc(k.vec_evac, 1)
            vec.drain()
            vec.tensor_tensor(k.prod[:, 0:1, 0:T2], k.tmp[:, 0:1, 0:T2], k.tmp[:, 1:2, 0:T2], ALU.add)
            vec.drain()
            vec.tensor_tensor(k.prod[:, 1:2, 0:T2], k.prod[:, 0:1, 0:T2], k.tmp[:, 2:3, 0:T2], ALU.add)
            vec.drain()
            vec.tensor_copy(k.x_hi[:, bass.ds(m, 1), 0:T2], k.prod[:, 1:2, 0:T2])
            vec.drain()
            vec.tensor_tensor(k.x_lo[:, bass.ds(m, 1), 0:T2], k.prod[:, 1:2, 0:T2], k.x_hi[:, bass.ds(m, 1), 0:T2], ALU.subtract).then_inc(k.merged_ready, 1)
        over_units_ahead(vec, s["branch"], 0, split, take_branch2)

        def take_wout(trip, j, g, q):
            c, b = (trip * SLOTS + j) * 2, 2 * (j % 2)
            unit_used(g, q)
            x = k.h[:, bass.ds(c, 2), META:T1]
            vec.scalar_tensor_tensor(x, k.ps[:, b:b + 2, 0:T2], UNW, x, ALU.mult, ALU.add).then_inc(k.vec_evac, 1)
        over_units_ahead(vec, s["wout"], 0, split, take_wout)
        vec.drain()
        if l == 1:
            vec.memset(k.zeros, 0.0).then_inc(k.zeros_set, 1)
        rms_norm(2 * l + 1, l, C2["ffn_g"], to_parts=l == 0)
        if l == 0:
            up(s["up"], 0, 0, T2, 1.0)
            down(s["down"], 0, add_plain)

    vec.wait_ge(k.routed, 1)
    vec.tensor_tensor(k.lg[:, :, :], k.ps[:, 6:8, 0:EXPERTS],
                      k.rb[:, :].unsqueeze(1).broadcast_to([P, 2, EXPERTS]), ALU.add)
    vec.drain()
    for b in range(2):
        vec.max(k.top[:, b, :], k.lg[:, b, :])
    vec.drain()
    for b in range(2):
        vec.max_index(k.topi[:, b, :], k.top[:, b, :], k.lg[:, b, :])
    vec.tensor_tensor(k.rt[:, :, 0], k.top[:, :, 1], k.top[:, :, 0], ALU.subtract).then_inc(k.lg_ready, 1)
    vec.drain()
    vec.tensor_copy(k.topf[:, :, :], k.topi[:, :, :])
    vec.drain()
    for b in range(2):
        for n, dst in enumerate((k.ga, k.gb)):
            vec.tensor_scalar(dst[:, b, :], k.eidx[:, :], k.topf[:, b, n:n + 1], None, ALU.is_equal)
    vec.drain()
    vec.tensor_tensor(k.member[:, :, :], k.ga[:, :, :], k.gb[:, :, :], ALU.add).then_inc(k.member_ready, 1)
    vec.wait_ge(k.lg_exped, 1)
    vec.tensor_scalar(k.rt[:, :, 2], k.rt[:, :, 1], 1.0, None, ALU.add)
    vec.drain()
    vec.reciprocal(k.rt[:, :, 3], k.rt[:, :, 2])
    vec.drain()
    vec.tensor_tensor(k.rt[:, :, 4], k.rt[:, :, 1], k.rt[:, :, 3], ALU.mult)
    vec.drain()
    for b in range(2):
        vec.tensor_scalar(k.ga[:, b, :], k.ga[:, b, :], k.rt[:, b, 3:4], None, ALU.mult)
    vec.drain()
    for b in range(2):
        vec.scalar_tensor_tensor(k.gates[:, b, :], k.gb[:, b, :], k.rt[:, b, 4:5], k.ga[:, b, :], ALU.mult, ALU.add)
    vec.wait_ge(k.rank_summed, 1)
    vec.tensor_tensor(k.sel[:, :, :], k.member[:, :, :], k.ps[:, 5, 0:2 * EXPERTS].rearrange("p (b e) -> p b e", e=EXPERTS), ALU.mult).then_inc(k.sel_ready, 1)

    def dispatch(r):
        first = SPREAD[r]
        spread = halves(k.ps[:, first:first + 4, :])
        vec.drain()
        for b in range(2):
            for e in range(EXPERTS):
                vec.tensor_scalar(k.to_slot[:, b, e, :], k.slots[:, :], float(P * r), k.sel[:, b, e:e + 1], ALU.add, ALU.is_equal)
        if r == 0:
            vec.wait_ge(k.xt_hi_ready, 1)
            vec.tensor_tensor(k.xt_lo[:, :, :], k.ps[:, 0:4, :].rearrange("p (b c) n -> p b (c n)", b=2), k.xt_hi[:, :, :], ALU.subtract).then_inc(k.xt_ready, 1)
        vec.wait_ge(k.sel_spread, r + 1)
        if r == 0:
            vec.tensor_reduce(k.most[:, :], spread, AX.XY, ALU.max)
        vec.tensor_scalar(k.to_token[:, :, :], spread, -float(P * r), k.slot_col[:, 0:1], ALU.add, ALU.is_equal).then_inc(k.choice_ready, 1)
        if r == 0:
            vec.drain()
            vec.tensor_scalar(k.more[:, :], k.most[:, :], float(P), None, ALU.is_gt).then_inc(k.more_ready, 1)
            take_gathered(r * EXPERTS)
        vec.wait_ge(k.gate_spread, r + 1)
        for e in range(EXPERTS):
            a = vec.scalar_tensor_tensor(k.squares[:, 0, e * P:e * P + T2 // 2].bitcast(F16), k.to_token[:, e, :], UNW, spread[:, e, :],
                                         ALU.mult, ALU.mult, accum_out=k.slot_gate[:, e:e + 1])
        a.then_inc(k.slots_ready, 1)
        if r == 1:
            take_gathered(r * EXPERTS)

    def take_gathered(n):
        vec.wait_ge(k.lo_gathered, n + 1)
        vec.tensor_copy(k.x_lo[:, :, 0:P], k.ps[:, 2:4, :].rearrange("p b (c s) -> p (b c) s", s=P)).then_inc(k.xe_ready, 1)

    def expert(r, e, sched, last):
        n = e + r * EXPERTS
        q = n * (E_UNITS // SLOTS)
        up(sched["up"], q, n * EC, P, 1.0)

        def take_block(trip, j, g, q):
            if (trip, j) == LO_TAKEN and not last:
                take_gathered(n + 1)
            if j == DOWN_GROUPS - 1:
                vec.wait_ge(k.down_hi_ready, n * DOWN_BLOCKS + trip + 1)
                vec.scalar_tensor_tensor(k.d_lo, k.ps[:, trip % 2, 0:DOWN_COLS], k.slot_gate[:, bass.ds(e, 1)], k.d_hi,
                                         ALU.mult, ALU.subtract).then_inc(k.down_ready, 1)
        over_units_ahead(vec, sched["down"], q, split, take_block, loop=False)

    def moe_round(r):
        dispatch(r)
        with vec.Fori(0, EXPERTS - 1) as e:
            expert(r, e, SE, last=False)
        expert(r, EXPERTS - 1, SE_LAST, last=True)
    moe_round(0)
    more = vec.value_load(k.more[0:1, 0:1], min_val=0, max_val=1)
    with vec.If(more > 0):
        q1 = EXPERTS * (E_UNITS // SLOTS)
        split(E_FIRST, q1, UNIT)
        split(E_FIRST + 1, q1, UNIT)
        moe_round(1)

    vec.wait_ge(k.final_g_loaded, 16)
    vec.wait_ge(k.final_std, 1)
    vec.reciprocal(k.ms[:, :, 2], k.ms[:, :, 1])
    vec.drain()
    y = k.ps[:, 4:8, :].rearrange("p (b c) n -> p b (c n)", b=2)
    for b in range(2):
        vec.scalar_tensor_tensor(k.out_rows[:, b, :], y[:, b, :], k.ms[:, b, 2:3], k.final_g, ALU.mult, ALU.mult).then_inc(k.row_ready, 1)


def pool_program(pool, k, i, out):
    def up(phase, vec0, t, a_hi, a_lo):
        def take(trip, j, g, q):
            o, b = trip * SLOTS + j, j % 2
            pool.wait_ge(k.vec_evac, vec0 + o + (phase.base + 2 + 1))
            pool.sem_inc(k.pool_steps, 1)
            pool.tensor_copy(a_hi[:, bass.ds(o, 1), :], k.prod[:, b:b + 1, 0:t])
            pool.drain()
            pool.tensor_tensor(a_lo[:, bass.ds(o, 1), :], k.prod[:, b:b + 1, 0:t], a_hi[:, bass.ds(o, 1), :], ALU.subtract).then_inc(k.ff_ready, 1)
        over_units(pool, phase, 0, take)

    n_const = 0
    for dst, src in ((k.tri, "c_tri"), (k.ntri, "c_ntri"), (k.mask, "c_mask"), (k.rot, "c_rot")):
        pool.dma_start(dst[:, :], i[src]).then_inc(k.const_loaded, 16)
        n_const += 1
    for dst, src in ((k.cos[64:96, :], i["c_cos"]), (k.sin[64:96, :], i["c_sin"]), (k.place[:, :, :], i["c_place"]),
                     (k.icnt[:, :, :], i["c_icnt"].rearrange("(a g) t -> a g t", a=1).broadcast_to([P, 4, 16])),
                     (k.eidx[:, :], i["c_eidx"].broadcast_to([P, EXPERTS])),
                     (k.slots[:, :], i["c_slots"].broadcast_to([P, P])),
                     (k.slot_col[:, :], i["c_slots"].rearrange("a s -> s a")),
                     (k.rb[:, :], i["moe_b_router_2"].broadcast_to([P, EXPERTS])),
                     (k.wr[:, :, :], i["moe_w_router_2"][0].rearrange("(c p) e -> p c e", p=P))):
        pool.dma_start(dst, src).then_inc(k.const_loaded, 16)
        n_const += 1
    for name, c0, n in (("ml_b_i_2", 0, 4), ("ml_b_f_2", 4, 4), ("fox_b_f_2", 8, 8)):
        pool.dma_start(k.gbias[:, :, c0:c0 + n], i[name].rearrange("(a l) n -> a l n", a=1).broadcast_to([P, DEPTH, n])).then_inc(k.const_loaded, 16)
        n_const += 1
    assert n_const == N_CONST
    for name, n in (("mix_g", 8), ("pool_s", 4), ("ml_g", 4), ("ffn_g", 8)):
        src = {"mix_g": "mix_norm_g_2", "pool_s": "pool_scale_2", "ml_g": "ml_norm_g_2", "ffn_g": "ffn_norm_g_2"}[name]
        pool.dma_start(k.rows2[C2[name]:C2[name] + n, :, :], i[src].rearrange("l (c p) -> c l p", p=P)).then_inc(k.rows2_loaded, 16)
    for l in range(DEPTH):
        pool.dma_start(k.rows2[C2["conv"]:C2["conv"] + 32, l, :], i["ml_conv_w_2"][l].rearrange("k (c p) -> (k c) p", p=P)).then_inc(k.rows2_loaded, 16)
    pool.memset(k.pa[:, :, :], 0.0)
    pool.memset(k.pb[:, :, :], 0.0)
    pool.drain()
    with pool.Fori(0, DEPTH) as l:
        up(S1["up1"], l * L_VEC, T1, k.a_hi1, k.a_lo1)
        pool.wait_ge(k.act_evac, l * L_ACT + (S1["win"].base + 8 + 2))
        pool.tensor_tensor(k.pa[:, :, 2:2 + T1], k.mix1[:, 4:8, :], k.mix1[:, 8:12, :], ALU.mult)
        pool.drain()
        c_acc, c_tap = k.mix1[:, 4:8, :], k.mix1[:, 8:12, :]
        for n in range(3):
            for c in range(4):
                w = k.col[:, C1["conv"] + 4 * n + c:C1["conv"] + 4 * n + c + 1]
                pool.tensor_scalar((c_tap if n else c_acc)[:, c, :], k.pa[:, c, n:n + T1], w, None, ALU.mult)
            pool.drain()
            if n:
                pool.tensor_tensor(c_acc, c_acc, c_tap, ALU.add)
                pool.drain()
        pool.tensor_tensor(c_acc, c_acc, k.mix1[:, 0:4, :], ALU.mult)
        pool.drain()
        pool.tensor_copy(k.y_hi[:, 0, :, :], c_acc)
        pool.drain()
        pool.tensor_tensor(k.y_lo[:, 0, :, :], c_acc, k.y_hi[:, 0, :, :], ALU.subtract).then_inc(k.conv_ready, 1)
        up(S1["up2"], l * L_VEC, T1, k.a_hi1, k.a_lo1)
    for l in range(DEPTH):
        s = S20 if l == 0 else S21
        pool.wait_ge(k.act_evac, s["plain"].base + 10 + 2)
        u = k.mix2[:, 4:12, :]
        for n in (3, 2, 1, 0):
            lag = 3 - n
            for c in range(8):
                w = k.col2[:, l, C2["conv"] + 8 * n + c:C2["conv"] + 8 * n + c + 1]
                pool.tensor_scalar((k.tap if lag else k.qkc)[:, c, :], u[:, c, :], w, None, ALU.mult)
            pool.drain()
            if lag:
                a = pool.tensor_tensor(k.qkc[:, :, lag:T2], k.qkc[:, :, lag:T2], k.tap[:, :, 0:T2 - lag], ALU.add)
                if n:
                    pool.drain()
        a.then_inc(k.taps_ready, 1)
        z = 16
        pool.memset(k.pa[:, :, 0:z], 0.0)
        pool.memset(k.pb[:, :, 0:z], 0.0)
        pool.tensor_copy(k.pa[:, :, z:z + T2], k.mix2[:, 0:4, :])
        a, b = k.pa, k.pb
        for n in range(4):
            pool.drain()
            w = 1 << n
            pool.tensor_tensor(b[:, n:4, z:z + T2], a[:, n:4, z:z + T2], a[:, n:4, z - w:z - w + T2], ALU.add)
            a, b = b, a
        pool.drain()
        for n in range(4):
            src = (k.pb, k.pa)[n % 2]
            pool.tensor_tensor(src[:, n, z:2 * z], src[:, n, z:2 * z], k.icnt[:, n, :], ALU.mult)
            pool.tensor_scalar(src[:, n, 2 * z:z + T2], src[:, n, 2 * z:z + T2], 1.0 / (2 << n), None, ALU.mult)
        pool.drain()
        for n in range(4):
            src = (k.pb, k.pa)[n % 2]
            pool.tensor_tensor(src[:, n, z:z + T2], src[:, n, z:z + T2], k.mix2[:, n, :], ALU.subtract)
        pool.drain()
        for n in range(4):
            src = (k.pb, k.pa)[n % 2]
            pool.tensor_copy(k.y_hi[:, 2, n, 0:T2], src[:, n, z:z + T2])
        pool.drain()
        for n in range(4):
            src = (k.pb, k.pa)[n % 2]
            a = pool.tensor_tensor(k.y_lo[:, 2, n, 0:T2], src[:, n, z:z + T2], k.y_hi[:, 2, n, 0:T2], ALU.subtract)
        a.then_inc(k.pool_ready, 1)
        if l == 0:
            up(s["up"], 0, T2, k.a_hi2, k.a_lo2)

    def moe_round(r):
        with pool.Fori(0, EXPERTS) as e:
            up(SE["up"], (e + r * EXPERTS) * EC, P, k.a_hi3, k.a_lo3)
    moe_round(0)
    pool.wait_ge(k.more_ready, 1)
    more = pool.value_load(k.more[0:1, 0:1], min_val=0, max_val=1)
    with pool.If(more > 0):
        moe_round(1)


def pe_program(pe, k, i, out):
    def parts(acc, w_hi, w_lo, x_hi, x_lo, first, last):
        pe.matmul(acc, w_hi, x_hi, start=first, stop=False)
        pe.matmul(acc, w_hi, x_lo, start=False, stop=False)
        return pe.matmul(acc, w_lo, x_hi, start=False, stop=last)

    def chain(acc, s, tiles, x_hi, x_lo, first=True, last=True, ready=None):
        for n, (c, m, kc) in enumerate(tiles):
            if ready is not None:
                pe.wait_ge(k.x_ready, ready + (kc + 1))
            a = parts(acc, k.w_hi[:, s, c:c + m], k.w_lo[:, s, c:c + m], x_hi[:, kc, :], x_lo[:, kc, :],
                      first and n == 0, last and n == len(tiles) - 1)
        return a

    def stand_alone():
        pe.sem_inc(k.pe_steps, 1)

    def weights(g, q):
        pe.wait_ge(k.parts_ready, q * SLOTS + (g + 1 + SLOTS))

    def all_out(vec, act):
        pe.wait_ge(k.vec_evac, vec)
        pe.wait_ge(k.act_evac, act)

    def up(phase, q, vec0, x_hi, x_lo, t, ready=None):
        def unit(trip, j, g, q):
            s, b = g % SLOTS, 2 * (j % 2)
            weights(g, q)
            pe.wait_ge(k.vec_evac, vec0 + (trip * SLOTS + j) + (phase.base + 1))
            for n in range(2):
                a = chain(k.ps[:, b + n, 0:t], s, [(n * D + kc * P, P, kc) for kc in range(KC)], x_hi, x_lo,
                          ready=ready if n == 0 and j == 0 else None)
            a.then_inc(k.unit_done, 1)
        over_units(pe, phase, q, unit)

    def down(phase, q, vec0, gates, a_hi, a_lo, t, fc):
        half = fc // 2

        def unit(trip, j, g, q):
            second = j % 2
            weights(g, q)
            pe.wait_ge(k.ff_ready, gates + (2 + (1 + second) * half))
            if not second:
                pe.wait_ge(k.vec_evac, vec0 + (trip * 2 + j // 2) + (phase.base + 1))
            chain(k.ps[:, 2 * (j // 2), 0:t], g % SLOTS, [(c * P, P, second * half + c) for c in range(half)], a_hi, a_lo,
                  first=not second, last=bool(second)).then_inc(k.unit_done, 1)
        over_units(pe, phase, q, unit)

    def wide(phase, q, evac, evac0, x_hi, x_lo, t, ready=None, behind=None):
        def unit(trip, j, g, q):
            s, b = g % SLOTS, 2 * (j % 2)
            weights(g, q)
            pe.wait_ge(evac, evac0 + (trip * SLOTS + j) + (phase.base + 1))
            for n in range(2):
                a = chain(k.ps[:, b + n, 0:t], s, [(kc * 256 + n * P, P, kc) for kc in range(KC)], x_hi, x_lo,
                          ready=ready if n == 0 and j == 0 and (behind is None or trip == 0) else None)
            a.then_inc(k.unit_done, 1)
            if behind is not None:
                behind(trip * SLOTS + j)
        over_units(pe, phase, q, unit, loop=behind is None)

    def layer_norm(n):
        pe.wait_ge(k.sum_added, n * KC + KC)
        pe.matmul(k.ps[:, 4, 0:T1], k.mean_w[:, :], k.tmp[:, 2, :], start=True, stop=True).then_inc(k.ln_mean, 1)
        for c in range(KC):
            pe.wait_ge(k.ln_squared, n * KC + (c + 1))
            a = pe.matmul(k.ps[:, 5, 0:T1], k.mean_w[:, :], k.sq[:, c, :], start=c == 0, stop=c == KC - 1)
        a.then_inc(k.ln_var, 1)

    def rms_norm(n):
        for c in range(KC):
            pe.wait_ge(k.rms_squared, n * KC + c + 1)
            a = pe.matmul(k.ps[:, 4, 0:T2], k.mean_w[:, :], k.sq[:, c, 0:T2], start=c == 0, stop=c == KC - 1)
        a.then_inc(k.rms_mean, 1)

    def heads(items0, heads0, qb, kb, heads, score, value, acc, free):
        nb = len(qb)
        items = heads * nb

        def turn(n):
            h, j = n // nb, n % nb
            first, queries, keys = qb[j]
            pe.wait_ge(k.probs_ready, items0 + n + 1)
            if j == 0 and h >= 2:
                pe.wait_ge(k.pt_ready, heads0 + h - 1)
            if queries < P:
                stand_alone()
            for k0, col, width, q0 in kb[:j + 1]:
                c = col + first - q0
                a = pe.transpose(k.ps[0:width, 6 + h % 2, c:c + queries], k.pr[0:queries, n % BUFS, k0:k0 + width], k.ident[0:queries, 0:queries])
            a.then_inc(k.pt_written, 1)

        def sum_values(h):
            pe.wait_ge(k.pt_ready, heads0 + h + 1)
            total = qb[-1][0] + qb[-1][1]
            for n, (k0, col, width, q0) in enumerate(kb):
                a = pe.matmul(acc(h, q0, total), value(h, n, width), k.pt[0:width, h % 2, col:col + total - q0],
                              start=n == 0, stop=n == len(kb) - 1)
            a.then_inc(k.heads_summed, 1)

        def score_next(n):
            if n >= 2:
                pe.wait_ge(free, items0 + n - 1)
            score(n // nb, n % nb, n % 2, *qb[n % nb]).then_inc(k.scored, 1)

        score_next(0)
        score_next(1)
        for n in range(-1, items):
            if 2 <= n + 3 < items:
                score_next(n + 3)
            if n >= 0:
                turn(n)
            if n >= nb + 1 and (n - nb - 1) % nb == 0:
                sum_values((n - nb - 1) // nb)
        sum_values(heads - 1)

    pe.wait_ge(k.tokens_loaded, 48)
    for c in range(KC):
        if c >= 4:
            pe.wait_ge(k.turned_out, c - 3)
        for b, (at, n) in enumerate(((0, META), (META, P), (META + P, P))):
            a = pe.transpose(k.ps[:, 4 + c % 4, at:at + n], k.tokens[0:n, b, c * P:(c + 1) * P], k.ident[0:n, 0:n])
        a.then_inc(k.turned, 1)
    with pe.Fori(0, DEPTH) as l:
        q, vec0, act0, gates0 = l * (L_UNITS // SLOTS), l * L_VEC, l * L_ACT, l * L_GATES
        up(S1["up1"], q, vec0, k.x_hi, k.x_lo, T1, l * (3 * KC))
        down(S1["down1"], q, vec0, gates0, k.a_hi1, k.a_lo1, T1, FC)
        pe.wait_ge(k.const_loaded, 16 * N_CONST)
        pe.wait_ge(k.consts_set, 1)
        pe.wait_ge(k.vec_loaded, l * 96 + 96)
        pe.transpose(k.ps[:, 6, 0:N1], k.rows[:, :], k.ident[0:N1, 0:N1]).then_inc(k.vec_turned, 1)
        layer_norm(l * 3)

        def towards_latents(u):
            if u != LAT_SUMMED:
                return
            pe.wait_ge(k.lat_squared, l + 1)
            pe.matmul(k.ps[:, 4, 0:T1], k.mean_w[:, :], k.sq[:, 0, :], start=True, stop=False)
            pe.matmul(k.ps[:, 4, 0:T1], k.mean_w[:, :], k.sq[:, 1, :], start=False, stop=True)
            pe.matmul(k.ps[:, 5, 0:T1], k.mean_w[:, :], k.sq[:, 2, :], start=True, stop=True).then_inc(k.lat_mean, 1)
            for n in range(2):
                a = pe.matmul(k.ps[0:QK, 6 + n, 0:T1], k.place[:, n, :], k.mix1[0:ROPE, 15, :], start=True, stop=True)
            a.then_inc(k.kr_placed, 1)
        wide(S1["win"], q, k.act_evac, act0, k.x_hi, k.x_lo, T1, l * (3 * KC) + KC, behind=towards_latents)
        pe.wait_ge(k.lat_ready, l + 1)
        x_hi, x_lo = k.y_hi[:, 2], k.y_lo[:, 2]
        o = 0

        def acc_free(o):
            pe.wait_ge(k.act_evac, act0 + (S1["uq"].base + o + 1))
        for u in range(2):
            g = S1["uq"].first + u
            weights(g, q)
            for pair in range(2):
                acc_free(o)
                for n in range(2):
                    c = (2 * pair + n) * QK
                    a = chain(k.ps[0:QK, 2 * (o % 2) + n, 0:T1], g % SLOTS, [(kc * 4 * QK + c, QK, kc) for kc in range(2)], x_hi, x_lo)
                a.then_inc(k.unit_done if pair == 1 else k.latent_out, 1)
                o += 1
        r = slice(NOPE, QK)

        def rotate(n):
            for h in range(4):
                a = pe.matmul(k.ps[r, 4 + h, 0:T1], k.rot[r, :], k.qf[r, 4 * n + h, :], start=True, stop=True)
            a.then_inc(k.q_turned, 1)
        pe.wait_ge(k.act_evac, act0 + (S1["uq"].base + 4 + 2))
        pe.wait_ge(k.k_full, l + 1)
        stand_alone()
        rotate(0)
        g = S1["uk"].first
        weights(g, q)
        for pair in range(4):
            acc_free(o)
            for n in range(2):
                a = chain(k.ps[0:NOPE, 2 * (o % 2) + n, 0:T1], g % SLOTS, [((2 * pair + n) * NOPE, NOPE, 2)], x_hi, x_lo)
            a.then_inc(k.unit_done if pair == 3 else k.latent_out, 1)
            o += 1
        pe.wait_ge(k.q_rot_used, l * 2 + 1)
        stand_alone()
        rotate(1)
        g = S1["uv"].first
        s = g % SLOTS
        weights(g, q)
        for b, (first, n, _) in enumerate(QB1):
            acc_free(o)
            acc, t = k.ps[0:n, 2 * (o % 2), :], slice(first, first + n)
            pe.matmul(acc, x_hi[:, 2, t], k.w_hi[:, s, 0:512], start=True, stop=False)
            pe.matmul(acc, x_lo[:, 2, t], k.w_hi[:, s, 0:512], start=False, stop=False)
            a = pe.matmul(acc, x_hi[:, 2, t], k.w_lo[:, s, 0:512], start=False, stop=True)
            a.then_inc(k.unit_done if b == 2 else k.latent_out, 1)
            o += 1
        pe.wait_ge(k.q_full, l + 1)
        all_out(vec0 + (S1["branch"].base + 2), act0 + (S1["uv"].base + 3 + 2))

        def mla_score(h, j, b, first, queries, keys):
            return pe.matmul(k.ps[0:queries, 4 + b, 0:keys], k.qf[0:QK, h, first:first + queries], k.kf[0:QK, h, 0:keys], start=True, stop=True)
        heads(l * 24, l * 8, QB1, KB1, HEADS1, mla_score,
              lambda h, n, width: k.vt1[0:width, n, h * VH:(h + 1) * VH],
              lambda h, q0, total: k.ps[VH * (h % 2):VH * (h % 2) + VH, h // 2, q0:total], k.masked)
        pe.wait_ge(k.y_ready, l + 1)
        pe.wait_ge(k.conv_ready, l + 1)
        stand_alone()

        def branch(trip, j, g, q):
            s, b = g % SLOTS, 2 * (j % 2)
            weights(g, q)
            pe.wait_ge(k.vec_evac, vec0 + (trip * SLOTS + j) + (S1["branch"].base + 1))
            for n in range(2):
                a = chain(k.ps[:, b + n, 0:T1], s, [(n * 512 + c * P, P, c) for c in range(4)], k.y_hi[:, n], k.y_lo[:, n])
            a.then_inc(k.unit_done, 1)
        over_units(pe, S1["branch"], q, branch)
        pe.wait_ge(k.merged_ready, l * KC + KC)
        stand_alone()
        wide(S1["wo"], q, k.vec_evac, vec0, k.x_hi, k.x_lo, T1)
        layer_norm(l * 3 + 1)

        up(S1["up2"], q, vec0, k.x_hi, k.x_lo, T1, l * (3 * KC) + 2 * KC)
        down(S1["down2"], q, vec0, gates0 + FC, k.a_hi1, k.a_lo1, T1, FC)
        layer_norm(l * 3 + 2)

    pe.wait_ge(k.rows2_loaded, 16 * 6)
    for l in range(DEPTH):
        a = pe.transpose(k.ps[:, 6, l * N2:(l + 1) * N2], k.rows2[:, l, :], k.ident[0:N2, 0:N2])
    a.then_inc(k.cols2_turned, 1)

    x_hi, x_lo = k.x_hi[:, :, 0:T2], k.x_lo[:, :, 0:T2]
    for l in range(DEPTH):
        s = S20 if l == 0 else S21
        rms_norm(2 * l)
        all_out((DEPTH * L_VEC if l == 0 else V_LAYER1) + 2, s["values"].base + 2)

        def values(trip, j, g, q):
            st, b = g % SLOTS, 2 * (j % 2)
            weights(g, q)
            pe.wait_ge(k.act_evac, s["values"].base + j + 1)
            for t in range(2):
                for kc in range(KC):
                    if j == 0 and t == 0:
                        pe.wait_ge(k.x_ready, (3 * DEPTH + 2 * l + 1) * KC + kc + 1)
                    a = parts_turned(k.ps[:, b + t, 0:256], st, kc * 256, 256, kc, t, kc == 0, kc == KC - 1)
            a.then_inc(k.unit_done, 1)

        def parts_turned(acc, st, c, n, kc, t, first, last):
            tok = slice(t * P, (t + 1) * P)
            pe.matmul(acc, k.x_hi[:, kc, tok], k.w_hi[:, st, c:c + n], start=first, stop=False)
            pe.matmul(acc, k.x_lo[:, kc, tok], k.w_hi[:, st, c:c + n], start=False, stop=False)
            return pe.matmul(acc, k.x_hi[:, kc, tok], k.w_lo[:, st, c:c + n], start=False, stop=last)
        over_units(pe, s["values"], 0, values)
        g = s["small"].first
        weights(g, 0)
        pe.wait_ge(k.act_evac, s["small"].base + 2)
        for t in range(2):
            for half in range(2):
                for kc in range(KC):
                    a = parts_turned(k.ps[:, t, 8 * half:8 * half + 8], g % SLOTS, half * KC * 8 + kc * 8, 8, kc, t, kc == 0, kc == KC - 1)
        a.then_inc(k.unit_done, 1)
        pe.wait_ge(k.act_evac, s["plain"].base + 2)
        wide(s["plain"], 0, k.act_evac, 0, x_hi, x_lo, T2)
        pe.wait_ge(k.lf_ready, l + 1)
        pe.matmul(k.ps[:, 4, 0:12], k.tri[:, :], k.lf[:, 0, :], start=True, stop=True)
        pe.matmul(k.ps[:, 4, 16:28], k.ones[:, :], k.lf[:, 0, :], start=True, stop=False)
        pe.matmul(k.ps[:, 4, 16:28], k.tri[:, :], k.lf[:, 1, :], start=False, stop=True).then_inc(k.cum_summed, 1)
        wide(s["gated"], 0, k.act_evac, 0, x_hi, x_lo, T2)
        g = s["group"].first
        weights(g, 0)
        pe.wait_ge(k.pool_ready, l + 1)
        all_out(s["branch"].base + 2, s["group"].base + 2)
        for n in range(4):
            a = chain(k.ps[:, n, 0:T2], g % SLOTS, [(n * P, P, n)], k.y_hi[:, 2, :, 0:T2], k.y_lo[:, 2, :, 0:T2])
        a.then_inc(k.unit_done, 1)
        pe.wait_ge(k.qk_ready, l + 1)
        pe.wait_ge(k.cum_ready, l + 1)
        all_out(s["branch"].base + 2, s["group"].base + 2 + 2)

        def column(x, c, n):
            return x[:, c, n:n + 1].broadcast_to([P, P])

        def minus_sums(acc, x, n, keys):
            for c in range(keys // P):
                pe.matmul(acc[:, c * P:keys], column(x, c, n), k.ntri[:, 0:keys - c * P], start=c == 0, stop=False)

        def ml_score(h, j, b, first, queries, keys):
            decay = k.ps[:, 4 + b, 256:512]
            minus_sums(decay, k.lf, h, keys)
            for c in range(keys // P):
                pe.matmul(decay[:, c * P:(c + 1) * P], column(k.gx, c, h), k.ident[:, :], start=False, stop=c == keys // P - 1)
            return pe.matmul(k.ps[:, 4 + b, 0:keys], k.qkc[:, h, first:first + P], k.qkc[:, 4 + h, 0:keys], start=True, stop=True)

        def fox_score(h, j, b, first, queries, keys):
            if (h, j) == (1, 0):
                pe.wait_ge(k.ml_std, l + 1)
            acc = k.ps[:, 4 + b, 0:keys]
            minus_sums(acc, k.lf_fox, h, keys)
            pe.matmul(acc[:, keys - P:keys], k.ident[:, :], k.mask[:, 2 * P:3 * P], start=False, stop=False)
            p = slice(FOX_DH * (h % 2), FOX_DH * (h % 2) + FOX_DH)
            return pe.matmul(acc, k.mix2[p, 12 + h // 2, first:first + P], k.mix2[p, 16 + h // 2, 0:keys], start=False, stop=True)

        i0, h0 = (DEPTH + l) * 24, DEPTH * 8 + l * 12
        heads(i0, h0, QB2, KB2, ML_HEADS, ml_score, lambda h, n, width: k.vtok[:, n, h * P:(h + 1) * P],
              lambda h, q0, total: k.ps[:, h // 2, (h % 2) * T2 + q0:(h % 2) * T2 + total], k.probs_ready)
        pe.wait_ge(k.ml_squared, l + 1)
        for h in range(ML_HEADS):
            a = pe.matmul(k.ps[:, 6 + h // 2, (h % 2) * T2:(h % 2) * T2 + T2], k.mean_w[:, :], k.sq[:, h, 0:T2], start=True, stop=True)
        a.then_inc(k.ml_mean, 1)
        pe.wait_ge(k.lf_fox_ready, l + 1)
        heads(i0 + 2 * ML_HEADS, h0 + ML_HEADS, QB2, KB2, FOX_HEADS, fox_score,
              lambda h, n, width: k.vtok[:, n, 512 + h * FOX_DH:512 + (h + 1) * FOX_DH],
              lambda h, q0, total: k.ps[FOX_DH * (h % 2):FOX_DH * (h % 2) + FOX_DH, 2 + h // 4,
                                        (h // 2 % 2) * T2 + q0:(h // 2 % 2) * T2 + total], k.masked)
        pe.wait_ge(k.y_ready, DEPTH + l + 1)
        pe.wait_ge(k.ml_parts, l + 1)

        def branch2(trip, j, g, q):
            st, b = g % SLOTS, 2 * (j % 2)
            weights(g, q)
            pe.wait_ge(k.vec_evac, (trip * SLOTS + j) + (s["branch"].base + 1))
            for n in range(3):
                a = chain(k.ps[:, b + n // 2, 256 * (n % 2):256 * (n % 2) + 256], st, [(n * 512 + c * P, P, c) for c in range(4)],
                          k.y_hi[:, n, :, 0:T2], k.y_lo[:, n, :, 0:T2])
            a.then_inc(k.unit_done, 1)
        over_units(pe, s["branch"], 0, branch2)
        pe.wait_ge(k.merged_ready, (DEPTH + l) * KC + KC)
        wide(s["wout"], 0, k.vec_evac, 0, x_hi, x_lo, T2)
        rms_norm(2 * l + 1)
        if l == 0:
            up(s["up"], 0, 0, x_hi, x_lo, T2, (3 * DEPTH + 2 * l + 2) * KC)
            down(s["down"], 0, 0, s["up"].gates, k.a_hi2, k.a_lo2, T2, FC)

    for c in range(KC):
        pe.wait_ge(k.rms_scaled, (2 * DEPTH - 1) * KC + c + 1)
        for t in range(2):
            a = pe.matmul(k.ps[:, 6 + t, 0:EXPERTS], k.sq[:, c, t * P:(t + 1) * P], k.wr[:, c, :], start=c == 0, stop=c == KC - 1)
    a.then_inc(k.routed, 1)
    for t in range(2):
        for c in range(KC):
            a = pe.transpose(k.ps[:, 2 * t + c // 4, (c % 4) * P:(c % 4 + 1) * P], k.sq[:, c, t * P:(t + 1) * P], k.ident[:, :])
    a.then_inc(k.xt_turned, 1)
    pe.wait_ge(k.member_ready, 1)
    pe.matmul(k.ps[:, 5, 0:EXPERTS], k.tri[:, :], k.member[:, 0, :], start=True, stop=True)
    pe.matmul(k.ps[:, 5, EXPERTS:2 * EXPERTS], k.ones[:, :], k.member[:, 0, :], start=True, stop=False)
    pe.matmul(k.ps[:, 5, EXPERTS:2 * EXPERTS], k.tri[:, :], k.member[:, 1, :], start=False, stop=True).then_inc(k.rank_summed, 1)
    pe.wait_ge(k.sel_ready, 1)

    def start_experts_sum():
        pe.wait_ge(k.zeros_set, 1)
        for b in range(4):
            pe.matmul(k.ps[:, 4 + b, :], k.zeros[:, 0:P], k.zeros, start=True, stop=False)
        for t in range(2):
            for c in range(KC):
                pe.matmul(k.ps[:, 4 + 2 * t + c // 4, (c % 4) * P:(c % 4 + 1) * P], k.h[:, c, META + t * P:META + (t + 1) * P], k.ident[:, :],
                          start=False, stop=False)

    def spread_columns(x, first):
        for e in range(EXPERTS):
            for t in range(2):
                a = pe.matmul(k.ps[:, first + e // 2, (e % 2) * T2 + t * P:(e % 2) * T2 + (t + 1) * P],
                              x[:, t, e:e + 1].broadcast_to([P, P]), k.ident[:, :], start=True, stop=True)
        return a

    y = k.ps[:, 4:8, :].rearrange("p b n -> p (b n)")

    def gather(x, e):
        for c in range(KC):
            for t in range(2):
                a = pe.matmul(k.ps[:, 2 + c // 4, (c % 4) * P:(c % 4 + 1) * P], x[:, t, c * P:(c + 1) * P],
                              k.to_slot[:, t, bass.ds(e, 1), :], start=t == 0, stop=t == 1)
        return a

    def expert(r, e, sched, last):
        n = e + r * EXPERTS
        q = n * (E_UNITS // SLOTS)
        pe.wait_ge(k.xe_ready, n + 1)
        stand_alone()
        up(sched["up"], q, n * EC, k.x_hi[:, :, 0:P], k.x_lo[:, :, 0:P], P)
        chunks = EC // DOWN_GROUPS

        def unit(trip, j, g, q):
            s = g % SLOTS
            weights(g, q)
            if trip == 0:
                pe.wait_ge(k.ff_ready, n * EC + (sched["up"].gates + 2 + (j + 1) * chunks))
            if trip < 2 and j == 0:
                pe.wait_ge(k.vec_evac, n * EC + (sched["down"].base + 1))
            acc = k.ps[:, trip % 2, 0:DOWN_COLS]
            for c in range(chunks):
                ff, w = j * chunks + c, slice(c * DOWN_COLS, (c + 1) * DOWN_COLS)
                pe.matmul(acc, k.a_hi3[:, ff, :], k.w_hi[:, s, w], start=ff == 0, stop=False)
                pe.matmul(acc, k.a_lo3[:, ff, :], k.w_hi[:, s, w], start=False, stop=False)
                a = pe.matmul(acc, k.a_hi3[:, ff, :], k.w_lo[:, s, w], start=False, stop=ff == EC - 1)
            a.then_inc(k.unit_done, 1)
            if trip and j == 0:
                add_block(trip - 1)
            if (trip, j) == HI_GATHERED and not last:
                gather(k.xt_hi, e + 1).then_inc(k.hi_gathered, 1)
            if (trip, j) == LO_GATHERED and not last:
                pe.wait_ge(k.xe_hi_ready, n + 2)
                stand_alone()
                gather(k.xt_lo, e + 1).then_inc(k.lo_gathered, 1)

        def add_block(block):
            pe.wait_ge(k.down_ready, n * DOWN_BLOCKS + block + 1)
            for t in range(2):
                for x in (k.d_hi, k.d_lo):
                    pe.matmul(y[:, block * DOWN_COLS + t * D:(block + 1) * DOWN_COLS + t * D],
                              k.to_token[:, bass.ds(e, 1), t * P:(t + 1) * P].rearrange("p a t -> p (a t)"), x, start=False, stop=False)
        over_units(pe, sched["down"], q, unit, loop=False)
        add_block(DOWN_BLOCKS - 1)

    def gather_first(r):
        gather(k.xt_hi, 0).then_inc(k.hi_gathered, 1)
        pe.wait_ge(k.xe_hi_ready, r * EXPERTS + 1)
        gather(k.xt_lo, 0).then_inc(k.lo_gathered, 1)

    def moe_round(r):
        spread_columns(k.sel, SPREAD[r]).then_inc(k.sel_spread, 1)
        if r == 0:
            pe.wait_ge(k.xt_ready, 1)
            gather_first(r)
        pe.wait_ge(k.choice_ready, r + 1)
        spread_columns(k.gates, SPREAD[r]).then_inc(k.gate_spread, 1)
        pe.wait_ge(k.slots_ready, r + 1)
        if r == 0:
            start_experts_sum()
        else:
            gather_first(r)
        with pe.Fori(0, EXPERTS - 1) as e:
            expert(r, e, SE, last=False)
        expert(r, EXPERTS - 1, SE_LAST, last=True)
    moe_round(0)
    pe.wait_ge(k.more_ready, 1)
    more = pe.value_load(k.more[0:1, 0:1], min_val=0, max_val=1)
    with pe.If(more > 0):
        moe_round(1)
    for b in range(4):
        a = pe.matmul(k.ps[:, 4 + b, :], k.zeros[:, 0:P], k.zeros, start=False, stop=True)
    a.then_inc(k.all_added, 1)


def build(nc, i, out):
    with ExitStack() as ctx:
        k = allocate(nc, ctx)
        block = ctx.enter_context(nc.Block())

        @block.sync
        def _(sp):
            sp_program(sp, k, i, out)

        @block.scalar
        def _(act):
            act_program(act, k, i, out)

        @block.vector
        def _(vec):
            vec_program(vec, k, i, out)

        @block.gpsimd
        def _(pool):
            pool_program(pool, k, i, out)

        @block.tensor
        def _(pe):
            pe_program(pe, k, i, out)


def constants():
    t = np.arange(T1, dtype=np.float32)
    freq = (np.float32(1.0) / (np.float32(10000.0) ** (np.arange(0, ROPE, 2, dtype=np.float32) / np.float32(ROPE)))).astype(np.float32)
    ang = (freq[:, None] * t[None, :]).astype(np.float32)
    half = ROPE // 2
    rot = np.zeros((P, ROPE), np.float32)
    place = np.zeros((ROPE, 2, QK), np.float32)
    for m in range(half):
        rot[NOPE + m + half, m], rot[NOPE + m, m + half] = -1.0, 1.0
        place[m + half, 1, NOPE + m], place[m, 1, NOPE + m + half] = -1.0, 1.0
    for m in range(ROPE):
        place[m, 0, NOPE + m] = 1.0
    row = np.arange(P)
    tri = (row[:, None] <= row[None, :]).astype(np.float32)
    mask = np.zeros((P, 3 * P), np.float32)
    mask[:, 2 * P:] = np.where(row[None, :] <= row[:, None], 0.0, NEG)
    pos = np.arange(16)
    icnt = np.stack([1.0 / np.minimum(pos + 1, w) for w in (2, 4, 8, 16)]).astype(np.float32)
    return {
        "c_ident": np.eye(P, dtype=np.float32), "c_tri": tri,
        "c_ntri": np.concatenate([-tri, -np.ones((P, P), np.float32)], 1), "c_mask": mask, "c_rot": rot,
        "c_cos": np.tile(np.cos(ang), (2, 1)), "c_sin": np.tile(np.sin(ang), (2, 1)), "c_place": place, "c_icnt": icnt,
        "c_eidx": np.arange(EXPERTS, dtype=np.float32)[None, :],
        "c_slots": np.arange(1, P + 1, dtype=np.float32)[None, :],
    }


def kernel(**inputs):
    import concourse.bacc as bacc
    from concourse.bass_utils import run_bass_kernel_spmd

    nc = bacc.Bacc("TRN2", target_bir_lowering=False, num_devices=1)
    arrays, aps = {}, {}
    for name, a in {**inputs, **constants()}.items():
        a = np.ascontiguousarray(a)
        arrays[f"in_{name}"] = a
        aps[name] = nc.dram_tensor(f"in_{name}", a.shape, mybir.dt.from_np(a.dtype), kind="ExternalInput").ap()
    out = nc.dram_tensor("out", (1, SEQ, D), F32, kind="ExternalOutput").ap()
    build(nc, aps, out)
    r = run_bass_kernel_spmd(nc, [arrays], core_ids=[0])
    return r.results[0]["out"]
```
